# Optimizing a Trainium2 kernel written in Bass

```python
import jax, jax.numpy as jnp
from jax import lax
import numpy as np
import math

D_MODEL = 1024
BATCH = 1
SEQ = 512
DEPTH = 1

N_HEADS = 16
HEAD_DIM = 64
N_KV = 4
HPG = N_HEADS // N_KV
ATTN_DIM = N_HEADS * HEAD_DIM
KV_DIM = N_KV * HEAD_DIM
CMP_BLOCK = 32
CMP_STRIDE = 16
CMP_HIDDEN = 256
SEL_BLOCK = 64
N_SEL = 16
WINDOW = 512
Q_BLOCK = 128
FORCE_BONUS = 1e4
LRU_WIDTH = 1024
LRU_BLOCKS = 16
LRU_BW = LRU_WIDTH // LRU_BLOCKS
CONV_W = 4
LRU_C = 8.0
D_FF = -(-8 * D_MODEL // 768) * 256
IN_DIM = ATTN_DIM + 6 * KV_DIM + 3 * N_HEADS + 2 * LRU_WIDTH + 2 * D_MODEL
EPS = 1e-6


def _rmsnorm(x, g):
    xf = x.astype(jnp.float32)
    y = xf * lax.rsqrt(jnp.mean(xf * xf, axis=-1, keepdims=True) + EPS)
    return (y * g.astype(jnp.float32)).astype(x.dtype)

def _masked_softmax(s, mask):
    s = jnp.where(mask, s.astype(jnp.float32), -1e30)
    m = jnp.max(s, axis=-1, keepdims=True)
    e = jnp.exp(s - m) * mask
    return e / jnp.maximum(jnp.sum(e, axis=-1, keepdims=True), 1e-30)

def _alibi_slopes():
    return np.power(2.0, -8.0 * np.arange(1, N_HEADS + 1) / N_HEADS).astype(np.float32)

def _cmp_to_sel_map(n_cmp, n_blk):
    cs = np.arange(n_cmp) * CMP_STRIDE
    ce = cs + CMP_BLOCK - 1
    bs = np.arange(n_blk) * SEL_BLOCK
    be = bs + SEL_BLOCK - 1
    return ((cs[:, None] <= be[None, :]) & (ce[:, None] >= bs[None, :])).astype(np.float32)

def _compress(kv, pos, w1, b1, w2, b2):
    B, T, G, D = kv.shape
    chunks = kv.reshape(B, T // CMP_STRIDE, CMP_STRIDE, G, D)
    blocks = jnp.concatenate([chunks[:, :-1], chunks[:, 1:]], axis=2) + pos[None, None, :, None, :]
    hid = jax.nn.gelu(jnp.einsum('bnlgd,ldf->bngf', blocks, w1) + b1)
    return jnp.einsum('bngf,fd->bngd', hid, w2) + b2

def _nsa(q, k_cmp, v_cmp, k_slc, v_slc, k_win, v_win, gates):
    B, T = q.shape[0], q.shape[1]
    n_cmp = k_cmp.shape[1]
    n_blk = T // SEL_BLOCK
    n_sel = min(N_SEL, n_blk)
    n_tok = n_sel * SEL_BLOCK
    scale = HEAD_DIM ** -0.5
    slopes = jnp.asarray(_alibi_slopes()).reshape(1, N_KV, HPG, 1, 1)
    cmp_end = jnp.arange(n_cmp) * CMP_STRIDE + CMP_BLOCK - 1
    blk_map = jnp.asarray(_cmp_to_sel_map(n_cmp, n_blk))
    kb = k_slc.reshape(B, n_blk, SEL_BLOCK, N_KV, HEAD_DIM).transpose(0, 3, 1, 2, 4)
    vb = v_slc.reshape(B, n_blk, SEL_BLOCK, N_KV, HEAD_DIM).transpose(0, 3, 1, 2, 4)
    k_pad = jnp.pad(k_win, ((0, 0), (WINDOW, 0), (0, 0), (0, 0)))
    v_pad = jnp.pad(v_win, ((0, 0), (WINDOW, 0), (0, 0), (0, 0)))
    b_ix = jnp.arange(B)[:, None, None, None]
    g_ix = jnp.arange(N_KV)[None, :, None, None]
    blk_ids = jnp.arange(n_blk)

    def block(i):
        qs = i * Q_BLOCK
        qb = lax.dynamic_slice_in_dim(q, qs, Q_BLOCK, axis=1)
        gb = lax.dynamic_slice_in_dim(gates, qs, Q_BLOCK, axis=1)
        t = qs + jnp.arange(Q_BLOCK)
        dist = (t[:, None] - cmp_end[None, :]).astype(jnp.float32)
        s = jnp.einsum('bqghd,bngd->bghqn', qb, k_cmp) * scale
        p_cmp = _masked_softmax(s - slopes * dist, dist >= 0)
        o_cmp = jnp.einsum('bghqn,bngd->bqghd', p_cmp.astype(v_cmp.dtype), v_cmp)
        imp = jnp.einsum('bghqn,nj->bgqj', p_cmp, blk_map)
        cur = (t // SEL_BLOCK)[:, None]
        forced = ((blk_ids == 0) | (blk_ids == cur) | (blk_ids == cur - 1)).astype(jnp.float32)
        valid = blk_ids[None, :] * SEL_BLOCK <= t[:, None]
        imp = jnp.where(valid, imp + FORCE_BONUS * forced, -1e30)
        _, idx = lax.top_k(imp, n_sel)
        k_sel = kb[b_ix, g_ix, idx].reshape(B, N_KV, Q_BLOCK, n_tok, HEAD_DIM)
        v_sel = vb[b_ix, g_ix, idx].reshape(B, N_KV, Q_BLOCK, n_tok, HEAD_DIM)
        s_pos = (idx[..., None] * SEL_BLOCK + jnp.arange(SEL_BLOCK)).reshape(B, N_KV, 1, Q_BLOCK, n_tok)
        dist = (t[None, None, None, :, None] - s_pos).astype(jnp.float32)
        s = jnp.einsum('bqghd,bgqmd->bghqm', qb, k_sel) * scale
        p = _masked_softmax(s - slopes * dist, dist >= 0)
        o_slc = jnp.einsum('bghqm,bgqmd->bqghd', p.astype(v_sel.dtype), v_sel)
        kw = lax.dynamic_slice_in_dim(k_pad, qs, WINDOW + Q_BLOCK, axis=1)
        vw = lax.dynamic_slice_in_dim(v_pad, qs, WINDOW + Q_BLOCK, axis=1)
        w_pos = qs - WINDOW + jnp.arange(WINDOW + Q_BLOCK)
        wd = t[:, None] - w_pos[None, :]
        wmask = (wd >= 0) & (wd < WINDOW) & (w_pos[None, :] >= 0)
        s = jnp.einsum('bqghd,bkgd->bghqk', qb, kw) * scale
        p = _masked_softmax(s - slopes * wd.astype(jnp.float32), wmask)
        o_win = jnp.einsum('bghqk,bkgd->bqghd', p.astype(vw.dtype), vw)
        o = gb[..., 0:1] * o_cmp + gb[..., 1:2] * o_slc + gb[..., 2:3] * o_win
        return o.reshape(B, Q_BLOCK, ATTN_DIM)

    out = lax.map(block, jnp.arange(T // Q_BLOCK))
    return out.transpose(1, 0, 2, 3).reshape(B, T, ATTN_DIM)

def _lin_combine(c1, c2):
    a1, b1 = c1
    a2, b2 = c2
    return a1 * a2, a2 * b1 + b2

def _rglru_branch(xb, gate, conv_w, conv_b, wa, ba, wi, bi, lam):
    B, T, W = xb.shape
    xc = lax.conv_general_dilated(xb, conv_w, window_strides=(1,), padding=[(CONV_W - 1, 0)],
                                  dimension_numbers=('NWC', 'WIO', 'NWC'),
                                  feature_group_count=LRU_WIDTH) + conv_b
    xr = xc.reshape(B, T, LRU_BLOCKS, LRU_BW)
    r = jax.nn.sigmoid(jnp.einsum('btnk,nkj->btnj', xr, wa).reshape(B, T, W) + ba)
    i = jax.nn.sigmoid(jnp.einsum('btnk,nkj->btnj', xr, wi).reshape(B, T, W) + bi)
    log_a = -LRU_C * r.astype(jnp.float32) * jax.nn.softplus(-lam.astype(jnp.float32))
    a = jnp.exp(log_a)
    b = jnp.sqrt(-jnp.expm1(2.0 * log_a)) * (i * xc).astype(jnp.float32)
    _, h = lax.associative_scan(_lin_combine, (a, b), axis=1)
    return h.astype(xb.dtype) * jax.nn.gelu(gate)

def _layer(x, norm1_g, w_in, q_norm_g, k_norm_g, cmp_pos_k, cmp_w1_k, cmp_b1_k, cmp_w2_k, cmp_b2_k,
           cmp_pos_v, cmp_w1_v, cmp_b1_v, cmp_w2_v, cmp_b2_v, conv_w, conv_b, lru_wa, lru_ba,
           lru_wi, lru_bi, lru_lambda, w_o_attn, w_o_lru, w_out, norm2_g, w_gate, w_up, w_down):
    B, T, _ = x.shape
    h = _rmsnorm(x, norm1_g)
    proj = h @ w_in
    o1 = ATTN_DIM
    o2 = o1 + 6 * KV_DIM
    o3 = o2 + 3 * N_HEADS
    o4 = o3 + LRU_WIDTH
    o5 = o4 + LRU_WIDTH
    q = _rmsnorm(proj[..., :o1].reshape(B, T, N_KV, HPG, HEAD_DIM), q_norm_g)
    kv = proj[..., o1:o2].reshape(B, T, 6, N_KV, HEAD_DIM)
    nsa_g = jax.nn.sigmoid(proj[..., o2:o3].reshape(B, T, N_KV, HPG, 3))
    lru_x = proj[..., o3:o4]
    lru_gate = proj[..., o4:o5]
    merge_g = jax.nn.sigmoid(proj[..., o5:].reshape(B, T, 2, D_MODEL))
    k_cmp = _rmsnorm(_compress(kv[:, :, 0], cmp_pos_k, cmp_w1_k, cmp_b1_k, cmp_w2_k, cmp_b2_k), k_norm_g[0])
    v_cmp = _compress(kv[:, :, 1], cmp_pos_v, cmp_w1_v, cmp_b1_v, cmp_w2_v, cmp_b2_v)
    k_slc = _rmsnorm(kv[:, :, 2], k_norm_g[1])
    k_win = _rmsnorm(kv[:, :, 4], k_norm_g[2])
    attn = _nsa(q, k_cmp, v_cmp, k_slc, kv[:, :, 3], k_win, kv[:, :, 5], nsa_g)
    lru = _rglru_branch(lru_x, lru_gate, conv_w, conv_b, lru_wa, lru_ba, lru_wi, lru_bi, lru_lambda)
    merged = merge_g[:, :, 0] * (attn @ w_o_attn) + merge_g[:, :, 1] * (lru @ w_o_lru)
    x = x + merged @ w_out
    h2 = _rmsnorm(x, norm2_g)
    return x + (jax.nn.silu(h2 @ w_gate) * (h2 @ w_up)) @ w_down

def first_inputs(seed: int = 0) -> dict:
    key = jax.random.key(seed)
    ks = jax.random.split(key, 32)
    L = DEPTH
    nrm = lambda k, shape, fan: jax.random.normal(k, shape, jnp.float32) * (fan ** -0.5)
    small = lambda k, shape, s: jax.random.normal(k, shape, jnp.float32) * s
    u = jax.random.uniform(ks[31], (L, LRU_WIDTH), jnp.float32, minval=0.9, maxval=0.999)
    a0 = u ** (1.0 / LRU_C)
    return {
        "x": jax.random.normal(ks[0], (BATCH, SEQ, D_MODEL), jnp.float32),
        "norm1_g": 1.0 + small(ks[1], (L, D_MODEL), 0.02),
        "w_in": nrm(ks[2], (L, D_MODEL, IN_DIM), D_MODEL),
        "q_norm_g": 1.0 + small(ks[3], (L, HEAD_DIM), 0.02),
        "k_norm_g": 1.0 + small(ks[4], (L, 3, HEAD_DIM), 0.02),
        "cmp_pos_k": small(ks[5], (L, CMP_BLOCK, HEAD_DIM), 0.1),
        "cmp_w1_k": nrm(ks[6], (L, CMP_BLOCK, HEAD_DIM, CMP_HIDDEN), CMP_BLOCK * HEAD_DIM),
        "cmp_b1_k": small(ks[7], (L, CMP_HIDDEN), 0.01),
        "cmp_w2_k": nrm(ks[8], (L, CMP_HIDDEN, HEAD_DIM), CMP_HIDDEN),
        "cmp_b2_k": small(ks[9], (L, HEAD_DIM), 0.01),
        "cmp_pos_v": small(ks[10], (L, CMP_BLOCK, HEAD_DIM), 0.1),
        "cmp_w1_v": nrm(ks[11], (L, CMP_BLOCK, HEAD_DIM, CMP_HIDDEN), CMP_BLOCK * HEAD_DIM),
        "cmp_b1_v": small(ks[12], (L, CMP_HIDDEN), 0.01),
        "cmp_w2_v": nrm(ks[13], (L, CMP_HIDDEN, HEAD_DIM), CMP_HIDDEN),
        "cmp_b2_v": small(ks[14], (L, HEAD_DIM), 0.01),
        "conv_w": nrm(ks[15], (L, CONV_W, 1, LRU_WIDTH), CONV_W),
        "conv_b": small(ks[16], (L, LRU_WIDTH), 0.01),
        "lru_wa": nrm(ks[17], (L, LRU_BLOCKS, LRU_BW, LRU_BW), LRU_BW),
        "lru_ba": small(ks[18], (L, LRU_WIDTH), 0.01),
        "lru_wi": nrm(ks[19], (L, LRU_BLOCKS, LRU_BW, LRU_BW), LRU_BW),
        "lru_bi": small(ks[20], (L, LRU_WIDTH), 0.01),
        "lru_lambda": jnp.log(a0) - jnp.log1p(-a0),
        "w_o_attn": nrm(ks[21], (L, ATTN_DIM, D_MODEL), ATTN_DIM),
        "w_o_lru": nrm(ks[22], (L, LRU_WIDTH, D_MODEL), LRU_WIDTH),
        "w_out": nrm(ks[23], (L, D_MODEL, D_MODEL), D_MODEL),
        "norm2_g": 1.0 + small(ks[24], (L, D_MODEL), 0.02),
        "w_gate": nrm(ks[25], (L, D_MODEL, D_FF), D_MODEL),
        "w_up": nrm(ks[26], (L, D_MODEL, D_FF), D_MODEL),
        "w_down": nrm(ks[27], (L, D_FF, D_MODEL), D_FF),
    }

def first_block(x, norm1_g, w_in, q_norm_g, k_norm_g, cmp_pos_k, cmp_w1_k, cmp_b1_k, cmp_w2_k, cmp_b2_k,
              cmp_pos_v, cmp_w1_v, cmp_b1_v, cmp_w2_v, cmp_b2_v, conv_w, conv_b, lru_wa, lru_ba,
              lru_wi, lru_bi, lru_lambda, w_o_attn, w_o_lru, w_out, norm2_g, w_gate, w_up, w_down):
    for l in range(DEPTH):
        x = _layer(x, norm1_g[l], w_in[l], q_norm_g[l], k_norm_g[l], cmp_pos_k[l], cmp_w1_k[l],
                   cmp_b1_k[l], cmp_w2_k[l], cmp_b2_k[l], cmp_pos_v[l], cmp_w1_v[l], cmp_b1_v[l],
                   cmp_w2_v[l], cmp_b2_v[l], conv_w[l], conv_b[l], lru_wa[l], lru_ba[l], lru_wi[l],
                   lru_bi[l], lru_lambda[l], w_o_attn[l], w_o_lru[l], w_out[l], norm2_g[l],
                   w_gate[l], w_up[l], w_down[l])
    return x


DEPTH_2 = 2

CHUNK = 64
QBLK = 128
POOL_WIDTH = D_MODEL
POOL_GROUPS = 4
POOL_GROUP = POOL_WIDTH // POOL_GROUPS
POOL_WINDOWS = (2, 4, 8, 16)
DIFF_QK_DIM = 128
DIFF_V_DIM = 2 * DIFF_QK_DIM
DIFF_HEADS = D_MODEL // DIFF_V_DIM
DIFF_QK_WIDTH = DIFF_HEADS * 2 * DIFF_QK_DIM
DIFF_V_WIDTH = DIFF_HEADS * DIFF_V_DIM
ROT_DIM = DIFF_QK_DIM // 4
ROPE_THETA = 500000.0
N_BRANCHES = 2
IN_WIDTH = POOL_WIDTH + 2 * DIFF_QK_WIDTH + DIFF_V_WIDTH + N_BRANCHES * D_MODEL
FFN_HIDDEN = -(-8 * D_MODEL // (3 * 256)) * 256
NORM_EPS = 1e-6


def rmsnorm(x, g):
    xf = x.astype(jnp.float32)
    y = xf * lax.rsqrt(jnp.mean(xf * xf, axis=-1, keepdims=True) + NORM_EPS)
    return (y * g.astype(jnp.float32)).astype(x.dtype)

def rotary_tables(seq, dtype):
    pos = jnp.arange(seq, dtype=jnp.float32)
    inv_freq = ROPE_THETA ** (-jnp.arange(0, ROT_DIM, 2, dtype=jnp.float32) / ROT_DIM)
    ang = pos[:, None] * inv_freq[None, :]
    return jnp.cos(ang).astype(dtype), jnp.sin(ang).astype(dtype)

def apply_partial_rotary(t, cos, sin):
    half = ROT_DIM // 2
    t1, t2, rest = t[..., :half], t[..., half:ROT_DIM], t[..., ROT_DIM:]
    return jnp.concatenate([t1 * cos - t2 * sin, t2 * cos + t1 * sin, rest], axis=-1)

def pool_mixer(u, w_pool, scale):
    b, s, _ = u.shape
    ug = u.reshape(b, s, POOL_GROUPS, POOL_GROUP)
    t_idx = jnp.arange(s, dtype=jnp.float32)[None, :, None]
    outs = []
    for gi, w in enumerate(POOL_WINDOWS):
        xg = ug[:, :, gi, :].astype(jnp.float32)
        c = jnp.cumsum(xg, axis=1)
        c_shift = jnp.pad(c, ((0, 0), (w, 0), (0, 0)))[:, :s]
        count = jnp.minimum(t_idx + 1.0, float(w))
        outs.append((c - c_shift) / count - xg)
    pooled = jnp.stack(outs, axis=2).astype(u.dtype)
    y = jnp.einsum('bsgc,gcd->bsgd', pooled, w_pool)
    return y.reshape(b, s, POOL_WIDTH) * scale

def diff_attention(q, k, v, lam):
    b, h, _, s, d = q.shape
    nblk = s // QBLK
    chunk_ids = jnp.arange(s) // CHUNK
    qb = q.reshape(b, h, 2, nblk, QBLK, d).transpose(3, 0, 1, 2, 4, 5)
    qc = chunk_ids.reshape(nblk, QBLK)
    scale = DIFF_QK_DIM ** -0.5
    neg = jnp.finfo(jnp.float32).min

    def one_block(args):
        qi, ci = args
        sc = jnp.einsum('bhcqd,bhckd->bhcqk', qi, k).astype(jnp.float32) * scale
        mask = ci[:, None] >= chunk_ids[None, :]
        p = jax.nn.softmax(jnp.where(mask, sc, neg), axis=-1)
        a = p[:, :, 0] - lam * p[:, :, 1]
        return jnp.einsum('bhqk,bhkv->bhqv', a.astype(v.dtype), v)

    out = lax.map(one_block, (qb, qc))
    return out.transpose(1, 2, 0, 3, 4).reshape(b, h, s, DIFF_V_DIM)

def second_inputs(seed: int = 0) -> dict:
    key = jax.random.key(seed)
    ks = jax.random.split(key, 16)
    f32 = jnp.float32
    nrm = lambda k, shp, std: jax.random.normal(k, shp, f32) * std
    return {
        "x": jax.random.normal(ks[0], (BATCH, SEQ, D_MODEL), f32),
        "norm1_g": 1.0 + nrm(ks[1], (DEPTH_2, D_MODEL), 0.02),
        "w_in": nrm(ks[2], (DEPTH_2, D_MODEL, IN_WIDTH), D_MODEL ** -0.5),
        "q_norm_g": 1.0 + nrm(ks[3], (DEPTH_2, DIFF_QK_DIM), 0.02),
        "k_norm_g": 1.0 + nrm(ks[4], (DEPTH_2, DIFF_QK_DIM), 0.02),
        "lam_q1": nrm(ks[5], (DEPTH_2, DIFF_QK_DIM), 0.1),
        "lam_k1": nrm(ks[6], (DEPTH_2, DIFF_QK_DIM), 0.1),
        "lam_q2": nrm(ks[7], (DEPTH_2, DIFF_QK_DIM), 0.1),
        "lam_k2": nrm(ks[8], (DEPTH_2, DIFF_QK_DIM), 0.1),
        "subln_g": 1.0 + nrm(ks[9], (DEPTH_2, DIFF_V_DIM), 0.02),
        "pool_w": nrm(ks[10], (DEPTH_2, POOL_GROUPS, POOL_GROUP, POOL_GROUP), POOL_GROUP ** -0.5),
        "pool_scale": 1.0 + nrm(ks[11], (DEPTH_2, POOL_WIDTH), 0.02),
        "w_out": nrm(ks[12], (DEPTH_2, D_MODEL, D_MODEL), D_MODEL ** -0.5),
        "norm2_g": 1.0 + nrm(ks[13], (DEPTH_2, D_MODEL), 0.02),
        "w_ffn_in": nrm(ks[14], (DEPTH_2, D_MODEL, 2 * FFN_HIDDEN), D_MODEL ** -0.5),
        "w_ffn_out": nrm(ks[15], (DEPTH_2, FFN_HIDDEN, D_MODEL), FFN_HIDDEN ** -0.5),
    }

def second_block(x, norm1_g, w_in, q_norm_g, k_norm_g, lam_q1, lam_k1, lam_q2, lam_k2,
              subln_g, pool_w, pool_scale, w_out, norm2_g, w_ffn_in, w_ffn_out):
    b, s, _ = x.shape
    cos, sin = rotary_tables(s, x.dtype)
    splits = np.cumsum([POOL_WIDTH, DIFF_QK_WIDTH, DIFF_QK_WIDTH, DIFF_V_WIDTH, D_MODEL]).tolist()
    for i in range(DEPTH_2):
        lam_init = 0.8 - 0.6 * math.exp(-0.3 * i)
        xn = rmsnorm(x, norm1_g[i])
        proj = xn @ w_in[i]
        u_pool, q, k, v, g_a, g_b = jnp.split(proj, splits, axis=-1)
        q = q.reshape(b, s, DIFF_HEADS, 2, DIFF_QK_DIM).transpose(0, 2, 3, 1, 4)
        k = k.reshape(b, s, DIFF_HEADS, 2, DIFF_QK_DIM).transpose(0, 2, 3, 1, 4)
        q = apply_partial_rotary(rmsnorm(q, q_norm_g[i]), cos, sin)
        k = apply_partial_rotary(rmsnorm(k, k_norm_g[i]), cos, sin)
        v = v.reshape(b, s, DIFF_HEADS, DIFF_V_DIM).transpose(0, 2, 1, 3)
        lam = (jnp.exp(jnp.sum(lam_q1[i].astype(jnp.float32) * lam_k1[i].astype(jnp.float32)))
               - jnp.exp(jnp.sum(lam_q2[i].astype(jnp.float32) * lam_k2[i].astype(jnp.float32)))
               + lam_init)
        o = diff_attention(q, k, v, lam)
        o = rmsnorm(o, subln_g[i]) * (1.0 - lam_init)
        attn_out = o.transpose(0, 2, 1, 3).reshape(b, s, DIFF_V_WIDTH)
        pool_out = pool_mixer(u_pool, pool_w[i], pool_scale[i])
        merged = jax.nn.sigmoid(g_a) * pool_out + jax.nn.sigmoid(g_b) * attn_out
        x = x + merged @ w_out[i]
        hn = rmsnorm(x, norm2_g[i])
        gate, up = jnp.split(hn @ w_ffn_in[i], 2, axis=-1)
        x = x + (jax.nn.silu(gate) * up) @ w_ffn_out[i]
    return x


def setup_inputs(seed=0):
    out = dict(first_inputs(seed))
    for name, value in second_inputs(seed + 1).items():
        if name != "x":
            out[name + "_2"] = value
    return out


def reference(
    x, norm1_g, w_in, q_norm_g, k_norm_g, cmp_pos_k, cmp_w1_k, cmp_b1_k, cmp_w2_k, cmp_b2_k,
    cmp_pos_v, cmp_w1_v, cmp_b1_v, cmp_w2_v, cmp_b2_v, conv_w, conv_b, lru_wa, lru_ba, lru_wi,
    lru_bi, lru_lambda, w_o_attn, w_o_lru, w_out, norm2_g, w_gate, w_up, w_down, norm1_g_2,
    w_in_2, q_norm_g_2, k_norm_g_2, lam_q1_2, lam_k1_2, lam_q2_2, lam_k2_2, subln_g_2, pool_w_2,
    pool_scale_2, w_out_2, norm2_g_2, w_ffn_in_2, w_ffn_out_2,
):
    x = first_block(
        x, norm1_g, w_in, q_norm_g, k_norm_g, cmp_pos_k, cmp_w1_k, cmp_b1_k, cmp_w2_k, cmp_b2_k,
        cmp_pos_v, cmp_w1_v, cmp_b1_v, cmp_w2_v, cmp_b2_v, conv_w, conv_b, lru_wa, lru_ba,
        lru_wi, lru_bi, lru_lambda, w_o_attn, w_o_lru, w_out, norm2_g, w_gate, w_up, w_down,
    )
    return second_block(
        x, norm1_g_2, w_in_2, q_norm_g_2, k_norm_g_2, lam_q1_2, lam_k1_2, lam_q2_2, lam_k2_2,
        subln_g_2, pool_w_2, pool_scale_2, w_out_2, norm2_g_2, w_ffn_in_2, w_ffn_out_2,
    )


_drawn_inputs = setup_inputs


def setup_inputs(seed=0):
    import zlib

    import numpy as np

    out = dict(_drawn_inputs(seed))
    spreads = {}
    factors = {'norm1_g': 4.325,
     'q_norm_g': 8.0,
     'k_norm_g': 8.0,
     'cmp_pos_k': 8.0,
     'cmp_b1_k': 8.0,
     'cmp_b2_k': 21.795,
     'cmp_b1_v': 23.353,
     'cmp_b2_v': 8.0,
     'lru_ba': 8.0,
     'lru_bi': 8.0,
     'norm2_g': 3.099,
     'norm1_g_2': 2.991,
     'q_norm_g_2': 7.037,
     'k_norm_g_2': 6.734,
     'lam_k1_2': 3.096,
     'subln_g_2': 35.154,
     'pool_scale_2': 5.596,
     'norm2_g_2': 3.45}
    for name, (base, spread) in spreads.items():
        noise = np.random.default_rng([zlib.crc32(name.encode()), seed]).standard_normal(out[name].shape)
        drawn = base * np.exp(spread * noise) if base else spread * noise
        out[name] = __import__('jax').numpy.asarray(drawn.astype(out[name].dtype))
    for name, factor in factors.items():
        out[name] = (out[name] * factor).astype(out[name].dtype)
    return out
```

```python
from contextlib import ExitStack

import numpy as np

import concourse.bass as bass
from concourse import mybir

F32 = mybir.dt.float32
F32R = mybir.dt.float32r
ALU = mybir.AluOpType
ACT = mybir.ActivationFunctionType
AX = mybir.AxisListType

P = 128
T = 512
TT = T // P
D = 1024
KT = D // P
EPS = 1e-6
HEADS, HD, GROUPS = 16, 64, 4
NBLK, STRIDE, BLOCK = 31, 16, 32
HID = 256
DFF = 2816
FT = DFF // P
HEADS2, QK2, V2 = 4, 128, 256
LAYERS = 2
POOL_W = (2, 4, 8, 16)
NEG = -1e32

RAW, SPLIT = 4, 2

C_KV, C_CMP, C_Q, C_LRU, C_MIX, C_WO, C_GU, C_DN, C_B2 = np.cumsum(
    [0, 12, 8, 8, 16, 32, 8, 44, 24]).tolist()
L_QKV, L_U, L_PW, L_GAB, L_WO, L_GU, L_DN, C_LAYER = np.cumsum(
    [0, 24, 8, 4, 16, 8, 44, 24]).tolist()
C_ALL = C_B2 + LAYERS * C_LAYER
T_IN, T_KV, T_CMP, T_Q, T_LRU, T_MIX, T_WO, T_GU, T_DN, T_B2 = np.cumsum(
    [0, 8, 12, 4, 8, 16, 32, 8, 44, 8]).tolist()
U_QKV, U_U, U_PW, U_GAB, U_WO, U_GU, U_DN, T_LAYER = np.cumsum(
    [0, 24, 8, 8, 16, 8, 44, 8]).tolist()

CONST = {}
_at = 0
for _name, _n in (("ident", P), ("ones", P), ("blk", P), ("dist", T), ("cdist", TT * 32),
                  ("cmask", TT * 32), ("slope", HEADS), ("cos", T), ("sin", T), ("chunk", T),
                  ("edge", 32), ("lam", 4)):
    CONST[_name] = slice(_at, _at + _n)
    _at += _n
CONST_N = _at

PAR = {}
_at = 0
for _name, _n in (("n1", KT), ("n2", KT), ("cw", 4 * KT), ("cb", KT), ("ba", KT), ("bi", KT),
                  ("lam", KT), ("b1k", 2), ("b1v", 2), ("qg", 1), ("kg", 3), ("b2k", 1),
                  ("posk", 16), ("posv", 16)):
    PAR[_name] = slice(_at, _at + _n)
    _at += _n
PAR_N = _at
PAR2 = {}
_at = 0
for _name, _n in (("n1", KT), ("n2", KT), ("ps", KT), ("qg", 1), ("kg", 1), ("lam", 4),
                  ("sub", 2)):
    PAR2[_name] = slice(_at, _at + _n)
    _at += _n
PAR2_N = _at


def constants():
    c = np.zeros((P, CONST_N), np.float32)
    p = np.arange(P)[:, None]
    c[:, CONST["ident"]] = np.eye(P)
    c[:, CONST["ones"]] = 1.0
    c[:, CONST["blk"]] = (p // HD == np.arange(P)[None] // HD)
    rel = np.arange(T)[None] - (T - P) - p
    c[:, CONST["dist"]] = np.where(rel <= 0, rel, NEG)
    t = np.arange(TT)[None, :, None] * P + p[:, :, None]
    n = np.arange(32)[None, None, :]
    d = t - (n * STRIDE + BLOCK - 1)
    ok = (d >= 0) & (n < NBLK)
    c[:, CONST["cdist"]] = np.where(ok, -d, NEG).reshape(P, -1)
    c[:, CONST["cmask"]] = ok.reshape(P, -1)
    slope = np.power(2.0, -8.0 * np.arange(1, HEADS + 1) / HEADS).astype(np.float32)
    c[:, CONST["slope"]] = slope * np.float32(HD ** 0.5)
    rot = 32
    inv = np.float32(500000.0) ** (-np.arange(0, rot, 2, dtype=np.float32) / np.float32(rot))
    ang = np.arange(T, dtype=np.float32)[None] * inv[:, None]
    c[0:rot, CONST["cos"]] = np.concatenate([np.cos(ang)] * 2)
    c[0:rot, CONST["sin"]] = np.concatenate([-np.sin(ang), np.sin(ang)])
    c[:, CONST["chunk"]] = np.where(p // 64 >= (np.arange(T)[None] - (T - P)) // 64, 0.0, -3e38)
    at = CONST["edge"].start
    for w in POOL_W:
        c[:, at:at + w] = np.float32(w) / np.arange(1, w + 1, dtype=np.float32)
        at += w
    for l in range(LAYERS):
        li = 0.8 - 0.6 * np.exp(-0.3 * l)
        c[:, CONST["lam"].start + 2 * l] = li
        c[:, CONST["lam"].start + 2 * l + 1] = -0.5 * (1.0 - li)
    return c


class Steps:

    def __init__(self, sem, names):
        self.sem, self.names = sem, {x: i for i, x in enumerate(names)}

    def at(self, n, name=None):
        return n * len(self.names) + (len(self.names) if name is None else self.names[name] + 1)


P_AT = (0, 128, 384, 768)
PT_AT = (0, 512, 1024, 896)
UNITS = 4


def unit_max(u):
    return [f"max{u}_{x}" for x in range(4)] + [f"max{u}"]


def unit_scale(u):
    return [f"rec{u}", f"gate{u}"] + [f"scale{u}_{q}" for q in range(3)] + [f"scale{u}"]


AT_PE = ["c_s"] + [f"s0_{x}" for x in range(4)] + ["c_t0"] + [f"s1_{x}" for x in range(4)] + [
    "c_v0", "t0", "v0"] + [f"s2_{x}" for x in range(4)] + ["t1", "v1", "c_t1", "c_v1"] + [
    f"s3_{x}" for x in range(4)] + ["t2", "v2", "t3", "v3"]
AT_DVE = (["bias0", "bias1", "cbias0", "cbias1", "c_add", "c_max", "c_sub"] + unit_max(0)
          + ["c_mask", "c_sum", "c_guard", "c_rec", "c_gate", "c_scale", "c_lo0"] + unit_max(1)
          + unit_scale(0) + ["lo0"] + unit_max(2) + unit_scale(1) + ["lo1", "out0", "c_lo1"]
          + unit_max(3) + unit_scale(2) + ["lo2"] + unit_scale(3) + ["lo3", "out1"])


def unit_exp(u):
    return [f"exp{u}_{q}" for q in range(4)]


AT_ACT = (["c_exp"] + unit_exp(0) + ["c_hi0"] + unit_exp(1) + ["hi0"] + unit_exp(2)
          + ["hi1", "out0", "c_hi1"] + unit_exp(3) + ["hi2", "hi3", "out1"])


A2_PE = [f"s{c}_{x}" for c in range(2) for x in range(4)] + ["t", "v", "sums"]
A2_DVE = ([f"max0_{x}" for x in range(4)] + ["max0"] + [f"max1_{x}" for x in range(4)] + ["max1", "rec", "neg"]
          + [f"scale{q}" for q in range(4)] + [f"a{q}" for q in range(4)] + ["lo", "copy0", "copy1", "newton", "scale",
                                                                            "out0", "out1"])
A2_ACT = [f"exp{c}_{q}" for c in range(2) for q in range(4)] + ["hi", "square0", "square1", "root", "root2"]


def pool_steps():
    return [x for m in range(KT) for x in [f"y{m}_{k}" for k in range(m // 2 + 1)]
            + [f"edge{m}", f"mean{m}", f"lo{m}"]]


P_DMAS = 37
G_DMAS = 6


def build(nc, a, out):
    with ExitStack() as ctx:
        top = [-(-nc.sbuf_base // 32) * 32]
        names = [0]

        def place(shape, dt, offset):
            names[0] += 1
            return nc.alloc_sbuf_tensor_at(f"b{names[0]}", [P] + list(shape), dt, offset=offset)

        def keep(*shape, dt=F32):
            t = place(shape, dt, top[0])
            top[0] += -(-int(np.prod(shape)) * 4 // 32) * 32
            return t

        def sem(name):
            return ctx.enter_context(nc.semaphore(name))

        def steps(name, each):
            return Steps(sem(name), each)

        xT = keep(KT, T)
        wraw = keep(RAW, KT * P)
        wsp = keep(SPLIT, 2, KT, P, dt=F32R)
        xg = keep(2, KT, T, dt=F32R)
        con = keep(CONST_N)
        par = keep(PAR_N)
        par2 = keep((LAYERS + 1) * PAR2_N)
        lay = keep(PAR2_N + KT)
        c_rs = keep(T)
        acc = keep(T)
        sq = keep(2, T)
        n_r0 = keep(T)
        n_r2 = keep(T)
        n_b = keep(T)
        small = keep(64)

        base = top[0]
        limit = nc.sbuf_usable_end

        class Plan:
            def __init__(self, at=0):
                self.at = at

            def __call__(self, *shape, dt=F32):
                t = place(shape, dt, base + self.at)
                self.at += -(-int(np.prod(shape)) * 4 // 32) * 32
                assert base + self.at <= limit, (base + self.at - limit)
                return t

        pl = Plan()
        attnT = pl(2, KT, T, dt=F32R)
        after_attn = pl.at
        kn = pl(2, 2, 2, T, dt=F32R)
        vtok = pl(2, 2, TT, GROUPS * HD, dt=F32R)
        kc = pl(2, P, dt=F32R)
        vc = pl(2, GROUPS, HD, dt=F32R)
        gates = pl(TT, 3 * HEADS)
        before_pair = pl.at
        qraw = pl(T)
        qn = pl(2, T, dt=F32R)
        h_sq, h_t = sq[:, 0, :], sq[:, 1, :]
        bias = pl(2, T)
        cbias = pl(2, TT * 32)
        Pm = pl(2, 1280)
        Pc = pl(2, TT, 32)
        PT = pl(2, 1280, dt=F32R)
        st = pl(64)
        cst = pl(64)
        pl = Plan()
        kvraw = pl(12, T)
        gwraw = pl(KT, 48)
        gw = pl(2, KT, 48, dt=F32R)
        w2raw = pl(2, 2, P)
        hidc = pl(2, P)
        kcraw = pl(P)
        assert pl.at <= after_attn
        pl = Plan(before_pair)
        E = pl(2, 2, 5, 264, dt=F32R)
        Et = pl(2, T, dt=F32R)
        w2 = pl(2, 2, 2, P, dt=F32R)
        gsc = sq[:, 1, :]
        hidr = pl(2, 2, 2, P, dt=F32R)
        bcol = pl(8)
        vcraw = pl(GROUPS, HD)
        b2v = pl(HD)
        pl = Plan()
        xin = pl(TT, D)
        prow = pl(P)
        prow2 = pl(P)
        pl = Plan(after_attn)
        lruT = pl(2, KT, T, dt=F32R)
        before_lru = pl.at
        lruw = pl(2, KT, HD)
        bd = pl(2, 2, P, dt=F32R)
        lx = pl(T + 3)
        xc = pl(T)
        xcr = pl(2, T, dt=F32R)
        gl = pl(T)
        lt = [pl(T) for _ in range(7)]
        pl = Plan(before_lru)
        mrgT = pl(2, KT, T, dt=F32R)
        mg = pl(2, T)
        mt = sq[:, 0, :]
        pl = Plan()
        aT2 = pl(KT, T)
        after_a2 = pl.at
        qk2 = pl(4, 2, T, dt=F32R)
        vtok2 = pl(2, TT, V2, dt=F32R)
        Pm2 = pl(2, 1280)
        PT2 = pl(2, 1280, dt=F32R)
        raw2 = pl(6, T)
        rot = pl(T)
        os2 = pl(2, T)
        st2 = pl(64)
        pl = Plan(after_a2)
        mix2 = pl(2, KT, T, dt=F32R)
        poolT = pl(KT, T)
        ur = pl(2, T + 16)
        ya, yb = pl(T + 16), pl(T + 16)
        pr = pl(T)
        mg2 = pl(2, T)
        mt2 = pl(T)
        pl = Plan()
        yout = pl(TT, D)
        pl = Plan()
        hid = pl(2, FT, T, dt=F32R)
        fg = pl(2, T)
        fu = pl(T)
        ft = pl(T)

        def pb(name, *shape):
            return ctx.enter_context(nc.psum_tensor(name, [P] + list(shape), F32))

        psA = pb("psA", 2, T)
        psS = pb("psS", 2, T)
        psT = pb("psT", 3, T)
        psO = pb("psO", T)

        ident, ones, blk = con[:, CONST["ident"]], con[:, CONST["ones"]], con[:, CONST["blk"]]

        wload = [sem(f"weights_loaded{s}") for s in range(RAW)]
        wsplit = steps("weights_split", ["hi", "lo"])
        used = steps("chunk_used", ["all"])
        drained = steps("tile_drained", ["all"])
        x_in = sem("x_loaded")
        c_in = sem("constants_loaded")
        p_in = sem("parameters_loaded")
        g_in = sem("small_weights_loaded")
        lw_in = sem("lru_weights_loaded")
        su_pe = steps("setup_transposed", ["one"])
        su_dve = steps("setup_vector", ["one"])
        res_act = steps("residual_scalar", ["hi", "square"])
        res_dve = steps("residual_vector", ["lo", "sum"])
        nm_pe = steps("norm_sums", ["sum"])
        nm_act = steps("norm_scalar", ["root", "root2"])
        nm_dve = steps("norm_vector", ["newton", "scale", "zero"])
        hn_act = steps("headnorm_scalar", ["square", "root", "root2", "hi"])
        hn_pe = steps("headnorm_sums", ["sum"])
        hn_dve = steps("headnorm_vector", ["newton", "scale", "apply", "lo"])
        cg_dve = steps("small_split_vector", ["gw_hi", "gw_lo", "w2_hi", "w2_lo", "gates"])
        cg_pe = steps("gate_products", ["gates", "transposed"])
        cg_act = steps("gate_sigmoid", ["all"])
        e_dve0 = steps("blocks_zeroed", ["zero", "hi_k", "lo_k", "hi_v", "lo_v"])
        e_act = steps("blocks_scalar", ["hi", "even", "odd"])
        e_dve = steps("blocks_vector", ["lo", "even", "odd"])
        ch_dve = steps("hidden_bias", ["bias"])
        ch_act = steps("hidden_scalar", ["gelu", "hi"])
        vt_pe = steps("values_transposed", ["all"])
        vt_act = steps("values_hi", ["all"])
        vt_dve = steps("values_lo", ["all"])
        kv_pe = steps("compressed_kv", ["all"])
        kv_dve = steps("compressed_vector", ["k", "v", "v_hi", "v_lo"])
        at_pe = steps("attention_products", AT_PE)
        at_dve = steps("attention_vector", AT_DVE)
        at_act = steps("attention_scalar", AT_ACT)
        sp_dve = steps("softplus_vector", ["abs"])
        sp_act = steps("softplus_scalar", ["exp"])
        eps_in = steps("epsilon_set", ["all"])
        lw_dve = steps("lru_zeroed", ["diagonal", "pad"])
        lr_pe = steps("lru_products", ["a", "i"])
        lr_dve = steps("lru_vector", ["tap0", "tap1", "tap2", "tap3", "lo", "w0", "w1", "one", "rec", "ratio",
                                      "ix", "b", "scan", "out", "out_lo"])
        lr_act = steps("lru_scalar", ["hi", "w0", "w1", "gelu", "r", "i", "tanh", "a", "root", "out_hi"])
        mx_act = steps("mix_scalar", ["gate0", "gate1", "hi"])
        mx_dve = steps("mix_vector", ["sum", "lo"])
        ff_act = steps("ffn_scalar", ["silu", "hi"])
        ff_dve = steps("ffn_vector", ["product", "lo"])
        ly_dve = steps("layer_vector", ["copy", "gains", "sub", "products", "diff", "lambda"])
        ly_pe = steps("layer_sums", ["sum"])
        ly_act = steps("layer_scalar", ["exp"])
        h2_act = steps("headnorm2_scalar", ["square", "root", "root2", "hi"])
        h2_pe = steps("headnorm2_sums", ["sum"])
        h2_dve = steps("headnorm2_vector", ["newton", "scale", "apply", "swap", "sin", "cos", "rot", "lo"])
        v2_raw = steps("values2_drained", ["all"])
        v2_pe = steps("values2_transposed", ["all"])
        v2_act = steps("values2_hi", ["all"])
        v2_dve = steps("values2_lo", ["all"])
        a2_pe = steps("attention2_products", A2_PE)
        a2_dve = steps("attention2_vector", A2_DVE)
        a2_act = steps("attention2_scalar", A2_ACT)
        up_dve = steps("pool_vector", ["pad0", "pad1"] + pool_steps())
        up_act = steps("pool_hi", ["hi"])
        m2_act = steps("mix2_scalar", ["ga", "gb", "hi"])
        m2_dve = steps("mix2_vector", ["pool", "attn", "sum", "lo"])
        ou_pe = steps("output_transposed", ["all"])
        ou_act = steps("output_copied", ["all"])
        stored = sem("stored")

        def hi_f(x):
            return x.bitcast(F32)

        settles = sem("waits_settled")

        def settled(engine):
            engine.sem_inc(settles, 1)

        block = ctx.enter_context(nc.Block())

        def col_tile(w, kts, m):
            v = w.rearrange("(k p) n -> p k n", p=P)
            h = kts // 2
            return [(0, h, v[:, 0:h, bass.ds(m, P)]), (h, kts, v[:, h:kts, bass.ds(m, P)])]

        w_in, w_in2 = a["w_in"][0], a["w_in_2"]

        def tail(stage, c0, wo, gate, up, down):
            stage(c0, 8, lambda i, s: wo(i * 4 * P + s * P))
            stage(c0 + 8, 2 * FT, lambda i, s: (up if s % 2 else gate)(i * 2 * P + (s // 2) * P))
            stage(c0 + 8 + 2 * FT, 24, lambda i, s: down(s % 3 * KT, i * 4 * P + (s // 3) * P), per=12)

        @block.sync
        def _(sp):
            def load(c, s, parts, dst=None, settle=False):
                if not isinstance(c, int) or c >= RAW:
                    sp.wait_ge(wsplit.sem, wsplit.at(c - RAW))
                    if settle:
                        settled(sp)
                slot = wraw[:, s, :].rearrange("p (k n) -> p k n", n=P)
                for lo, hi, src in parts:
                    sp.dma_start(slot[:, lo:hi, :] if dst is None else dst(slot, lo), src).then_inc(wload[s], 16)

            def stage(c0, n, parts, per=RAW, dst=None):
                with sp.Fori(0, n // per) as i:
                    for s in range(per):
                        load(c0 + i * per + s, s % RAW, parts(i, s), dst)

            sp.dma_start(xin[:, :, :], a["x"][0].rearrange("(t p) d -> p t d", p=P)).then_inc(x_in, 16)
            wc = w_in.rearrange("(k p) n -> p k n", p=P)

            def halves(col, apart):
                return [(b, 0, wc[:, :, bass.ds(col + b * apart, HD)]) for b in range(2)]

            def to_half(slot, b):
                return slot[:, :, b * HD:(b + 1) * HD]

            for s in range(RAW):
                load(s, s, halves(D + s // 2 * GROUPS * HD + s % 2 * HD, 2 * HD), to_half)
            stage(C_KV + 4, 8, lambda i, s: halves(i * (2 * GROUPS * HD) + D + (2 + s // 2) * GROUPS * HD + s % 2 * HD, 2 * HD),
                  dst=to_half)
            for kv, name in enumerate(("cmp_w1_k", "cmp_w1_v")):
                w1 = a[name][0].rearrange("l d f -> (l d) f")
                for s in range(4):
                    half = w1[(s % 2) * D:(s % 2 + 1) * D, :]
                    load(C_CMP + 4 * kv + s, s, col_tile(half, KT, (s // 2) * P))
            stage(C_Q, 8, lambda i, s: halves(i * (4 * HD) + s * HD, D // 2), dst=to_half)
            o3 = 2608
            stage(C_LRU, 16, lambda i, s: col_tile(w_in, KT, i * 2 * P + o3 + (s % 2) * D + (s // 2) * P))
            woa = a["w_o_attn"][0].rearrange("(b k d) n -> b d k n", b=2, d=HD)
            wol = a["w_o_lru"][0]
            o5 = o3 + 2 * D

            def mix_parts(i, s):
                if s == 1:
                    return [(b, 0, woa[b, :, :, bass.ds(i * P, P)]) for b in range(2)]
                if s == 3:
                    return col_tile(wol, KT, i * P)
                return col_tile(w_in, KT, i * P + o5 + (s // 2) * D)

            with sp.Fori(0, KT) as i:
                for s in range(4):
                    load(C_MIX + i * 4 + s, s, mix_parts(i, s),
                         (lambda slot, b: slot[b * HD:(b + 1) * HD, :, :]) if s == 1 else None, settle=s == 1)
            def down(r, m):
                k = min(KT, FT - r)
                return col_tile(a["w_down"][0][r * P:(r + k) * P, :], k, m)

            tail(stage, C_WO, lambda m: col_tile(a["w_out"][0], KT, m), lambda m: col_tile(a["w_gate"][0], KT, m),
                 lambda m: col_tile(a["w_up"][0], KT, m), down)

            def stacked(name):
                return a[name].rearrange("l (k p) n -> p (l k) n", p=P)

            wi2, wo2, wf2, wd2 = (stacked(x) for x in ("w_in_2", "w_out_2", "w_ffn_in_2", "w_ffn_out_2"))
            pw2 = a["pool_w_2"].rearrange("l g (k p) (m n) -> p (l g k) m n", p=P, n=P)
            with sp.Fori(0, LAYERS) as l:
                def col2(w, col, k0=0, kts=KT, each=KT):
                    h = kts // 2
                    return [(b, e, w[:, bass.ds(l * each + (k0 + b), e - b), bass.ds(col, P)]) for b, e in ((0, h), (h, kts))]

                c0 = l * C_LAYER + C_B2
                with sp.Fori(0, 2) as i:
                    for s in range(12):
                        x = s % 6
                        load(c0 + i * 12 + s, s % RAW,
                             col2(wi2, i * (2 * V2) + (D * (1 + x // 2) + s // 6 * V2 + x % 2 * P)))
                stage(c0 + L_U, 8, lambda i, s: col2(wi2, i * 4 * P + s * P))
                for g in range(4):
                    load(c0 + (L_PW + g), g, [(2 * k, 2 * k + 2, pw2[:, bass.ds(l * 8 + (g * 2 + k), 1), :, :].squeeze(1)) for k in range(2)], settle=True)
                stage(c0 + L_GAB, 16, lambda i, s: col2(wi2, i * 2 * P + (D * (4 + s % 2) + s // 2 * P)))
                tail(stage, c0 + L_WO, lambda m: col2(wo2, m), lambda m: col2(wf2, m), lambda m: col2(wf2, m + DFF),
                     lambda r, m: col2(wd2, m, r, min(KT, FT - r), FT))

        @block.gpsimd
        def _(pool):
            def split(c, rnd, s):
                pool.wait_ge(wload[s], rnd * 32 + 32)
                if not isinstance(c, int) or c >= SPLIT:
                    pool.wait_ge(used.sem, used.at(c - SPLIT))
                if not isinstance(c, int):
                    settled(pool)
                w = wsp[:, s % SPLIT].rearrange("p h k n -> p h (k n)")
                nc.gpsimd.tensor_copy(w[:, 0], wraw[:, s]).then_inc(wsplit.sem, 1)
                pool.wait_ge(wsplit.sem, wsplit.at(c, "hi"))
                nc.gpsimd.tensor_tensor(w[:, 1], wraw[:, s], hi_f(w[:, 0]), ALU.subtract).then_inc(wsplit.sem, 1)

            for s in range(RAW):
                split(s, 0, s)
            with pool.Fori(1, C_ALL // RAW) as i:
                for s in range(RAW):
                    split(i * RAW + s, i, s)

        def tail_pe(pe, chunk, free, proj, norm, c0, t0, src, k, n, ff):
            with pe.Fori(0, 4) as i:
                for s in range(2):
                    proj(c0 + i * 2 + s, t0 + i * 2 + s, s, lambda h, kt: src[:, h, kt, :])
            norm(k, n + 7)
            with pe.Fori(0, FT) as i:
                for s in range(2):
                    proj(c0 + 8 + i * 2 + s, t0 + 8 + i * 2 + s, s)
            pe.wait_ge(ff_dve.sem, ff_dve.at(ff + FT - 1))
            settled(pe)
            c1, t1 = c0 + 8 + 2 * FT, t0 + 8 + 2 * FT
            with pe.Fori(0, 4) as i:
                for m in range(2):
                    free(t1 + i * 2 + m)
                    for q in range(3):
                        s = 3 * m + q
                        chunk(c1 + i * 6 + s, s, psA[:, m, :], lambda h, kt: hid[:, h, q * KT + kt, :],
                              min(KT, FT - q * KT), q == 0, q == 2)
            norm(k + 1, n + 15)

        def pair_pe(pe, chunk, free, three, headnorm, pa, n, s):
            free(T_Q + n)
            chunk(C_Q + n, s, psA[:, s, :], lambda h, kt: xg[:, h, kt, :])
            headnorm(n + 5, blk)
            pe.wait_ge(hn_dve.sem, hn_dve.at(n + 5))

            def q(hd, h, qt):
                return qn[hd * HD:(hd + 1) * HD, h, qt * P:(qt + 1) * P]

            def scores(u):
                hd, br = u // 2, u % 2
                for x, qt in enumerate((3, 2, 1, 0)):
                    if x >= 2:
                        pe.wait_ge(at_dve.sem, at_dve.at(n, f"max{u}_{x - 2}"))
                    elif u:
                        pe.wait_ge(at_dve.sem, at_dve.at(n, f"max{u - 1}_{x + 2}"))
                    else:
                        pe.wait_ge(at_dve.sem, at_dve.at(n, "c_add"))
                    w = P * (qt + 1)
                    three(psS[:, x % 2, 0:w], lambda h: q(hd, h, qt),
                          lambda h: kn[hd * HD:(hd + 1) * HD, br, pa, h, 0:w], True, True).then_inc(at_pe.sem, 1)

            def transposes(u):
                pe.wait_ge(at_dve.sem, at_dve.at(n, f"scale{u}"))
                for kt in range(TT):
                    for qt in range(kt, TT):
                        src = Pm[:, u % 2, P_AT[qt] + kt * P:P_AT[qt] + (kt + 1) * P]
                        to = PT_AT[kt] + (qt - kt) * P
                        i = nc.tensor.transpose(psT[:, to // T, to % T:to % T + P], src, ident)
                i.then_inc(at_pe.sem, 1)

            def values(u):
                hd, br = u // 2, u % 2
                g = 2 * pa + hd
                pe.wait_ge(at_dve.sem, at_dve.at(n, f"lo{u}"))
                for kt in range(TT):
                    w = T - kt * P
                    i = three(psO[0:HD, kt * P:T], lambda h: vtok[:, br, h, kt, g * HD:(g + 1) * HD],
                              lambda h: PT[:, h, PT_AT[kt]:PT_AT[kt] + w], False, br == 1 and kt == TT - 1, True)
                i.then_inc(at_pe.sem, 1)

            def c_transposes(hd):
                pe.wait_ge(at_dve.sem, at_dve.at(n, "c_scale" if hd == 0 else "lo1"))
                for qt in range(TT):
                    i = nc.tensor.transpose(psT[0:32, 0, qt * P:(qt + 1) * P], Pc[:, hd, qt, :], ident)
                i.then_inc(at_pe.sem, 1)

            def c_values(hd):
                g = 2 * pa + hd
                if hd:
                    pe.wait_ge(at_dve.sem, at_dve.at(n, "out0"))
                pe.wait_ge(at_dve.sem, at_dve.at(n, f"c_lo{hd}"))
                three(psO[0:HD, :], lambda h: vc[0:32, h, g, :], lambda h: PT[0:32, h, 0:T], True, False, True).then_inc(at_pe.sem, 1)

            for hd in range(2):
                for qt in range(TT):
                    g = 2 * pa + hd
                    i = three(psS[:, hd, qt * 32:qt * 32 + 32], lambda h: q(hd, h, qt),
                              lambda h: kc[hd * HD:(hd + 1) * HD, h, 32 * g:32 * g + 32], True, True)
            i.then_inc(at_pe.sem, 1)
            scores(0)
            c_transposes(0)
            scores(1)
            c_values(0)
            transposes(0)
            values(0)
            scores(2)
            transposes(1)
            values(1)
            c_transposes(1)
            c_values(1)
            scores(3)
            transposes(2)
            values(2)
            transposes(3)
            values(3)

        @block.tensor
        def _(pe):
            mm = nc.tensor.matmul

            def chunk(c, s, dst, rhs, kts=KT, first=True, last=True):
                pe.wait_ge(wsplit.sem, wsplit.at(c))
                w = wsp[:, s % SPLIT]
                for kt in range(kts):
                    for n, (wh, xh) in enumerate(((0, 0), (0, 1), (1, 0))):
                        i = mm(dst, w[:, wh, kt, :], rhs(xh, kt), start=first and kt == 0 and n == 0,
                               stop=last and kt == kts - 1 and n == 2)
                i.then_inc(used.sem, 1)

            def free(t):
                pe.wait_ge(drained.sem, drained.at(t - 2))

            def rhs_x(h, kt):
                return xg[:, h, kt, :]

            def proj(c, t, s, rhs=rhs_x):
                free(t)
                chunk(c, s, psA[:, s % 2, :], rhs)

            def three(dst, lh, rh, start=False, stop=False, skip=False):
                for n, (x, y) in enumerate(((0, 0), (0, 1), (1, 0))):
                    i = mm(dst, lh(x), rh(y), start=start and n == 0, stop=stop and n == 2, skip_group_check=skip)
                return i

            def norm(k, n):
                pe.wait_ge(res_dve.sem, res_dve.at(n))
                mm(psO[:, :], ones, acc[:, :], start=True, stop=True).then_inc(nm_pe.sem, 1)

            def headnorm(n, sums, w=T):
                pe.wait_ge(hn_act.sem, hn_act.at(n, "square"))
                mm(psO[:, 0:w], sums, h_sq[:, 0:w], start=True, stop=True).then_inc(hn_pe.sem, 1)

            def headnorm2(n, x):
                pe.wait_ge(h2_act.sem, h2_act.at(n * 4 + x, "square"))
                mm(psO[:, :], ones, sq[:, x % 2, :], start=True, stop=True).then_inc(h2_pe.sem, 1)

            def values2(n, x):
                pe.wait_ge(v2_raw.sem, v2_raw.at(n * 2 + x))
                for t in range(TT):
                    i = nc.tensor.transpose(psT[:, x, t * P:(t + 1) * P], raw2[:, 4 + x, t * P:(t + 1) * P], ident)
                i.then_inc(v2_pe.sem, 1)

            def attention2(n):
                def dve(name):
                    pe.wait_ge(a2_dve.sem, a2_dve.at(n, name))

                pe.wait_ge(h2_dve.sem, h2_dve.at(n * 4 + 3))
                for c in range(2):
                    for x, qt in enumerate((3, 2, 1, 0)):
                        if c or x >= 2:
                            dve(f"max{c}_{x - 2}" if x >= 2 else f"max0_{x + 2}")
                        three(psS[:, x % 2, 0:P * (qt + 1)], lambda h: qk2[:, c, h, qt * P:(qt + 1) * P],
                              lambda h: qk2[:, 2 + c, h, 0:P * (qt + 1)], True, True).then_inc(a2_pe.sem, 1)
                pe.wait_ge(v2_dve.sem, v2_dve.at(n * 2 + 1))
                for qt in range(TT):
                    dve(f"a{qt}")
                    for kt in range(qt + 1):
                        to = PT_AT[kt] + (qt - kt) * P
                        i = nc.tensor.transpose(psT[:, to // T, to % T:to % T + P],
                                                Pm2[:, 0, P_AT[qt] + kt * P:P_AT[qt] + (kt + 1) * P], ident)
                i.then_inc(a2_pe.sem, 1)
                dve("lo")
                for d in range(2):
                    for kt in range(TT):
                        w = T - kt * P
                        i = three(psS[:, d, kt * P:T], lambda h: vtok2[:, h, kt, d * P:(d + 1) * P],
                                  lambda h: PT2[:, h, PT_AT[kt]:PT_AT[kt] + w], kt == 0, kt == TT - 1, True)
                i.then_inc(a2_pe.sem, 1)
                pe.wait_ge(a2_act.sem, a2_act.at(n, "square1"))
                mm(psO[:, :], ones, sq[:, 0, :], start=True, stop=False)
                mm(psO[:, :], ones, sq[:, 1, :], start=False, stop=True).then_inc(a2_pe.sem, 1)

            pe.wait_ge(c_in, 16)
            pe.wait_ge(p_in, P_DMAS * 16)
            nc.tensor.transpose(psT[:, 0, 0:PAR_N], prow[0:PAR_N, :], con[0:PAR_N, 0:PAR_N]).then_inc(su_pe.sem, 1)
            nc.tensor.transpose(psT[:, 1, 0:2 * PAR2_N], prow2[0:2 * PAR2_N, :],
                                con[0:2 * PAR2_N, 0:2 * PAR2_N]).then_inc(su_pe.sem, 1)
            pe.wait_ge(x_in, 16)
            for f in range(KT):
                if f >= 2:
                    free(f)
                for t in range(TT):
                    i = nc.tensor.transpose(psA[:, f % 2, t * P:(t + 1) * P], xin[:, t, f * P:(f + 1) * P], ident)
                i.then_inc(su_pe.sem, 1)
            norm(0, 7)
            pe.wait_ge(res_dve.sem, res_dve.at(7))
            with pe.Fori(0, 3) as i:
                for s in range(4):
                    proj(C_KV + i * 4 + s, T_KV + i * 4 + s, s)
            pe.wait_ge(cg_dve.sem, cg_dve.at(0, "gw_lo"))
            for kt in range(KT):
                i = three(psS[0:48, 0, :], lambda h: gw[:, h, kt, :], lambda h: xg[:, h, kt, :], kt == 0, kt == KT - 1)
            i.then_inc(cg_pe.sem, 1)
            pe.wait_ge(cg_dve.sem, cg_dve.at(0, "gates"))
            for t in range(TT):
                i = nc.tensor.transpose(psS[:, 1, 48 * t:48 * t + 48], gsc[0:48, t * P:(t + 1) * P], con[0:48, 0:48])
            i.then_inc(cg_pe.sem, 1)
            pe.wait_ge(e_act.sem, e_act.at(3))
            pe.wait_ge(e_dve.sem, e_dve.at(3))
            for kv in range(2):
                for s in range(4):
                    m, half = s // 2, s % 2
                    if half == 0:
                        free(T_CMP + 2 * kv + m)
                    chunk(C_CMP + 4 * kv + s, s, psA[:, m, 0:160].rearrange("p (g n) -> p g n", n=32),
                          lambda h, kt: E[:, kv, h, :, half * KT + kt:half * KT + kt + 249:8],
                          first=half == 0, last=half == 1)
            for n in range(4):
                if n:
                    pe.wait_ge(hn_dve.sem, hn_dve.at(n - 1, "newton"))
                else:
                    pe.wait_ge(nm_dve.sem, nm_dve.at(0, "newton"))
                headnorm(n, blk)
            for n in range(4):
                if n == 3:
                    pe.wait_ge(vt_dve.sem, vt_dve.at(0))
                src = kvraw[:, (6, 7, 10, 11)[n], :]
                for t in range(TT):
                    i = nc.tensor.transpose(psT[:, n % 3, t * P:(t + 1) * P], src[:, t * P:(t + 1) * P], ident)
                i.then_inc(vt_pe.sem, 1)
            pe.wait_ge(drained.sem, drained.at(T_CMP + 3))
            for kt in range(2):
                i = three(psS[:, 0, 0:P], lambda h: w2[:, 0, h, kt, :], lambda h: hidr[:, 0, h, kt, :], kt == 0, kt == 1)
            for g in range(GROUPS):
                for kt in range(2):
                    i = three(psS[0:32, 1, 256 + g * HD:256 + (g + 1) * HD],
                              lambda h: hidr[:, 1, h, kt, 32 * g:32 * g + 32],
                              lambda h: w2[:, 1, h, kt, 0:HD], kt == 0, kt == 1)
            i.then_inc(kv_pe.sem, 1)
            pe.wait_ge(hn_dve.sem, hn_dve.at(3, "newton"))
            headnorm(4, blk, P)
            for pa in range(2):
                with pe.Fori(0, 2) as i:
                    for s in range(2):
                        pair_pe(pe, chunk, free, three, headnorm, pa, i * 2 + (4 * pa + s), s)
            pe.wait_ge(lw_dve.sem, lw_dve.at(0))
            with pe.Fori(0, KT) as m:
                proj(C_LRU + m * 2, T_LRU + m * 2, 0)
                proj(C_LRU + m * 2 + 1, T_LRU + m * 2 + 1, 1)
                pe.wait_ge(lr_dve.sem, lr_dve.at(m, "w1"))
                for w in range(2):
                    three(psS[:, w, :], lambda h: bd[:, h, w, :], lambda h: xcr[:, h, :], True, True).then_inc(lr_pe.sem, 1)
            with pe.Fori(0, KT) as m:
                for s in range(4):
                    src = (xg, attnT, xg, lruT)[s]
                    proj(C_MIX + m * 4 + s, T_MIX + m * 4 + s, s, lambda h, kt: src[:, h, kt, :])
            pe.wait_ge(mx_dve.sem, mx_dve.at(7))
            tail_pe(pe, chunk, free, proj, norm, C_WO, T_WO, mrgT, 1, 8, 0)

            with pe.Fori(0, LAYERS) as l:
                c0, t0 = l * C_LAYER + C_B2, l * T_LAYER + T_B2
                pe.wait_ge(ly_dve.sem, ly_dve.at(l, "products"))
                mm(psO[:, 0:2], ones, small[:, 32:34], start=True, stop=True).then_inc(ly_pe.sem, 1)
                pe.wait_ge(ly_dve.sem, ly_dve.at(l))
                settled(pe)
                with pe.Fori(0, HEADS2) as h:
                    n = l * HEADS2 + h
                    for x in range(6):
                        proj(c0 + h * 6 + x, t0 + h * 6 + x, x)
                        if x < 4:
                            headnorm2(n, x)
                        else:
                            values2(n, x - 4)
                    attention2(n)
                with pe.Fori(0, KT // 2) as i:
                    for s in range(2):
                        proj(c0 + L_U + i * 2 + s, t0 + U_U + i * 2 + s, s)
                pe.wait_ge(up_dve.sem, up_dve.at(l))
                for g in range(4):
                    c, t = c0 + (L_PW + g), t0 + (U_PW + 2 * g)
                    pe.wait_ge(wsplit.sem, wsplit.at(c))
                    for m in range(2):
                        free(t + m)
                        for k in range(2):
                            i = three(psA[:, m, :], lambda x: wsp[:, g % SPLIT, x, 2 * k + m, :],
                                      lambda x: mix2[:, x, 2 * g + k, :], k == 0, k == 1)
                    i.then_inc(used.sem, 1)
                with pe.Fori(0, KT) as m:
                    for s in range(2):
                        proj(c0 + L_GAB + m * 2 + s, t0 + U_GAB + m * 2 + s, s)
                pe.wait_ge(m2_dve.sem, m2_dve.at(l * KT + 7))
                settled(pe)
                tail_pe(pe, chunk, free, proj, norm, c0 + L_WO, t0 + U_WO, mix2, l * 2 + 3, l * 16 + 24, l * FT + FT)
            for t in range(TT):
                if t:
                    pe.wait_ge(ou_act.sem, ou_act.at(t - 1))
                for f in range(KT):
                    i = nc.tensor.transpose(psT[:, f // 4, f % 4 * P:(f % 4 + 1) * P], xT[:, f, t * P:(t + 1) * P], ident)
                i.then_inc(ou_pe.sem, 1)

        @block.vector
        def _(dve):
            v = nc.vector
            count = [0]

            def link(i):
                i.then_inc(su_dve.sem, 1)
                count[0] += 1
                dve.wait_ge(su_dve.sem, count[0])

            def drain(c, t, s, dst):
                dve.wait_ge(used.sem, used.at(c))
                v.scalar_tensor_tensor(dst, psA[:, s % 2, :], -0.5, c_rs[:, :], ALU.mult, ALU.mult).then_inc(drained.sem, 1)

            def flat(b):
                return b[:, :, :, :].rearrange("p h k t -> p h (k t)")

            def residual(n, m, s, gain, add, c=None):
                x = xT[:, :, :].rearrange("p k t -> p (k t)")[:, bass.ds(m * T, T)]
                g2 = flat(xg)
                if add:
                    dve.wait_ge(used.sem, used.at(c))
                    v.tensor_tensor(x, x, psA[:, s, :], ALU.add).then_inc(drained.sem, 1)
                else:
                    dve.wait_ge(su_pe.sem, 3 + n)
                    v.tensor_copy(x, psA[:, s, :]).then_inc(drained.sem, 1)
                dve.wait_ge(res_act.sem, res_act.at(n, "hi"))
                v.scalar_tensor_tensor(g2[:, 1, bass.ds(m * T, T)], x, gain, hi_f(g2[:, 0, bass.ds(m * T, T)]),
                                       ALU.mult, ALU.subtract).then_inc(res_dve.sem, 1)
                dve.wait_ge(res_act.sem, res_act.at(n, "square"))
                v.tensor_tensor(acc[:, :], acc[:, :], sq[:, s, :], ALU.add).then_inc(res_dve.sem, 1)

            def norm(k):
                dve.wait_ge(nm_act.sem, nm_act.at(k))
                v.scalar_tensor_tensor(n_b[:, :], psO[:, :], D * EPS, n_r2[:, :], ALU.add, ALU.mult).then_inc(nm_dve.sem, 1)
                dve.wait_ge(nm_dve.sem, nm_dve.at(k, "newton"))
                v.scalar_tensor_tensor(c_rs[:, :], n_b[:, :], 3.0, n_r0[:, :], ALU.subtract, ALU.mult).then_inc(nm_dve.sem, 1)
                v.memset(acc[:, :], 0.0).then_inc(nm_dve.sem, 1)
                dve.wait_ge(nm_dve.sem, nm_dve.at(k))
                settled(dve)

            def headnorm(n, src, gain, dst_lo, dst_hi, dim, w=T):
                dve.wait_ge(hn_act.sem, hn_act.at(n, "root2"))
                v.scalar_tensor_tensor(n_b[:, 0:w], psO[:, 0:w], dim * EPS, n_r2[:, 0:w], ALU.add, ALU.mult).then_inc(hn_dve.sem, 1)
                dve.wait_ge(hn_dve.sem, hn_dve.at(n, "newton"))
                v.scalar_tensor_tensor(n_b[:, 0:w], n_b[:, 0:w], 3.0, n_r0[:, 0:w], ALU.subtract, ALU.mult).then_inc(hn_dve.sem, 1)
                dve.wait_ge(hn_dve.sem, hn_dve.at(n, "scale"))
                v.scalar_tensor_tensor(h_t[:, 0:w], src, gain, n_b[:, 0:w], ALU.mult, ALU.mult).then_inc(hn_dve.sem, 1)
                dve.wait_ge(hn_act.sem, hn_act.at(n, "hi"))
                v.tensor_tensor(dst_lo, h_t[:, 0:w], hi_f(dst_hi), ALU.subtract).then_inc(hn_dve.sem, 1)

            def pcol(name, i=0):
                return par[:, PAR[name].start + i:PAR[name].start + i + 1]

            v.memset(small[:, 60:61], EPS).then_inc(eps_in.sem, 1)
            link(v.memset(acc[:, :], 0.0))
            link(v.memset(par2[:, :], 0.0))
            link(v.memset(E[:, :, :, :, :].bitcast(F32), 0.0))
            dve.wait_ge(su_pe.sem, 2)
            link(v.tensor_copy(par[:, :], psT[:, 0, 0:PAR_N]))
            link(v.tensor_copy(par2[:, 0:2 * PAR2_N], psT[:, 1, 0:2 * PAR2_N]))
            for f in range(KT):
                residual(f, f, f % 2, pcol("n1", f), False)
            for name in ("qg", "kg"):
                link(v.tensor_scalar(par[:, PAR[name]], par[:, PAR[name]], -0.5, None, ALU.mult))
            dve.wait_ge(g_in, G_DMAS * 16)
            v.tensor_copy(gw[:, 0], gwraw[:, :, :]).then_inc(cg_dve.sem, 1)
            v.tensor_copy(w2[:, :, 0], w2raw[:, :, :, :]).then_inc(su_dve.sem, 1)
            count[0] += 1
            dve.wait_ge(cg_dve.sem, cg_dve.at(0, "gw_hi"))
            v.tensor_tensor(gw[:, 1], gwraw[:, :, :], hi_f(gw[:, 0]), ALU.subtract).then_inc(cg_dve.sem, 1)
            for kv in range(2):
                dve.wait_ge(su_dve.sem, count[0])
                v.tensor_tensor(w2[:, kv, 1], w2raw[:, kv], hi_f(w2[:, kv, 0]), ALU.subtract).then_inc(cg_dve.sem, 1)
            norm(0)
            for kv, name in enumerate(("posk", "posv")):
                link(v.tensor_copy(E[:, kv, 0, 4, 0:16], par[:, PAR[name]]))
                link(v.tensor_tensor(E[:, kv, 1, 4, 0:16], par[:, PAR[name]], hi_f(E[:, kv, 0, 4, 0:16]), ALU.subtract))
            kvf = kvraw[:, :, :].rearrange("p k t -> p (k t)")
            with dve.Fori(0, 3) as i:
                for s in range(4):
                    drain(C_KV + i * 4 + s, T_KV + i * 4 + s, s, kvf[:, bass.ds(i * 4 * T + s * T, T)])
            dve.wait_ge(cg_pe.sem, cg_pe.at(0, "gates"))
            v.scalar_tensor_tensor(gsc[0:48, :], psS[0:48, 0, :], -0.5, c_rs[0:48, :], ALU.mult, ALU.mult).then_inc(cg_dve.sem, 1)
            for n in range(4):
                kv, x = n // 2, n % 2
                dve.wait_ge(e_act.sem, e_act.at(n, "hi"))
                v.tensor_tensor(Et[:, 1], kvraw[:, n, :], hi_f(Et[:, 0]), ALU.subtract).then_inc(e_dve.sem, 1)
                dve.wait_ge(e_dve.sem, e_dve.at(n, "lo"))
                for odd in range(2):
                    v.tensor_copy(E[odd * HD:(odd + 1) * HD, kv, :, 2 * x + 1, 0:T // 2],
                                  Et[HD:P, :, odd::2]).then_inc(e_dve.sem, 1)
            for n in range(4):
                kv, m = n // 2, n % 2
                dve.wait_ge(used.sem, used.at(C_CMP + 2 * n + 1))
                v.tensor_tensor(bcol[:, n:n + 1], psA[:, m, P:P + 1], pcol("b1v" if kv else "b1k", m), ALU.add).then_inc(ch_dve.sem, 1)
                dve.wait_ge(ch_act.sem, ch_act.at(n))
                v.tensor_tensor(hidr[:, kv, 1, m], hidc[:, m, :], hi_f(hidr[:, kv, 0, m]), ALU.subtract).then_inc(drained.sem, 1)
            for n in range(4):
                br, x = n // 2, n % 2
                headnorm(n, kvraw[:, 4 + 4 * br + x, :], pcol("kg", 1 + br), kn[:, br, x, 1], kn[:, br, x, 0], HD)
            for n in range(4):
                br, x = n // 2, n % 2
                dve.wait_ge(vt_act.sem, vt_act.at(n))
                v.tensor_tensor(vtok[:, br, 1, :, x * P:(x + 1) * P], psT[:, n % 3, :].rearrange("p (k d) -> p k d", d=P),
                                hi_f(vtok[:, br, 0, :, x * P:(x + 1) * P]), ALU.subtract).then_inc(vt_dve.sem, 1)
            dve.wait_ge(kv_pe.sem, 1)
            v.tensor_scalar(kcraw[:, :], psS[:, 0, 0:P], pcol("b2k"), None, ALU.add).then_inc(kv_dve.sem, 1)
            v.tensor_tensor(vcraw[0:32], psS[0:32, 1, 256:512].rearrange("p (g d) -> p g d", d=HD),
                            b2v[0:32, :].unsqueeze(1).broadcast_to([32, GROUPS, HD]), ALU.add).then_inc(kv_dve.sem, 1)
            dve.wait_ge(kv_dve.sem, kv_dve.at(0, "v"))
            v.tensor_copy(vc[0:32, 0], vcraw[0:32]).then_inc(kv_dve.sem, 1)
            dve.wait_ge(kv_dve.sem, kv_dve.at(0, "v_hi"))
            v.tensor_tensor(vc[0:32, 1], vcraw[0:32], hi_f(vc[0:32, 0]), ALU.subtract).then_inc(kv_dve.sem, 1)
            headnorm(4, kcraw[:, :], pcol("kg", 0), kc[:, 1], kc[:, 0], HD, P)

            def pair(pa, i, n, s):
                def own(name):
                    dve.wait_ge(at_dve.sem, at_dve.at(n, name))

                def act(name):
                    dve.wait_ge(at_act.sem, at_act.at(n, name))

                def pes(name):
                    dve.wait_ge(at_pe.sem, at_pe.at(n, name))

                def step(ins):
                    ins.then_inc(at_dve.sem, 1)

                drain(C_Q + n, T_Q + n, s, qraw[:, :])
                headnorm(n + 5, qraw[:, :], pcol("qg"), qn[:, 1], qn[:, 0], HD)
                for hd in range(2):
                    sl = con[:, bass.ds(i + (CONST["slope"].start + 4 * pa + 8 * hd), 1)]
                    step(v.tensor_scalar(bias[:, hd, :], con[:, CONST["dist"]], sl, None, ALU.mult))
                for hd in range(2):
                    sl = con[:, bass.ds(i + (CONST["slope"].start + 4 * pa + 8 * hd), 1)]
                    step(v.tensor_scalar(cbias[:, hd, :], con[:, CONST["cdist"]], sl, None, ALU.mult))
                pc = Pc[:, :, :, :].rearrange("p h q n -> p (h q) n")
                own("cbias1")
                pes("c_s")
                step(v.tensor_tensor(Pc[:, :, :, :].rearrange("p h q n -> p h (q n)"), psS[:, :, 0:P], cbias[:, :, :], ALU.add))
                own("c_add")
                step(v.tensor_reduce(cst[:, 0:8], pc, AX.X, ALU.max))
                own("c_max")
                step(v.tensor_tensor(pc, pc, cst[:, 0:8].unsqueeze(2).broadcast_to([P, 8, 32]), ALU.subtract))

                def maxima(u):
                    hd, o = u // 2, 32 * (u % 2)
                    for x, qt in enumerate((3, 2, 1, 0)):
                        w = P * (qt + 1)
                        pes(f"s{u}_{x}")
                        settled(dve)
                        step(v.tensor_tensor_reduce(out=Pm[:, u % 2, P_AT[qt]:P_AT[qt] + w], in0=bias[:, hd, T - w:T],
                                                    in1=psS[:, x % 2, 0:w], scale=1.0, scalar=-3e38, op0=ALU.add,
                                                    op1=ALU.max, accum_out=st[:, o + qt:o + qt + 1]))
                    own(f"max{u}_3")
                    step(v.tensor_scalar(st[:, o + 4:o + 8], st[:, o:o + 4], -HD ** -0.5, None, ALU.mult))

                def scale(u):
                    hd, br, o = u // 2, u % 2, 32 * (u % 2)
                    act(f"exp{u}_3")
                    step(v.reciprocal(st[:, o + 12:o + 16], st[:, o + 8:o + 12]))
                    own(f"rec{u}")
                    gt = gates[:, :, bass.ds(i * 3 + (3 * (4 * pa + 8 * hd) + 1 + br), 1)]
                    step(v.tensor_tensor(st[:, o + 16:o + 20].unsqueeze(2), st[:, o + 12:o + 16].unsqueeze(2), gt, ALU.mult))
                    own(f"gate{u}")
                    for qt in range(TT):
                        pq = Pm[:, u % 2, P_AT[qt]:P_AT[qt] + P * (qt + 1)]
                        step(v.tensor_scalar(pq, pq, st[:, o + 16 + qt:o + 17 + qt], None, ALU.mult))

                def lo(u):
                    act(f"hi{u}")
                    step(v.tensor_tensor(PT[:, 1, :], psT[:, :, :].rearrange("p b t -> p (b t)")[:, 0:1280],
                                         hi_f(PT[:, 0, :]), ALU.subtract))

                def c_lo(hd):
                    act(f"c_hi{hd}")
                    step(v.tensor_tensor(PT[0:32, 1, 0:T], psT[0:32, 0, :], hi_f(PT[0:32, 0, 0:T]), ALU.subtract))

                def out_lo(hd):
                    rows, at = slice(hd * HD, (hd + 1) * HD), bass.ds(n * T, T)
                    act(f"out{hd}")
                    step(v.tensor_tensor(flat(attnT)[rows, 1, at], psO[0:HD, :], hi_f(flat(attnT)[rows, 0, at]), ALU.subtract))

                maxima(0)
                act("c_exp")
                step(v.tensor_tensor(Pc[:, :, :, :].rearrange("p h q n -> p h (q n)"), Pc[:, :, :, :].rearrange("p h q n -> p h (q n)"),
                                     con[:, CONST["cmask"]].unsqueeze(1).broadcast_to([P, 2, TT * 32]), ALU.mult))
                own("c_mask")
                step(v.tensor_reduce(cst[:, 8:16], pc, AX.X, ALU.add))
                own("c_sum")
                step(v.tensor_scalar(cst[:, 16:24], cst[:, 8:16], 1e-30, None, ALU.max))
                own("c_guard")
                step(v.reciprocal(cst[:, 24:32], cst[:, 16:24]))
                own("c_rec")
                gt = gates[:, :, :].rearrange("p q (b g i r) -> p g b q i r", g=2, b=2, i=4)[:, pa, :, :, bass.ds(i, 1), 0]
                step(v.tensor_tensor(cst[:, 32:40].rearrange("p (b q o) -> p b q o", b=2, o=1),
                                     cst[:, 24:32].rearrange("p (b q o) -> p b q o", b=2, o=1), gt, ALU.mult))
                own("c_gate")
                step(v.tensor_tensor(pc, pc, cst[:, 32:40].unsqueeze(2).broadcast_to([P, 8, 32]), ALU.mult))
                c_lo(0)
                maxima(1)
                scale(0)
                lo(0)
                maxima(2)
                scale(1)
                lo(1)
                out_lo(0)
                c_lo(1)
                maxima(3)
                scale(2)
                lo(2)
                scale(3)
                lo(3)
                out_lo(1)

            for pa in range(2):
                with dve.Fori(0, 2) as i:
                    for s in range(2):
                        pair(pa, i * 2 + s, i * 2 + (4 * pa + s), s)

            dve.wait_ge(at_pe.sem, at_pe.at(7))
            lam = par[:, PAR["lam"]]
            z, f1, f2, f3 = (small[:, 16 + 8 * j:24 + 8 * j] for j in range(4))
            v.scalar_tensor_tensor(z, lam, -1.0, lam, ALU.mult, ALU.max).then_inc(sp_dve.sem, 1)
            dve.wait_ge(sp_act.sem, 1)
            link(v.tensor_scalar(f1, z, 2.0, None, ALU.add))
            link(v.reciprocal(f2, f1))
            link(v.tensor_tensor(f1, z, f2, ALU.mult))
            link(v.tensor_tensor(f2, f1, f1, ALU.mult))
            link(v.tensor_scalar(f3, f2, 1.0 / 19, None, ALU.mult))
            for odd in (17, 15, 13, 11, 9, 7, 5, 3):
                link(v.scalar_tensor_tensor(f3, f3, 1.0 / odd, f2, ALU.add, ALU.mult))
            link(v.scalar_tensor_tensor(f3, f3, 1.0, f1, ALU.add, ALU.mult))
            link(v.tensor_scalar(f1, lam, -8.0, 0.0, ALU.mult, ALU.max))
            link(v.scalar_tensor_tensor(small[:, 0:8], f3, 16.0, f1, ALU.mult, ALU.add))
            link(v.tensor_scalar(small[:, 8:16], small[:, 0:8], -1.0, None, ALU.mult))
            v.memset(bd[:, :, :, :].bitcast(F32), 0.0).then_inc(lw_dve.sem, 1)
            v.memset(lx[:, 0:3], 0.0).then_inc(lw_dve.sem, 1)
            dve.wait_ge(lw_dve.sem, lw_dve.at(0))
            dve.wait_ge(lw_in, 32)

            def col(name, i):
                return par[:, bass.ds(i + PAR[name].start, 1)]

            r_, i_, t_, a_, s_, o_, u_ = lt
            with dve.Fori(0, KT) as m:
                def step(i):
                    i.then_inc(lr_dve.sem, 1)

                def own(name):
                    dve.wait_ge(lr_dve.sem, lr_dve.at(m, name))

                def act(name):
                    dve.wait_ge(lr_act.sem, lr_act.at(m, name))

                drain(C_LRU + m * 2, T_LRU + m * 2, 0, lx[:, 3:T + 3])
                dve.wait_ge(drained.sem, drained.at(T_LRU + m * 2))
                step(v.tensor_scalar(xc[:, :], lx[:, 3:T + 3], col("cw", m + 3 * KT), col("cb", m), ALU.mult, ALU.add))
                for k in range(3):
                    own(f"tap{k}")
                    step(v.scalar_tensor_tensor(xc[:, :], lx[:, 2 - k:T + 2 - k], col("cw", m + (2 - k) * KT), xc[:, :],
                                                ALU.mult, ALU.add))
                drain(C_LRU + m * 2 + 1, T_LRU + m * 2 + 1, 1, gl[:, :])
                act("hi")
                step(v.tensor_tensor(xcr[:, 1], xc[:, :], hi_f(xcr[:, 0]), ALU.subtract))
                for b in range(2):
                    rows = slice(b * HD, (b + 1) * HD)
                    act(f"w{b}")
                    raw = lruw[:, :, :, :].rearrange("p w m j -> p w (m j)")[rows, :, bass.ds(m * HD, HD)]
                    step(v.tensor_tensor(bd[rows, 1, :, rows], raw, hi_f(bd[rows, 0, :, rows]), ALU.subtract))
                act("tanh")
                step(v.tensor_scalar(u_[:, :], t_[:, :], 1.0, None, ALU.add))
                own("one")
                step(v.reciprocal(u_[:, :], u_[:, :]))
                own("rec")
                step(v.tensor_tensor(u_[:, :], u_[:, :], t_[:, :], ALU.mult))
                step(v.tensor_tensor(o_[:, :], i_[:, :], xc[:, :], ALU.mult))
                act("root")
                own("ix")
                step(v.tensor_tensor(u_[:, :], s_[:, :], o_[:, :], ALU.mult))
                own("b")
                step(v.tensor_tensor_scan(o_[:, :], a_[:, :], u_[:, :], 0.0, ALU.mult, ALU.add))
                own("scan")
                step(v.tensor_tensor(u_[:, :], o_[:, :], gl[:, :], ALU.mult))
                act("out_hi")
                at = bass.ds(m * T, T)
                step(v.tensor_tensor(flat(lruT)[:, 1, at], u_[:, :], hi_f(flat(lruT)[:, 0, at]), ALU.subtract))
                own("out_lo")

            with dve.Fori(0, KT) as m:
                for g in range(2):
                    drain(C_MIX + m * 4 + 2 * g, T_MIX + m * 4 + 2 * g, 0, mg[:, g, :])
                    dve.wait_ge(used.sem, used.at(C_MIX + m * 4 + 2 * g + 1))
                    dve.wait_ge(mx_act.sem, mx_act.at(m, f"gate{g}"))
                    v.tensor_tensor(mg[:, g, :], mg[:, g, :], psA[:, 1, :], ALU.mult).then_inc(drained.sem, 1)
                dve.wait_ge(drained.sem, drained.at(T_MIX + m * 4 + 3))
                v.tensor_tensor(mt[:, :], mg[:, 0, :], mg[:, 1, :], ALU.add).then_inc(mx_dve.sem, 1)
                dve.wait_ge(mx_act.sem, mx_act.at(m, "hi"))
                at = bass.ds(m * T, T)
                v.tensor_tensor(flat(mrgT)[:, 1, at], mt[:, :], hi_f(flat(mrgT)[:, 0, at]), ALU.subtract).then_inc(mx_dve.sem, 1)

            def tail_dve(c0, t0, k, n, ff, gain2, gain1):
                with dve.Fori(0, 4) as i:
                    for s in range(2):
                        residual(i * 2 + (n + s), i * 2 + s, s, gain2(i * 2 + s), True, c0 + i * 2 + s)
                norm(k)
                hf = flat(hid)
                with dve.Fori(0, FT) as f:
                    c, t = c0 + 8 + f * 2, t0 + 8 + f * 2
                    drain(c, t, 0, fg[:, 0, :])
                    drain(c + 1, t + 1, 1, fu[:, :])
                    dve.wait_ge(drained.sem, drained.at(t + 1))
                    dve.wait_ge(ff_act.sem, ff_act.at(f + ff, "silu"))
                    v.tensor_tensor(ft[:, :], fg[:, 1, :], fu[:, :], ALU.mult).then_inc(ff_dve.sem, 1)
                    dve.wait_ge(ff_act.sem, ff_act.at(f + ff, "hi"))
                    at = bass.ds(f * T, T)
                    v.tensor_tensor(hf[:, 1, at], ft[:, :], hi_f(hf[:, 0, at]), ALU.subtract).then_inc(ff_dve.sem, 1)
                c1, t1 = c0 + 8 + 2 * FT, t0 + 8 + 2 * FT
                with dve.Fori(0, 4) as i:
                    for s in range(2):
                        residual(i * 2 + (n + 8 + s), i * 2 + s, s, gain1(i * 2 + s), True, c1 + i * 6 + (3 * s + 2))
                norm(k + 1)

            def col2(i):
                return par2[:, bass.ds(i, 1)]

            tail_dve(C_WO, T_WO, 1, 8, 0, lambda m: col("n2", m), lambda m: col2(m + PAR2["n1"].start))

            def layer_col(name, m=0):
                return lay[:, PAR2[name].start + m:PAR2[name].start + m + 1]

            def headnorm2(n, x):
                c = n * 4 + x

                def step(i, name):
                    i.then_inc(h2_dve.sem, 1)
                    dve.wait_ge(h2_dve.sem, h2_dve.at(c, name))

                r32 = slice(0, 32)
                dve.wait_ge(h2_act.sem, h2_act.at(c, "root2"))
                step(v.scalar_tensor_tensor(n_b[:, :], psO[:, :], QK2 * EPS, n_r2[:, :], ALU.add, ALU.mult), "newton")
                step(v.scalar_tensor_tensor(n_b[:, :], n_b[:, :], 3.0, n_r0[:, :], ALU.subtract, ALU.mult), "scale")
                step(v.scalar_tensor_tensor(h_t[:, :], raw2[:, x, :], layer_col("kg" if x >= 2 else "qg"), n_b[:, :], ALU.mult, ALU.mult), "apply")
                settled(dve)
                step(v.stream_shuffle(rot[r32, :], h_t[r32, :], [(p + 16) % 32 for p in range(32)]), "swap")
                step(v.tensor_tensor(rot[r32, :], rot[r32, :], con[r32, CONST["sin"]], ALU.mult), "sin")
                step(v.tensor_tensor(h_t[r32, :], h_t[r32, :], con[r32, CONST["cos"]], ALU.mult), "cos")
                step(v.tensor_tensor(h_t[r32, :], h_t[r32, :], rot[r32, :], ALU.add), "rot")
                dve.wait_ge(h2_act.sem, h2_act.at(c, "hi"))
                v.tensor_tensor(qk2[:, x, 1], h_t[:, :], hi_f(qk2[:, x, 0]), ALU.subtract).then_inc(h2_dve.sem, 1)

            def values2(n, x):
                dve.wait_ge(v2_act.sem, v2_act.at(n * 2 + x))
                at = slice(x * P, (x + 1) * P)
                v.tensor_tensor(vtok2[:, 1, :, at], psT[:, x, :].rearrange("p (k d) -> p k d", d=P), hi_f(vtok2[:, 0, :, at]),
                                ALU.subtract).then_inc(v2_dve.sem, 1)

            def attention2(l, h):
                n = l * HEADS2 + h

                def step(i):
                    i.then_inc(a2_dve.sem, 1)

                def own(name):
                    dve.wait_ge(a2_dve.sem, a2_dve.at(n, name))

                def act(name):
                    dve.wait_ge(a2_act.sem, a2_act.at(n, name))

                for c in range(2):
                    o = 32 * c
                    for x, qt in enumerate((3, 2, 1, 0)):
                        w = P * (qt + 1)
                        dve.wait_ge(a2_pe.sem, a2_pe.at(n, f"s{c}_{x}"))
                        settled(dve)
                        step(v.tensor_tensor_reduce(out=Pm2[:, c, P_AT[qt]:P_AT[qt] + w], in0=con[:, CONST["chunk"]][:, T - w:T],
                                                    in1=psS[:, x % 2, 0:w], scale=1.0, scalar=-3.3e38, op0=ALU.add, op1=ALU.max,
                                                    accum_out=st2[:, o + qt:o + qt + 1]))
                    own(f"max{c}_3")
                    step(v.tensor_scalar(st2[:, o + 4:o + 8], st2[:, o:o + 4], -QK2 ** -0.5, None, ALU.mult))
                act("exp1_3")
                sums = st2[:, :].rearrange("p (c x) -> p c x", c=2)
                step(v.reciprocal(sums[:, :, 12:16], sums[:, :, 8:12]))
                own("rec")
                step(v.tensor_scalar(st2[:, 48:52], st2[:, 44:48], small[:, 36:37], None, ALU.mult))
                own("neg")
                for qt in range(TT):
                    at = slice(P_AT[qt], P_AT[qt] + P * (qt + 1))
                    step(v.tensor_scalar(Pm2[:, 0, at], Pm2[:, 0, at], st2[:, 12 + qt:13 + qt], None, ALU.mult))
                for qt in range(TT):
                    at = slice(P_AT[qt], P_AT[qt] + P * (qt + 1))
                    own(f"scale{qt}")
                    step(v.scalar_tensor_tensor(Pm2[:, 0, at], Pm2[:, 1, at], st2[:, 48 + qt:49 + qt], Pm2[:, 0, at], ALU.mult, ALU.add))
                act("hi")
                step(v.tensor_tensor(PT2[:, 1, :], psT[:, :, :].rearrange("p b t -> p (b t)")[:, 0:1280], hi_f(PT2[:, 0, :]), ALU.subtract))
                dve.wait_ge(a2_pe.sem, a2_pe.at(n, "v"))
                for d in range(2):
                    step(v.tensor_copy(os2[:, d, :], psS[:, d, :]))
                act("root2")
                step(v.scalar_tensor_tensor(n_b[:, :], psO[:, :], V2 * EPS, n_r2[:, :], ALU.add, ALU.mult))
                own("newton")
                step(v.scalar_tensor_tensor(n_b[:, :], n_b[:, :], 3.0, n_r0[:, :], ALU.subtract, ALU.mult))
                own("scale")
                af = aT2[:, :, :].rearrange("p k t -> p (k t)")
                for d in range(2):
                    step(v.scalar_tensor_tensor(af[:, bass.ds(h * 2 * T + d * T, T)], os2[:, d, :], layer_col("sub", d), n_b[:, :],
                                                ALU.mult, ALU.mult))
                own("out1")

            with dve.Fori(0, LAYERS) as l:
                c0, t0 = l * C_LAYER + C_B2, l * T_LAYER + T_B2

                def once(i, name):
                    i.then_inc(ly_dve.sem, 1)
                    dve.wait_ge(ly_dve.sem, ly_dve.at(l, name))

                once(v.tensor_copy(lay[:, :], par2[:, bass.ds(l * PAR2_N, PAR2_N + KT)]), "copy")
                once(v.tensor_scalar(lay[:, PAR2["qg"].start:PAR2["kg"].stop], lay[:, PAR2["qg"].start:PAR2["kg"].stop], -0.5, None, ALU.mult), "gains")
                init = con[:, bass.ds(l * 2 + CONST["lam"].start, 1)]
                once(v.tensor_scalar(lay[:, PAR2["sub"]], lay[:, PAR2["sub"]], con[:, bass.ds(l * 2 + (CONST["lam"].start + 1), 1)], None, ALU.mult), "sub")
                lq = lay[:, PAR2["lam"]].rearrange("p (c x) -> p c x", x=2)
                once(v.tensor_tensor(small[:, 32:34].unsqueeze(2), lq[:, :, 0:1], lq[:, :, 1:2], ALU.mult), "products")
                dve.wait_ge(ly_act.sem, ly_act.at(l))
                once(v.tensor_tensor(small[:, 36:37], small[:, 35:36], small[:, 34:35], ALU.subtract), "diff")
                once(v.tensor_tensor(small[:, 36:37], small[:, 36:37], init, ALU.subtract), "lambda")
                settled(dve)
                with dve.Fori(0, HEADS2) as h:
                    n = l * HEADS2 + h
                    for x in range(6):
                        if x < 4:
                            drain(c0 + h * 6 + x, t0 + h * 6 + x, x, raw2[:, x, :])
                            headnorm2(n, x)
                        else:
                            drain(c0 + h * 6 + x, t0 + h * 6 + x, x, raw2[:, x, :])
                            dve.wait_ge(drained.sem, drained.at(t0 + h * 6 + x))
                            v.sem_inc(v2_raw.sem, 1)
                            values2(n, x - 4)
                    attention2(l, h)

                def upool(i):
                    i.then_inc(up_dve.sem, 1)

                for b in range(2):
                    upool(v.memset(ur[:, b, 0:16], 0.0))
                edge = CONST["edge"].start
                for m in range(KT):
                    g = m // 2
                    w, e = POOL_W[g], edge + sum(POOL_W[:g])
                    t, c = t0 + (U_U + m), c0 + (L_U + m)
                    drain(c, t, m, ur[:, m % 2, 16:T + 16])
                    dve.wait_ge(drained.sem, drained.at(t))
                    src = ur[:, m % 2]
                    for k in range(g + 1):
                        dst, b = (ya, yb)[k % 2], 1 << k
                        lo = 2 * b - 1
                        upool(v.tensor_tensor(dst[:, lo:T + 16], src[:, lo:T + 16], src[:, lo - b:T + 16 - b], ALU.add))
                        dve.wait_ge(up_dve.sem, up_dve.at(l, f"y{m}_{k}"))
                        src = dst
                    upool(v.tensor_tensor(src[:, 16:16 + w], src[:, 16:16 + w], con[:, e:e + w], ALU.mult))
                    dve.wait_ge(up_dve.sem, up_dve.at(l, f"edge{m}"))
                    upool(v.scalar_tensor_tensor(pr[:, :], src[:, 16:T + 16], 1.0 / w, ur[:, m % 2, 16:T + 16], ALU.mult, ALU.subtract))
                    dve.wait_ge(up_act.sem, up_act.at(l * KT + m))
                    upool(v.tensor_tensor(mix2[:, 1, m], pr[:, :], hi_f(mix2[:, 0, m]), ALU.subtract))
                for m in range(KT):
                    dve.wait_ge(used.sem, used.at(c0 + (L_PW + m // 2)))
                    v.tensor_scalar(poolT[:, m, :], psA[:, m % 2, :], layer_col("ps", m), None, ALU.mult).then_inc(drained.sem, 1)
                dve.wait_ge(drained.sem, drained.at(t0 + (U_PW + 7)))
                settled(dve)
                pf, af = (x[:, :, :].rearrange("p k t -> p (k t)") for x in (poolT, aT2))
                with dve.Fori(0, KT) as m:
                    n = l * KT + m
                    at = bass.ds(m * T, T)
                    for s in range(2):
                        drain(c0 + L_GAB + m * 2 + s, t0 + U_GAB + m * 2 + s, s, mg2[:, s, :])
                    for s, (name, src) in enumerate((("ga", pf), ("gb", af))):
                        dve.wait_ge(m2_act.sem, m2_act.at(n, name))
                        v.tensor_tensor(mg2[:, s, :], mg2[:, s, :], src[:, at], ALU.mult).then_inc(m2_dve.sem, 1)
                    dve.wait_ge(m2_dve.sem, m2_dve.at(n, "attn"))
                    v.tensor_tensor(mt2[:, :], mg2[:, 0, :], mg2[:, 1, :], ALU.add).then_inc(m2_dve.sem, 1)
                    dve.wait_ge(m2_act.sem, m2_act.at(n, "hi"))
                    v.tensor_tensor(flat(mix2)[:, 1, at], mt2[:, :], hi_f(flat(mix2)[:, 0, at]), ALU.subtract).then_inc(m2_dve.sem, 1)

                def gain(name):
                    start = PAR2_N if name == "next" else PAR2[name].start
                    return lambda m: lay[:, bass.ds(m + start, 1)]

                tail_dve(c0 + L_WO, t0 + U_WO, l * 2 + 3, l * 16 + 24, l * FT + FT, gain("n2"), gain("next"))

        @block.scalar
        def _(act):
            ac = nc.scalar.activation

            def flat(b):
                return b[:, :, :, :].rearrange("p h k t -> p h (k t)")

            act.dma_start(con[:, :], a["const"]).then_inc(c_in, 16)
            done = [0]

            def rows(dst, r0, src, cols=slice(0, P)):
                n = src.shape[0]
                act.dma_start(dst[r0:r0 + n, cols], src).then_inc(p_in, 16)
                done[0] += 1

            def vec(name, l=0):
                return a[name][l].rearrange("(r p) -> r p", p=P)

            for key, name in (("n1", "norm1_g"), ("n2", "norm2_g"), ("cb", "conv_b"), ("ba", "lru_ba"), ("bi", "lru_bi"),
                              ("lam", "lru_lambda"), ("b1k", "cmp_b1_k"), ("b1v", "cmp_b1_v")):
                rows(prow, PAR[key].start, vec(name))
            rows(prow, PAR["cw"].start, a["conv_w"][0].rearrange("k o (m p) -> (k o m) p", p=P))
            for half in range(2):
                cols = slice(half * HD, (half + 1) * HD)
                rows(prow, PAR["qg"].start, a["q_norm_g"], cols)
                rows(prow, PAR["kg"].start, a["k_norm_g"][0], cols)
                rows(prow, PAR["b2k"].start, a["cmp_b2_k"], cols)
            for key, name in (("posk", "cmp_pos_k"), ("posv", "cmp_pos_v")):
                rows(prow, PAR[key].start, a[name][0].rearrange("(j l) d -> j (l d)", l=2))
            for l in range(LAYERS):
                for key, name in (("n1", "norm1_g_2"), ("n2", "norm2_g_2"), ("ps", "pool_scale_2"), ("qg", "q_norm_g_2"),
                                  ("kg", "k_norm_g_2"), ("sub", "subln_g_2")):
                    rows(prow2, l * PAR2_N + PAR2[key].start, vec(name, l))
                for j, name in enumerate(("lam_q1_2", "lam_k1_2", "lam_q2_2", "lam_k2_2")):
                    rows(prow2, l * PAR2_N + PAR2["lam"].start + j, vec(name, l))
            assert done[0] == P_DMAS, done
            gd = 0
            for dst, src in ((gwraw[:, :, :], w_in.rearrange("(k p) n -> p k n", p=P)[:, :, 2560:2608]),
                             (w2raw[:, 0, :, 0:HD], a["cmp_w2_k"][0].rearrange("(k p) d -> p k d", p=P)),
                             (w2raw[:, 0, :, HD:P], a["cmp_w2_k"][0].rearrange("(k p) d -> p k d", p=P)),
                             (w2raw[:, 1, :, 0:HD], a["cmp_w2_v"][0].rearrange("(k p) d -> p k d", p=P)),
                             (w2raw[:, 1, :, HD:P], a["cmp_w2_v"][0].rearrange("(k p) d -> p k d", p=P)),
                             (b2v[0:32, :], a["cmp_b2_v"][0].partition_broadcast(32))):
                act.dma_start(dst, src).then_inc(g_in, 16)
                gd += 1
            assert gd == G_DMAS

            def residual(n, t, m, s, gain):
                x = xT[:, :, :].rearrange("p k t -> p (k t)")[:, bass.ds(m * T, T)]
                act.wait_ge(drained.sem, drained.at(t))
                ac(flat(xg)[:, 0, bass.ds(m * T, T)], x, ACT.Copy, scale=gain).then_inc(res_act.sem, 1)
                ac(sq[:, s, :], x, ACT.Square).then_inc(res_act.sem, 1)

            def norm(k):
                act.wait_ge(nm_pe.sem, nm_pe.at(k))
                ac(n_r0[:, :], psO[:, :], ACT.Abs_reciprocal_sqrt, bias=small[:, 60:61], scale=1.0 / D).then_inc(nm_act.sem, 1)
                act.wait_ge(nm_act.sem, nm_act.at(k, "root"))
                ac(n_r2[:, :], n_r0[:, :], ACT.Square, scale=D ** -0.5).then_inc(nm_act.sem, 1)

            def headnorm(n, src, dst_hi, dim, w=T):
                ac(h_sq[:, 0:w], src, ACT.Square).then_inc(hn_act.sem, 1)
                act.wait_ge(hn_pe.sem, hn_pe.at(n))
                ac(n_r0[:, 0:w], psO[:, 0:w], ACT.Abs_reciprocal_sqrt, bias=small[:, 60:61], scale=1.0 / dim).then_inc(hn_act.sem, 1)
                act.wait_ge(hn_act.sem, hn_act.at(n, "root"))
                ac(n_r2[:, 0:w], n_r0[:, 0:w], ACT.Square, scale=dim ** -0.5).then_inc(hn_act.sem, 1)
                act.wait_ge(hn_dve.sem, hn_dve.at(n, "apply"))
                ac(dst_hi, h_t[:, 0:w], ACT.Copy).then_inc(hn_act.sem, 1)

            def pcol(name, i=0):
                return par[:, PAR[name].start + i:PAR[name].start + i + 1]

            act.wait_ge(eps_in.sem, 1)
            for f in range(KT):
                residual(f, f, f, f % 2, pcol("n1", f))
            norm(0)
            for n in range(4):
                kv, x = n // 2, n % 2
                if n:
                    act.wait_ge(e_dve.sem, e_dve.at(n - 1))
                    act.wait_ge(e_act.sem, e_act.at(n - 1))
                act.wait_ge(drained.sem, drained.at(T_KV + n))
                ac(Et[:, 0], kvraw[:, n, :], ACT.Copy).then_inc(e_act.sem, 1)
                act.wait_ge(e_dve.sem, e_dve.at(n, "lo"))
                for odd in range(2):
                    ac(E[odd * HD:(odd + 1) * HD, kv, :, 2 * x, 0:T // 2], hi_f(Et[0:HD, :, odd::2]), ACT.Copy).then_inc(e_act.sem, 1)
            act.wait_ge(cg_pe.sem, cg_pe.at(0))
            ac(gates[:, :, :], psS[:, 1, 0:192].rearrange("p (t g) -> p t g", g=48), ACT.Sigmoid).then_inc(cg_act.sem, 1)
            for n in range(4):
                kv, m = n // 2, n % 2
                act.wait_ge(ch_dve.sem, n + 1)
                ac(hidc[:, m, :], psA[:, m, 0:P], ACT.Gelu_apprx_tanh, bias=bcol[:, n:n + 1]).then_inc(ch_act.sem, 1)
                act.wait_ge(ch_act.sem, ch_act.at(n, "gelu"))
                ac(hidr[:, kv, 0, m], hidc[:, m, :], ACT.Copy).then_inc(ch_act.sem, 1)
            for n in range(4):
                br, x = n // 2, n % 2
                headnorm(n, kvraw[:, 4 + 4 * br + x, :], kn[:, br, x, 0], HD)
            for n in range(4):
                br, x = n // 2, n % 2
                act.wait_ge(vt_pe.sem, vt_pe.at(n))
                ac(vtok[:, br, 0, :, x * P:(x + 1) * P], psT[:, n % 3, :].rearrange("p (k d) -> p k d", d=P), ACT.Copy).then_inc(vt_act.sem, 1)
            act.wait_ge(kv_dve.sem, kv_dve.at(0, "k"))
            headnorm(4, kcraw[:, :], kc[:, 0], HD, P)

            def pair(n, s):
                def own(name):
                    act.wait_ge(at_act.sem, at_act.at(n, name))

                def dve(name):
                    act.wait_ge(at_dve.sem, at_dve.at(n, name))

                def pes(name):
                    act.wait_ge(at_pe.sem, at_pe.at(n, name))

                def step(i):
                    i.then_inc(at_act.sem, 1)

                act.wait_ge(drained.sem, drained.at(T_Q + n))
                headnorm(n + 5, qraw[:, :], qn[:, 0], HD)
                pcf = Pc[:, :, :, :].rearrange("p h q n -> p (h q n)")
                dve("c_sub")
                step(ac(pcf, pcf, ACT.Exp, scale=HD ** -0.5))

                def exps(u):
                    o = 32 * (u % 2)
                    dve(f"max{u}")
                    for qt in range(TT):
                        pq = Pm[:, u % 2, P_AT[qt]:P_AT[qt] + P * (qt + 1)]
                        step(ac(pq, pq, ACT.Exp, bias=st[:, o + 4 + qt:o + 5 + qt], scale=HD ** -0.5,
                                accum_out=st[:, o + 8 + qt:o + 9 + qt]))

                def hi(u):
                    pes(f"t{u}")
                    if u in (1, 3):
                        pes(f"v{u - 1}")
                    elif u == 0:
                        pes("c_v0")
                    else:
                        pes("c_v1")
                    step(ac(PT[:, 0, :], psT[:, :, :].rearrange("p b t -> p (b t)")[:, 0:1280], ACT.Copy))

                def c_hi(hd):
                    pes(f"c_t{hd}")
                    step(ac(PT[0:32, 0, 0:T], psT[0:32, 0, :], ACT.Copy))

                def out_hi(hd):
                    pes(f"v{2 * hd + 1}")
                    step(ac(flat(attnT)[hd * HD:(hd + 1) * HD, 0, bass.ds(n * T, T)], psO[0:HD, :], ACT.Copy))

                exps(0)
                c_hi(0)
                exps(1)
                hi(0)
                exps(2)
                hi(1)
                out_hi(0)
                c_hi(1)
                exps(3)
                hi(2)
                hi(3)
                out_hi(1)

            for pa in range(2):
                with act.Fori(0, 2) as i:
                    for s in range(2):
                        pair(i * 2 + (4 * pa + s), s)

            act.wait_ge(at_pe.sem, at_pe.at(7))
            act.wait_ge(at_dve.sem, at_dve.at(7))
            for w, name in enumerate(("lru_wa", "lru_wi")):
                act.dma_start(lruw[:, w, :, :], a[name][0].rearrange("(m b) k j -> (b k) m j", b=2)).then_inc(lw_in, 16)
            z = small[:, 16:24]
            act.wait_ge(sp_dve.sem, 1)
            ac(z, z, ACT.Exp, scale=-1.0).then_inc(sp_act.sem, 1)
            act.wait_ge(lw_in, 32)
            act.wait_ge(lw_dve.sem, lw_dve.at(0))

            def col(name, i):
                return par[:, bass.ds(i + PAR[name].start, 1)]

            r_, i_, t_, a_, s_, o_, u_ = lt
            with act.Fori(0, KT) as m:
                def step(i):
                    i.then_inc(lr_act.sem, 1)

                def own(name):
                    act.wait_ge(lr_act.sem, lr_act.at(m, name))

                def dve(name):
                    act.wait_ge(lr_dve.sem, lr_dve.at(m, name))

                dve("tap3")
                step(ac(xcr[:, 0], xc[:, :], ACT.Copy))
                for b in range(2):
                    rw = slice(b * HD, (b + 1) * HD)
                    raw = lruw[:, :, :, :].rearrange("p w m j -> p w (m j)")[rw, :, bass.ds(m * HD, HD)]
                    step(ac(bd[rw, 0, :, rw], raw, ACT.Copy))
                act.wait_ge(drained.sem, drained.at(T_LRU + m * 2 + 1))
                step(ac(gl[:, :], gl[:, :], ACT.Gelu_apprx_tanh))
                act.wait_ge(lr_pe.sem, lr_pe.at(m))
                step(ac(r_[:, :], psS[:, 0, :], ACT.Sigmoid, bias=col("ba", m)))
                step(ac(i_[:, :], psS[:, 1, :], ACT.Sigmoid, bias=col("bi", m)))
                own("r")
                step(ac(t_[:, :], r_[:, :], ACT.Tanh, scale=small[:, bass.ds(m, 1)]))
                step(ac(a_[:, :], r_[:, :], ACT.Exp, scale=small[:, bass.ds(m + 8, 1)]))
                dve("ratio")
                step(ac(s_[:, :], u_[:, :], ACT.Sqrt, scale=2.0))
                dve("out")
                step(ac(flat(lruT)[:, 0, bass.ds(m * T, T)], u_[:, :], ACT.Copy))

            with act.Fori(0, KT) as m:
                for g in range(2):
                    act.wait_ge(drained.sem, drained.at(T_MIX + m * 4 + 2 * g))
                    ac(mg[:, g, :], mg[:, g, :], ACT.Sigmoid).then_inc(mx_act.sem, 1)
                act.wait_ge(mx_dve.sem, mx_dve.at(m, "sum"))
                ac(flat(mrgT)[:, 0, bass.ds(m * T, T)], mt[:, :], ACT.Copy).then_inc(mx_act.sem, 1)

            def tail_act(t0, k, n, ff, gain2, gain1):
                with act.Fori(0, 4) as i:
                    for s in range(2):
                        residual(i * 2 + (n + s), t0 + i * 2 + s, i * 2 + s, s, gain2(i * 2 + s))
                norm(k)
                with act.Fori(0, FT) as f:
                    act.wait_ge(drained.sem, drained.at(t0 + 8 + f * 2))
                    ac(fg[:, 1, :], fg[:, 0, :], ACT.Silu).then_inc(ff_act.sem, 1)
                    act.wait_ge(ff_dve.sem, ff_dve.at(f + ff, "product"))
                    ac(flat(hid)[:, 0, bass.ds(f * T, T)], ft[:, :], ACT.Copy).then_inc(ff_act.sem, 1)
                t1 = t0 + 8 + 2 * FT
                with act.Fori(0, 4) as i:
                    for s in range(2):
                        residual(i * 2 + (n + 8 + s), t1 + i * 2 + s, i * 2 + s, s, gain1(i * 2 + s))
                norm(k + 1)

            tail_act(T_WO, 1, 8, 0, lambda m: col("n2", m), lambda m: par2[:, bass.ds(m + PAR2["n1"].start, 1)])
            def headnorm2(l, h, x):
                c = (l * HEADS2 + h) * 4 + x
                act.wait_ge(drained.sem, drained.at(l * T_LAYER + T_B2 + h * 6 + x))
                ac(sq[:, x % 2, :], raw2[:, x, :], ACT.Square).then_inc(h2_act.sem, 1)
                act.wait_ge(h2_pe.sem, h2_pe.at(c))
                ac(n_r0[:, :], psO[:, :], ACT.Abs_reciprocal_sqrt, bias=small[:, 60:61], scale=1.0 / QK2).then_inc(h2_act.sem, 1)
                act.wait_ge(h2_act.sem, h2_act.at(c, "root"))
                ac(n_r2[:, :], n_r0[:, :], ACT.Square, scale=QK2 ** -0.5).then_inc(h2_act.sem, 1)
                act.wait_ge(h2_dve.sem, h2_dve.at(c, "rot"))
                ac(qk2[:, x, 0], h_t[:, :], ACT.Copy).then_inc(h2_act.sem, 1)

            def values2(n, x):
                act.wait_ge(v2_pe.sem, v2_pe.at(n * 2 + x))
                ac(vtok2[:, 0, :, x * P:(x + 1) * P], psT[:, x, :].rearrange("p (k d) -> p k d", d=P), ACT.Copy).then_inc(v2_act.sem, 1)

            def attention2(n):
                def step(i):
                    i.then_inc(a2_act.sem, 1)

                for c in range(2):
                    o = 32 * c
                    act.wait_ge(a2_dve.sem, a2_dve.at(n, f"max{c}"))
                    for qt in range(TT):
                        pq = Pm2[:, c, P_AT[qt]:P_AT[qt] + P * (qt + 1)]
                        step(ac(pq, pq, ACT.Exp, bias=st2[:, o + 4 + qt:o + 5 + qt], scale=QK2 ** -0.5,
                                accum_out=st2[:, o + 8 + qt:o + 9 + qt]))
                act.wait_ge(a2_pe.sem, a2_pe.at(n, "t"))
                step(ac(PT2[:, 0, :], psT[:, :, :].rearrange("p b t -> p (b t)")[:, 0:1280], ACT.Copy))
                for d in range(2):
                    act.wait_ge(a2_dve.sem, a2_dve.at(n, f"copy{d}"))
                    step(ac(sq[:, d, :], os2[:, d, :], ACT.Square))
                act.wait_ge(a2_pe.sem, a2_pe.at(n, "sums"))
                step(ac(n_r0[:, :], psO[:, :], ACT.Abs_reciprocal_sqrt, bias=small[:, 60:61], scale=1.0 / V2))
                act.wait_ge(a2_act.sem, a2_act.at(n, "root"))
                step(ac(n_r2[:, :], n_r0[:, :], ACT.Square, scale=V2 ** -0.5))

            with act.Fori(0, LAYERS) as l:
                t0 = l * T_LAYER + T_B2
                act.wait_ge(ly_pe.sem, ly_pe.at(l))
                ac(small[:, 34:36], psO[:, 0:2], ACT.Exp).then_inc(ly_act.sem, 1)
                with act.Fori(0, HEADS2) as h:
                    n = l * HEADS2 + h
                    for x in range(6):
                        if x < 4:
                            headnorm2(l, h, x)
                        else:
                            values2(n, x - 4)
                    attention2(n)
                for m in range(KT):
                    act.wait_ge(up_dve.sem, up_dve.at(l, f"mean{m}"))
                    ac(mix2[:, 0, m], pr[:, :], ACT.Copy).then_inc(up_act.sem, 1)
                with act.Fori(0, KT) as m:
                    n = l * KT + m
                    for s in range(2):
                        act.wait_ge(drained.sem, drained.at(t0 + U_GAB + m * 2 + s))
                        ac(mg2[:, s, :], mg2[:, s, :], ACT.Sigmoid).then_inc(m2_act.sem, 1)
                    act.wait_ge(m2_dve.sem, m2_dve.at(n, "sum"))
                    ac(flat(mix2)[:, 0, bass.ds(m * T, T)], mt2[:, :], ACT.Copy).then_inc(m2_act.sem, 1)
                tail_act(t0 + U_WO, l * 2 + 3, l * 16 + 24, l * FT + FT, lambda m: lay[:, bass.ds(m + PAR2["n2"].start, 1)],
                         lambda m: lay[:, bass.ds(m + PAR2_N, 1)])

            for t in range(TT):
                act.wait_ge(ou_pe.sem, ou_pe.at(t))
                ac(yout[:, t, :], psT[:, 0:2, :].rearrange("p b d -> p (b d)"), ACT.Copy).then_inc(ou_act.sem, 1)
                act.wait_ge(ou_act.sem, ou_act.at(t))
                act.dma_start(out[0, t * P:(t + 1) * P, :], yout[:, t, :]).then_inc(stored, 16)
            act.wait_ge(stored, TT * 16)


def kernel(**inputs):
    import concourse.bacc as bacc
    from concourse.bass_utils import run_bass_kernel_spmd

    nc = bacc.Bacc("TRN2", target_bir_lowering=False, num_devices=1)
    arrays = {name: np.ascontiguousarray(value) for name, value in inputs.items()}
    arrays["const"] = constants()
    args = {name: nc.dram_tensor(f"in_{name}", x.shape, F32, kind="ExternalInput").ap() for name, x in arrays.items()}
    out = nc.dram_tensor("result", (1, T, D), F32, kind="ExternalOutput").ap()
    build(nc, args, out)
    ran = run_bass_kernel_spmd(nc, [{f"in_{name}": x for name, x in arrays.items()}], core_ids=[0])
    return ran.results[0]["result"]
```

```python
from contextlib import ExitStack

import numpy as np

import concourse.bass as bass
from concourse import mybir

F32 = mybir.dt.float32
F32R = mybir.dt.float32r
ALU = mybir.AluOpType
ACT = mybir.ActivationFunctionType
AX = mybir.AxisListType

P = 128
T = 512
TT = T // P
D = 1024
KT = D // P
EPS = 1e-6
HEADS, HD, GROUPS = 16, 64, 4
NBLK, STRIDE, BLOCK = 31, 16, 32
HID = 256
DFF = 2816
FT = DFF // P
HEADS2, QK2, V2 = 4, 128, 256
LAYERS = 2
POOL_W = (2, 4, 8, 16)
NEG = -1e32

RAW, SPLIT = 4, 2

C_KV, C_CMP, C_Q, C_LRU, C_MIX, C_WO, C_GU, C_DN, C_B2 = np.cumsum(
    [0, 12, 8, 8, 32, 16, 8, 44, 24]).tolist()
L_QKV, L_U, L_PW, L_GAB, L_WO, L_GU, L_DN, C_LAYER = np.cumsum(
    [0, 24, 8, 4, 16, 8, 44, 24]).tolist()
C_ALL = C_B2 + LAYERS * C_LAYER
T_IN, T_KV, T_CMP, T_Q, T_LRU, T_MIX, T_WO, T_GU, T_DN, T_B2 = np.cumsum(
    [0, 8, 12, 4, 8, 32, 16, 8, 44, 8]).tolist()
U_QKV, U_U, U_PW, U_GAB, U_WO, U_GU, U_DN, T_LAYER = np.cumsum(
    [0, 24, 8, 8, 16, 8, 44, 8]).tolist()

CONST = {}
_at = 0
for _name, _n in (("ident", P), ("ones", P), ("blk", P), ("dist", T), ("cdist", TT * 32),
                  ("cmask", TT * 32), ("slope", HEADS), ("edge", 32), ("lam", 4),
                  ("cos", T), ("sin", T), ("chunk", T)):
    CONST[_name] = slice(_at, _at + _n)
    _at += _n
CONST_N = _at
CONST_2 = CONST["cos"].start
CON2 = {n: slice(x.start - CONST_2, x.stop - CONST_2) for n, x in CONST.items() if x.start >= CONST_2}

PAR = {}
_at = 0
for _name, _n in (("n1", KT), ("n2", KT), ("cw", 4 * KT), ("cb", KT), ("ba", KT), ("bi", KT),
                  ("lam", KT), ("b1k", 2), ("b1v", 2), ("qg", 1), ("kg", 3), ("b2k", 1),
                  ("posk", 16), ("posv", 16)):
    PAR[_name] = slice(_at, _at + _n)
    _at += _n
PAR_N = _at
PAR2 = {}
_at = 0
for _name, _n in (("n1", KT), ("n2", KT), ("ps", KT), ("qg", 1), ("kg", 1), ("lam", 4),
                  ("sub", 2)):
    PAR2[_name] = slice(_at, _at + _n)
    _at += _n
PAR2_N = _at


def constants():
    c = np.zeros((P, CONST_N), np.float32)
    p = np.arange(P)[:, None]
    c[:, CONST["ident"]] = np.eye(P)
    c[:, CONST["ones"]] = 1.0
    c[:, CONST["blk"]] = (p // HD == np.arange(P)[None] // HD)
    rel = np.arange(T)[None] - (T - P) - p
    c[:, CONST["dist"]] = np.where(rel <= 0, rel, NEG)
    t = np.arange(TT)[None, :, None] * P + p[:, :, None]
    n = np.arange(32)[None, None, :]
    d = t - (n * STRIDE + BLOCK - 1)
    ok = (d >= 0) & (n < NBLK)
    c[:, CONST["cdist"]] = np.where(ok, -d, NEG).reshape(P, -1)
    c[:, CONST["cmask"]] = ok.reshape(P, -1)
    slope = np.power(2.0, -8.0 * np.arange(1, HEADS + 1) / HEADS).astype(np.float32)
    c[:, CONST["slope"]] = slope * np.float32(HD ** 0.5)
    rot = 32
    inv = np.float32(500000.0) ** (-np.arange(0, rot, 2, dtype=np.float32) / np.float32(rot))
    ang = np.arange(T, dtype=np.float32)[None] * inv[:, None]
    c[0:rot, CONST["cos"]] = np.concatenate([np.cos(ang)] * 2)
    c[0:rot, CONST["sin"]] = np.concatenate([-np.sin(ang), np.sin(ang)])
    c[:, CONST["chunk"]] = np.where(p // 64 >= (np.arange(T)[None] - (T - P)) // 64, 0.0, -3e38)
    at = CONST["edge"].start
    for w in POOL_W:
        c[:, at:at + w] = np.float32(w) / np.arange(1, w + 1, dtype=np.float32)
        at += w
    for l in range(LAYERS):
        li = 0.8 - 0.6 * np.exp(-0.3 * l)
        c[:, CONST["lam"].start + 2 * l] = li
        c[:, CONST["lam"].start + 2 * l + 1] = -0.5 * (1.0 - li)
    return c


class Steps:

    def __init__(self, sem, names):
        self.sem, self.names = sem, {x: i for i, x in enumerate(names)}

    def at(self, n, name=None):
        return n * len(self.names) + (len(self.names) if name is None else self.names[name] + 1)


P_AT = (0, 128, 384, 768)
PT_AT = (0, 512, 1024, 896)
A2_PE = [f"s{c}_{x}" for c in range(2) for x in range(4)] + ["t", "v", "sums"]
A2_DVE = ([f"max0_{x}" for x in range(4)] + ["max0"] + [f"max1_{x}" for x in range(4)] + ["max1", "rec", "neg"]
          + [f"scale{q}" for q in range(4)] + [f"a{q}" for q in range(4)] + ["lo", "copy0", "copy1", "newton", "scale",
                                                                            "out0", "out1"])
A2_ACT = [f"exp{c}_{q}" for c in range(2) for q in range(4)] + ["hi", "square0", "square1", "log", "root", "root2"]


def pool_steps():
    return [x for m in range(KT) for x in [f"y{m}_{k}" for k in range(m // 2 + 1)]
            + [f"edge{m}", f"mean{m}", f"lo{m}"]]


P_DMAS = 37
G_DMAS = 6


def build(nc, a, out):
    with ExitStack() as ctx:
        top = [-(-nc.sbuf_base // 32) * 32]
        names = [0]

        def place(shape, dt, offset):
            names[0] += 1
            return nc.alloc_sbuf_tensor_at(f"b{names[0]}", [P] + list(shape), dt, offset=offset)

        def keep(*shape, dt=F32):
            t = place(shape, dt, top[0])
            top[0] += -(-int(np.prod(shape)) * 4 // 32) * 32
            return t

        def sem(name):
            return ctx.enter_context(nc.semaphore(name))

        def steps(name, each):
            return Steps(sem(name), each)

        xT = keep(KT, T)
        wraw = keep(RAW, KT * P)
        wsp = keep(SPLIT, 2, KT, P, dt=F32R)
        xg = keep(2, KT, T, dt=F32R)
        con = keep(CONST_2)
        par = keep(PAR_N)
        par2 = keep((LAYERS + 1) * PAR2_N)
        lay = keep(PAR2_N + KT)
        c_rs = keep(T)
        acc_at = top[0]
        acc = keep(T)
        sq = keep(2, T)
        n_r0 = keep(T)
        n_r2 = keep(T)
        n_b = keep(T)
        small = keep(64)

        base = top[0]
        limit = nc.sbuf_usable_end

        class Plan:
            def __init__(self, at=0):
                self.at = at

            def __call__(self, *shape, dt=F32):
                t = place(shape, dt, base + self.at)
                self.at += -(-int(np.prod(shape)) * 4 // 32) * 32
                assert base + self.at <= limit, (base + self.at - limit)
                return t

        pl = Plan()
        attnT = pl(2, KT, T, dt=F32R)
        after_attn = pl.at
        kn = pl(2, 2, 2, T, dt=F32R)
        vtok = pl(2, 2, TT, GROUPS * HD, dt=F32R)
        kc = pl(2, P, dt=F32R)
        vc = pl(2, 2, P, dt=F32R)
        gates = pl(TT, 3 * HEADS)
        before_pair = pl.at
        qraw = pl(T)
        qz = pl(2, 2, T, dt=F32R)
        h_sq, h_t = sq[:, 0, :], sq[:, 1, :]
        bias = pl(2, T)
        cbias = pl(2, TT * 32)
        Pm = pl(2, 1280)
        Pc = pl(TT, 2, 32)
        PT = pl(2, 1280, dt=F32R)
        st = pl(64)
        cst = pl(64)
        PTc = [place([T], F32R, acc_at), pl(T, dt=F32R)]
        pl = Plan()
        kvraw = pl(12, T)
        gwraw = pl(KT, 48)
        gw = pl(2, KT, 48, dt=F32R)
        w2raw = pl(2, 2, P)
        hidc = pl(2, P)
        kcraw = pl(P)
        assert pl.at <= after_attn
        pl = Plan(before_pair)
        E = pl(2, 2, 5, 264, dt=F32R)
        Et = pl(2, T, dt=F32R)
        w2 = pl(2, 2, 2, P, dt=F32R)
        gsc = sq[:, 1, :]
        hidr = pl(2, 2, 2, P, dt=F32R)
        bcol = pl(8)
        vcraw = pl(GROUPS, HD)
        vcraw2 = pl(GROUPS, HD)
        b2v = pl(HD)
        pl = Plan()
        xin = pl(TT, D)
        prow = pl(P)
        prow2 = pl(P)
        pl = Plan(after_attn)
        lruT = pl(2, KT, T, dt=F32R)
        lruw = pl(2, KT, HD)
        bd = pl(2, 2, P, dt=F32R)
        lx = pl(T + 3)
        xc = pl(T)
        xcr = pl(2, T, dt=F32R)
        gl = pl(T)
        lt = [pl(T) for _ in range(5)]
        mg = sq[:, 0, :]
        mixT = pl(KT, T)
        con2 = place([CONST_N - CONST_2], F32, (limit - (CONST_N - CONST_2) * 4) // 32 * 32)
        pl = Plan()
        aT2 = pl(KT, T)
        after_a2 = pl.at
        Pm2 = pl(2, 1280)
        PT2 = pl(2, 1280, dt=F32R)
        os2 = pl(2, T)
        st2 = pl(64)
        vtok2 = pl(2, TT, V2, dt=F32R)
        before_qk2 = pl.at
        qk2 = pl(4, 2, T, dt=F32R)
        raw2 = pl(6, T)
        rot = pl(T)
        norm2 = pl(T)
        pl = Plan(before_qk2)
        mix2 = pl(2, KT, T, dt=F32R)
        ur = pl(2, T + 16)
        ya, yb = pl(T + 16), pl(T + 16)
        pr = pl(T)
        mg2 = pl(2, T)
        mt2 = pl(T)
        pl = Plan(after_a2)
        poolT = pl(KT, T)
        pl = Plan()
        yout = pl(TT, D)
        pl = Plan()
        hid = pl(2, FT, T, dt=F32R)
        fg = pl(2, T)
        fu = pl(T)
        ft = pl(T)

        def pb(name, *shape):
            return ctx.enter_context(nc.psum_tensor(name, [P] + list(shape), F32))

        psA = pb("psA", 2, T)
        psS = pb("psS", 2, T)
        psT = pb("psT", 3, T)
        psO = pb("psO", T)

        ident, ones, blk = con[:, CONST["ident"]], con[:, CONST["ones"]], con[:, CONST["blk"]]

        wload = [sem(f"weights_loaded{s}") for s in range(RAW)]
        wsplit = steps("weights_split", ["hi", "lo"])
        used = steps("chunk_used", ["all"])
        drained = steps("tile_drained", ["all"])
        x_in = sem("x_loaded")
        c_in = sem("constants_loaded")
        c2_in = sem("constants2_loaded")
        p_in = sem("parameters_loaded")
        g_in = sem("small_weights_loaded")
        lw_in = sem("lru_weights_loaded")
        su_pe = steps("setup_transposed", ["one"])
        su_dve = steps("setup_vector", ["one"])
        res_act = steps("residual_scalar", ["hi", "square"])
        res_dve = steps("residual_vector", ["lo", "sum"])
        nm_pe = steps("norm_sums", ["sum"])
        nm_act = steps("norm_scalar", ["log", "root", "root2"])
        nm_dve = steps("norm_vector", ["newton", "scale", "zero"])
        hn_act = steps("headnorm_scalar", ["square", "log", "root", "root2", "hi"])
        hn_pe = steps("headnorm_sums", ["sum"])
        hn_dve = steps("headnorm_vector", ["newton", "scale", "apply", "lo"])
        cg_dve = steps("small_split_vector", ["gw_hi", "gw_lo", "w2_hi", "w2_lo", "gates"])
        cg_pe = steps("gate_products", ["gates", "transposed"])
        cg_act = steps("gate_sigmoid", ["all"])
        e_dve0 = steps("blocks_zeroed", ["zero", "hi_k", "lo_k", "hi_v", "lo_v"])
        e_act = steps("blocks_scalar", ["hi", "even", "odd"])
        e_dve = steps("blocks_vector", ["lo", "even", "odd"])
        ch_dve = steps("hidden_bias", ["bias"])
        ch_act = steps("hidden_scalar", ["gelu", "hi"])
        vt_pe = steps("values_transposed", ["all"])
        vt_act = steps("values_hi", ["all"])
        vt_dve = steps("values_lo", ["all"])
        kv_pe = steps("compressed_kv", ["all"])
        kv_dve = steps("compressed_vector", ["k", "v", "v_hi0", "v_hi1", "v_lo0", "v_moved", "v_lo1"])
        pad_dve = steps("padding_zeroed", ["vc", "qz0", "ptc0", "qz1", "ptc1"])
        qs_act = steps("query_squares", ["square"])
        qr_act = steps("query_roots", ["log", "root", "root2"])
        qi_act = steps("query_hi", ["head0", "head1"])
        q_pe = steps("query_sums", ["sum"])
        q_dve = steps("query_vector", ["newton", "scale", "apply", "lo0", "lo1"])
        b_dve = steps("biases", ["head0", "head1", "compressed0", "compressed1"])
        us_pe = steps("unit_scores", ["s0", "s1", "s2", "s3"])
        um_dve = steps("unit_maxima", ["max0", "max1", "max2", "max3", "neg"])
        ue_act = steps("unit_exps", ["e0", "e1", "e2", "e3"])
        ug_dve = steps("unit_gates", ["rec", "gate"])
        up_dve1 = steps("unit_probabilities", ["k0", "k1", "k2", "k3"])
        ut_pe = steps("unit_transposed", ["all"])
        uh_act = steps("unit_hi", ["all"])
        ul_dve = steps("unit_lo", ["all"])
        uv_pe = steps("unit_values", ["all"])
        cs_pe = steps("compressed_scores", ["all"])
        cm_dve = steps("compressed_maxima", ["add", "max", "sub"])
        ce_act = steps("compressed_exps", ["exp"])
        cp_dve = steps("compressed_probabilities", ["mask", "sum", "guard", "rec", "gate", "scale"])
        ct_pe = steps("compressed_transposed", ["all"])
        ch_act2 = steps("compressed_hi", ["all"])
        cl_dve = steps("compressed_lo", ["all"])
        cv_pe = steps("head_output", ["all"])
        oh_act = steps("head_output_hi", ["all"])
        ol_dve = steps("head_output_lo", ["all"])
        sp_dve = steps("softplus_vector", ["abs"])
        sp_act = steps("softplus_scalar", ["exp"])
        eps_in = steps("epsilon_set", ["all"])
        lw_dve = steps("lru_zeroed", ["diagonal", "pad"])
        lr_pe = steps("lru_products", ["a", "i"])
        lr_dve = steps("lru_vector", ["tap0", "tap1", "tap2", "tap3", "lo", "w0", "w1", "one", "rec", "ratio",
                                      "ix", "b", "scan", "out", "out_lo"])
        lr_act = steps("lru_scalar", ["hi", "w0", "w1", "gelu", "gate", "r", "i", "tanh", "a", "root", "out_hi"])
        mx_act = steps("mix_scalar", ["gate", "hi"])
        mx_dve = steps("mix_vector", ["sum", "lo"])
        ff_act = steps("ffn_scalar", ["silu", "hi"])
        ff_dve = steps("ffn_vector", ["product", "lo"])
        ly_dve = steps("layer_vector", ["copy", "gains", "sub", "products", "diff", "lambda"])
        ly_pe = steps("layer_sums", ["sum"])
        ly_act = steps("layer_scalar", ["exp"])
        h2_act = steps("headnorm2_squares", ["square"])
        h2_root = steps("headnorm2_roots", ["log", "root", "root2"])
        h2_hi = steps("headnorm2_hi", ["hi"])
        h2_pe = steps("headnorm2_sums", ["sum"])
        h2_dve = steps("headnorm2_vector", ["newton", "scale", "apply", "swap", "sin", "cos", "rot", "lo"])
        v2_raw = steps("values2_drained", ["all"])
        v2_pe = steps("values2_transposed", ["all"])
        v2_act = steps("values2_hi", ["all"])
        v2_dve = steps("values2_lo", ["all"])
        a2_pe = steps("attention2_products", A2_PE)
        a2_dve = steps("attention2_vector", A2_DVE)
        a2_act = steps("attention2_scalar", A2_ACT)
        up_dve = steps("pool_vector", ["pad0", "pad1"] + pool_steps())
        up_act = steps("pool_hi", ["hi"])
        m2_act = steps("mix2_scalar", ["ga", "gb", "hi"])
        m2_dve = steps("mix2_vector", ["pool", "attn", "sum", "lo"])
        ou_pe = steps("output_transposed", ["all"])
        ou_act = steps("output_copied", ["all"])
        stored = sem("stored")

        def hi_f(x):
            return x.bitcast(F32)

        settles = sem("waits_settled")

        def settled(engine):
            engine.sem_inc(settles, 1)

        block = ctx.enter_context(nc.Block())

        def col_tile(w, kts, m):
            v = w.rearrange("(k p) n -> p k n", p=P)
            h = kts // 2
            return [(0, h, v[:, 0:h, bass.ds(m, P)]), (h, kts, v[:, h:kts, bass.ds(m, P)])]

        w_in, w_in2 = a["w_in"][0], a["w_in_2"]

        def tail(stage, c0, wo, gate, up, down):
            stage(c0, 8, lambda i, s: wo(i * 4 * P + s * P))
            stage(c0 + 8, 2 * FT, lambda i, s: (up if s % 2 else gate)(i * 2 * P + (s // 2) * P))
            stage(c0 + 8 + 2 * FT, 24, lambda i, s: down(s % 3 * KT, i * 4 * P + (s // 3) * P), per=12)

        @block.sync
        def _(sp):
            def load(c, s, parts, dst=None, settle=False):
                if not isinstance(c, int) or c >= RAW:
                    sp.wait_ge(wsplit.sem, wsplit.at(c - RAW))
                    if settle:
                        settled(sp)
                slot = wraw[:, s, :].rearrange("p (k n) -> p k n", n=P)
                for lo, hi, src in parts:
                    sp.dma_start(slot[:, lo:hi, :] if dst is None else dst(slot, lo), src).then_inc(wload[s], 16)

            def stage(c0, n, parts, per=RAW, dst=None):
                with sp.Fori(0, n // per) as i:
                    for s in range(per):
                        load(c0 + i * per + s, s % RAW, parts(i, s), dst)

            sp.dma_start(xin[:, :, :], a["x"][0].rearrange("(t p) d -> p t d", p=P)).then_inc(x_in, 16)
            wc = w_in.rearrange("(k p) n -> p k n", p=P)

            def halves(col, apart):
                return [(b, 0, wc[:, :, bass.ds(col + b * apart, HD)]) for b in range(2)]

            def to_half(slot, b):
                return slot[:, :, b * HD:(b + 1) * HD]

            for s in range(RAW):
                load(s, s, halves(D + s // 2 * GROUPS * HD + s % 2 * HD, 2 * HD), to_half)
            stage(C_KV + 4, 8, lambda i, s: halves(i * (2 * GROUPS * HD) + D + (2 + s // 2) * GROUPS * HD + s % 2 * HD, 2 * HD),
                  dst=to_half)
            for kv, name in enumerate(("cmp_w1_k", "cmp_w1_v")):
                w1 = a[name][0].rearrange("l d f -> (l d) f")
                for s in range(4):
                    half = w1[(s % 2) * D:(s % 2 + 1) * D, :]
                    load(C_CMP + 4 * kv + s, s, col_tile(half, KT, (s // 2) * P))
            stage(C_Q, 8, lambda i, s: halves(i * (4 * HD) + s * HD, D // 2), dst=to_half)
            o3 = 2608
            woa = a["w_o_attn"][0].rearrange("(b k d) n -> b d k n", b=2, d=HD)
            o5 = o3 + 2 * D
            with sp.Fori(0, KT) as i:
                for s in range(3):
                    load(C_LRU + i * 4 + s, s, col_tile(w_in, KT, i * P + o3 + s * D))
                load(C_LRU + i * 4 + 3, 3, [(b, 0, woa[b, :, :, bass.ds(i * P, P)]) for b in range(2)],
                     lambda slot, b: slot[b * HD:(b + 1) * HD, :, :], settle=True)
            with sp.Fori(0, KT // 2) as i:
                for s in range(4):
                    m = i * 2 * P + (s // 2) * P
                    load(C_MIX + i * 4 + s, s, col_tile(a["w_o_lru"][0], KT, m) if s % 2 else col_tile(w_in, KT, m + (o5 + D)), settle=s == 1)

            def down(r, m):
                k = min(KT, FT - r)
                return col_tile(a["w_down"][0][r * P:(r + k) * P, :], k, m)

            tail(stage, C_WO, lambda m: col_tile(a["w_out"][0], KT, m), lambda m: col_tile(a["w_gate"][0], KT, m),
                 lambda m: col_tile(a["w_up"][0], KT, m), down)

            def stacked(name):
                return a[name].rearrange("l (k p) n -> p (l k) n", p=P)

            wi2, wo2, wf2, wd2 = (stacked(x) for x in ("w_in_2", "w_out_2", "w_ffn_in_2", "w_ffn_out_2"))
            pw2 = a["pool_w_2"].rearrange("l g (k p) (m n) -> p (l g k) m n", p=P, n=P)
            with sp.Fori(0, LAYERS) as l:
                def col2(w, col, k0=0, kts=KT, each=KT):
                    h = kts // 2
                    return [(b, e, w[:, bass.ds(l * each + (k0 + b), e - b), bass.ds(col, P)]) for b, e in ((0, h), (h, kts))]

                c0 = l * C_LAYER + C_B2
                with sp.Fori(0, 2) as i:
                    for s in range(12):
                        x = s % 6
                        load(c0 + i * 12 + s, s % RAW,
                             col2(wi2, i * (2 * V2) + (D * (1 + x // 2) + s // 6 * V2 + x % 2 * P)))
                stage(c0 + L_U, 8, lambda i, s: col2(wi2, i * 4 * P + s * P))
                for g in range(4):
                    load(c0 + (L_PW + g), g, [(2 * k, 2 * k + 2, pw2[:, bass.ds(l * 8 + (g * 2 + k), 1), :, :].squeeze(1)) for k in range(2)], settle=True)
                stage(c0 + L_GAB, 16, lambda i, s: col2(wi2, i * 2 * P + (D * (4 + s % 2) + s // 2 * P)))
                tail(stage, c0 + L_WO, lambda m: col2(wo2, m), lambda m: col2(wf2, m), lambda m: col2(wf2, m + DFF),
                     lambda r, m: col2(wd2, m, r, min(KT, FT - r), FT))

        @block.gpsimd
        def _(pool):
            def split(c, rnd, s):
                pool.wait_ge(wload[s], rnd * 32 + 32)
                if not isinstance(c, int) or c >= SPLIT:
                    pool.wait_ge(used.sem, used.at(c - SPLIT))
                if not isinstance(c, int):
                    settled(pool)
                w = wsp[:, s % SPLIT].rearrange("p h k n -> p h (k n)")
                nc.gpsimd.tensor_tensor(w[:, 0], wraw[:, s], ones[:, 0:1].broadcast_to([P, KT * P]), ALU.mult).then_inc(wsplit.sem, 1)
                pool.wait_ge(wsplit.sem, wsplit.at(c, "hi"))
                nc.gpsimd.tensor_tensor(w[:, 1], wraw[:, s], hi_f(w[:, 0]), ALU.subtract).then_inc(wsplit.sem, 1)

            pool.wait_ge(c_in, 16)
            for s in range(RAW):
                split(s, 0, s)
            with pool.Fori(1, C_ALL // RAW) as i:
                for s in range(RAW):
                    split(i * RAW + s, i, s)

        def tail_pe(pe, chunk, free, proj, norm, c0, t0, src, k, n, ff):
            with pe.Fori(0, 4) as i:
                for s in range(2):
                    proj(c0 + i * 2 + s, t0 + i * 2 + s, s, lambda h, kt: src[:, h, kt, :])
            norm(k, n + 7)
            with pe.Fori(0, FT) as i:
                for s in range(2):
                    proj(c0 + 8 + i * 2 + s, t0 + 8 + i * 2 + s, s)
            pe.wait_ge(ff_dve.sem, ff_dve.at(ff + FT - 1))
            settled(pe)
            c1, t1 = c0 + 8 + 2 * FT, t0 + 8 + 2 * FT
            with pe.Fori(0, 4) as i:
                for m in range(2):
                    free(t1 + i * 2 + m)
                    for q in range(3):
                        s = 3 * m + q
                        chunk(c1 + i * 6 + s, s, psA[:, m, :], lambda h, kt: hid[:, h, q * KT + kt, :],
                              min(KT, FT - q * KT), q == 0, q == 2)
            norm(k + 1, n + 15)

        def attention_pe(pe, chunk, free, three):
            mm = nc.tensor.matmul

            def query(n, kts):
                if kts[0] == 0:
                    free(T_Q + n)
                    if n:
                        pe.wait_ge(q_dve.sem, q_dve.at(n - 1, "newton"))
                    pe.wait_ge(wsplit.sem, wsplit.at(C_Q + n))
                for kt in kts:
                    i = three(psA[:, n % 2, :], lambda h: wsp[:, n % 2, h, kt, :], lambda h: xg[:, h, kt, :], kt == 0, kt == KT - 1, True)
                if kts[-1] == KT - 1:
                    i.then_inc(used.sem, 1)

            def query_sums(n):
                pe.wait_ge(qs_act.sem, qs_act.at(n))
                mm(psA[:, (n + 1) % 2, :], blk, h_sq[:, :], start=True, stop=True).then_inc(q_pe.sem, 1)

            def scores(U, xs):
                n, hd, br = U // 4, U % 4 // 2, U % 2
                if U % 4 == 0 and 0 in xs:
                    pe.wait_ge(q_dve.sem, q_dve.at(n))
                for x in xs:
                    qt = TT - 1 - x
                    if x >= 2:
                        pe.wait_ge(um_dve.sem, um_dve.at(U, f"max{x - 2}"))
                    elif U % 4 == 2 or U == 1:
                        pe.wait_ge(cm_dve.sem, cm_dve.at(n, "add")) if U > 1 else pe.wait_ge(um_dve.sem, um_dve.at(0, f"max{x + 2}"))
                    elif U:
                        pe.wait_ge(um_dve.sem, um_dve.at(U - 1, f"max{x + 2}"))
                    w = P * (qt + 1)
                    three(psS[:, x % 2, 0:w], lambda h: qz[:, hd, h, qt * P:(qt + 1) * P],
                          lambda h: kn[:, br, n // 4, h, 0:w], True, True).then_inc(us_pe.sem, 1)

            def transposes(U):
                if U:
                    pe.wait_ge(ul_dve.sem, ul_dve.at(U - 1))
                for qt in range(TT):
                    pe.wait_ge(up_dve1.sem, up_dve1.at(U, f"k{qt}"))
                    for kt in range(qt + 1):
                        to = PT_AT[kt] + (qt - kt) * P
                        i = nc.tensor.transpose(psT[:, to // T, to % T:to % T + P],
                                                Pm[:, U % 2, P_AT[qt] + kt * P:P_AT[qt] + (kt + 1) * P], ident)
                i.then_inc(ut_pe.sem, 1)

            def values(U):
                n, hd, br = U // 4, U % 4 // 2, U % 2
                if br == 0 and U:
                    pe.wait_ge(ol_dve.sem, ol_dve.at(U // 2 - 1))
                pe.wait_ge(ul_dve.sem, ul_dve.at(U))
                for kt in range(TT):
                    w = T - kt * P
                    i = three(psO[:, kt * P:T], lambda h: vtok[:, br, h, kt, n // 4 * P:(n // 4 + 1) * P],
                              lambda h: PT[:, h, PT_AT[kt]:PT_AT[kt] + w], br == 0 and kt == 0, False, True)
                i.then_inc(uv_pe.sem, 1)

            def c_scores(n):
                for hd in range(2):
                    pe.wait_ge(um_dve.sem, um_dve.at(4 * n + 1, f"max{hd + 2}"))
                    for qt in range(TT):
                        i = three(psS[:, hd, qt * 32:qt * 32 + 32], lambda h: qz[:, hd, h, qt * P:(qt + 1) * P],
                                  lambda h: kc[:, h, 32 * (2 * (n // 4) + hd):32 * (2 * (n // 4) + hd) + 32], True, True)
                i.then_inc(cs_pe.sem, 1)

            def c_transposes(n):
                pe.wait_ge(cp_dve.sem, cp_dve.at(n))
                if n < 7:
                    pe.wait_ge(q_dve.sem, q_dve.at(n + 1, "newton"))
                for qt in range(TT):
                    i = nc.tensor.transpose(psA[0:HD, n % 2, qt * P:(qt + 1) * P],
                                            Pc[:, qt, :, :].rearrange("p h n -> p (h n)"), ident)
                i.then_inc(ct_pe.sem, 1)

            def c_values(n, hd):
                pe.wait_ge(cl_dve.sem, cl_dve.at(n))
                three(psO[:, :], lambda h: vc[:, h, n // 4, :], lambda h: PTc[h][:, :], False, True, True).then_inc(cv_pe.sem, 1)

            x4 = range(4)
            query(0, range(KT))
            query_sums(0)
            query(1, range(KT))
            scores(0, x4)
            scores(1, x4)
            c_scores(0)
            for n in range(8):
                U, last = 4 * n, n == 7
                transposes(U)
                scores(U + 2, x4)
                if not last:
                    query_sums(n + 1)
                values(U)
                transposes(U + 1)
                scores(U + 3, x4)
                c_transposes(n)
                values(U + 1)
                c_values(n, 0)
                transposes(U + 2)
                if not last:
                    scores(U + 4, x4)
                if n < 6:
                    query(n + 2, range(4))
                values(U + 2)
                transposes(U + 3)
                if not last:
                    scores(U + 5, x4)
                if n < 6:
                    query(n + 2, range(4, KT))
                values(U + 3)
                c_values(n, 1)
                if not last:
                    c_scores(n + 1)

        @block.tensor
        def _(pe):
            mm = nc.tensor.matmul

            def chunk(c, s, dst, rhs, kts=KT, first=True, last=True):
                pe.wait_ge(wsplit.sem, wsplit.at(c))
                w = wsp[:, s % SPLIT]
                for kt in range(kts):
                    for n, (wh, xh) in enumerate(((0, 0), (0, 1), (1, 0))):
                        i = mm(dst, w[:, wh, kt, :], rhs(xh, kt), start=first and kt == 0 and n == 0,
                               stop=last and kt == kts - 1 and n == 2)
                i.then_inc(used.sem, 1)

            def free(t):
                pe.wait_ge(drained.sem, drained.at(t - 2))

            def rhs_x(h, kt):
                return xg[:, h, kt, :]

            def proj(c, t, s, rhs=rhs_x):
                free(t)
                chunk(c, s, psA[:, s % 2, :], rhs)

            def three(dst, lh, rh, start=False, stop=False, skip=False):
                for n, (x, y) in enumerate(((0, 0), (0, 1), (1, 0))):
                    i = mm(dst, lh(x), rh(y), start=start and n == 0, stop=stop and n == 2, skip_group_check=skip)
                return i

            def norm(k, n):
                pe.wait_ge(res_dve.sem, res_dve.at(n))
                mm(psO[:, :], ones, acc[:, :], start=True, stop=True).then_inc(nm_pe.sem, 1)

            def headnorm(n, sums, w=T):
                pe.wait_ge(hn_act.sem, hn_act.at(n, "square"))
                mm(psO[:, 0:w], sums, h_sq[:, 0:w], start=True, stop=True).then_inc(hn_pe.sem, 1)

            def headnorm2(n, x, after=True):
                if x and after:
                    pe.wait_ge(h2_dve.sem, h2_dve.at(n * 4 + (x - 1), "newton"))
                pe.wait_ge(h2_act.sem, h2_act.at(n * 4 + x, "square"))
                mm(psO[:, :], ones, sq[:, x % 2, :], start=True, stop=True).then_inc(h2_pe.sem, 1)

            def values2(n, x):
                pe.wait_ge(v2_raw.sem, v2_raw.at(n * 2 + x))
                for t in range(TT):
                    i = nc.tensor.transpose(psT[:, x, t * P:(t + 1) * P], raw2[:, 4 + x, t * P:(t + 1) * P], ident)
                i.then_inc(v2_pe.sem, 1)

            def scores2(n):
                pe.wait_ge(h2_dve.sem, h2_dve.at(n * 4 + 3))
                for c in range(2):
                    for x, qt in enumerate((3, 2, 1, 0)):
                        if c or x >= 2:
                            pe.wait_ge(a2_dve.sem, a2_dve.at(n, f"max{c}_{x - 2}" if x >= 2 else f"max0_{x + 2}"))
                        three(psS[:, x % 2, 0:P * (qt + 1)], lambda h: qk2[:, c, h, qt * P:(qt + 1) * P],
                              lambda h: qk2[:, 2 + c, h, 0:P * (qt + 1)], True, True).then_inc(a2_pe.sem, 1)

            def transposes2(n):
                pe.wait_ge(v2_dve.sem, v2_dve.at(n * 2 + 1))
                for qt in range(TT):
                    pe.wait_ge(a2_dve.sem, a2_dve.at(n, f"a{qt}"))
                    for kt in range(qt + 1):
                        to = PT_AT[kt] + (qt - kt) * P
                        i = nc.tensor.transpose(psT[:, to // T, to % T:to % T + P],
                                                Pm2[:, 0, P_AT[qt] + kt * P:P_AT[qt] + (kt + 1) * P], ident)
                i.then_inc(a2_pe.sem, 1)

            def products2(n):
                pe.wait_ge(a2_dve.sem, a2_dve.at(n, "lo"))
                for d in range(2):
                    for kt in range(TT):
                        w = T - kt * P
                        i = three(psS[:, d, kt * P:T], lambda h: vtok2[:, h, kt, d * P:(d + 1) * P],
                                  lambda h: PT2[:, h, PT_AT[kt]:PT_AT[kt] + w], kt == 0, kt == TT - 1, True)
                i.then_inc(a2_pe.sem, 1)

            def sums2(n):
                pe.wait_ge(a2_act.sem, a2_act.at(n, "square1"))
                mm(psO[:, :], ones, Pm2[:, 1, 0:T], start=True, stop=False)
                mm(psO[:, :], ones, Pm2[:, 1, T:2 * T], start=False, stop=True).then_inc(a2_pe.sem, 1)

            pe.wait_ge(c_in, 16)
            pe.wait_ge(p_in, P_DMAS * 16)
            nc.tensor.transpose(psT[:, 0, 0:PAR_N], prow[0:PAR_N, :], con[0:PAR_N, 0:PAR_N]).then_inc(su_pe.sem, 1)
            nc.tensor.transpose(psT[:, 1, 0:2 * PAR2_N], prow2[0:2 * PAR2_N, :],
                                con[0:2 * PAR2_N, 0:2 * PAR2_N]).then_inc(su_pe.sem, 1)
            pe.wait_ge(x_in, 16)
            for f in range(KT):
                if f >= 2:
                    free(f)
                for t in range(TT):
                    i = nc.tensor.transpose(psA[:, f % 2, t * P:(t + 1) * P], xin[:, t, f * P:(f + 1) * P], ident)
                i.then_inc(su_pe.sem, 1)
            norm(0, 7)
            pe.wait_ge(res_dve.sem, res_dve.at(7))
            with pe.Fori(0, 3) as i:
                for s in range(4):
                    proj(C_KV + i * 4 + s, T_KV + i * 4 + s, s)
            pe.wait_ge(cg_dve.sem, cg_dve.at(0, "gw_lo"))
            for kt in range(KT):
                i = three(psS[0:48, 0, :], lambda h: gw[:, h, kt, :], lambda h: xg[:, h, kt, :], kt == 0, kt == KT - 1)
            i.then_inc(cg_pe.sem, 1)
            pe.wait_ge(cg_dve.sem, cg_dve.at(0, "gates"))
            for t in range(TT):
                i = nc.tensor.transpose(psS[:, 1, 48 * t:48 * t + 48], gsc[0:48, t * P:(t + 1) * P], con[0:48, 0:48])
            i.then_inc(cg_pe.sem, 1)
            pe.wait_ge(e_act.sem, e_act.at(3))
            pe.wait_ge(e_dve.sem, e_dve.at(3))
            for kv in range(2):
                for s in range(4):
                    m, half = s // 2, s % 2
                    if half == 0:
                        free(T_CMP + 2 * kv + m)
                    chunk(C_CMP + 4 * kv + s, s, psA[:, m, 0:160].rearrange("p (g n) -> p g n", n=32),
                          lambda h, kt: E[:, kv, h, :, half * KT + kt:half * KT + kt + 249:8],
                          first=half == 0, last=half == 1)
            for n in range(4):
                if n:
                    pe.wait_ge(hn_dve.sem, hn_dve.at(n - 1, "newton"))
                else:
                    pe.wait_ge(nm_dve.sem, nm_dve.at(0, "newton"))
                headnorm(n, blk)
            for n in range(4):
                if n == 3:
                    pe.wait_ge(vt_dve.sem, vt_dve.at(0))
                src = kvraw[:, (6, 7, 10, 11)[n], :]
                for t in range(TT):
                    i = nc.tensor.transpose(psT[:, n % 3, t * P:(t + 1) * P], src[:, t * P:(t + 1) * P], ident)
                i.then_inc(vt_pe.sem, 1)
            pe.wait_ge(drained.sem, drained.at(T_CMP + 3))
            for kt in range(2):
                i = three(psS[:, 0, 0:P], lambda h: w2[:, 0, h, kt, :], lambda h: hidr[:, 0, h, kt, :], kt == 0, kt == 1)
            for g in range(GROUPS):
                for kt in range(2):
                    i = three(psS[0:32, 1, 256 + g * HD:256 + (g + 1) * HD],
                              lambda h: hidr[:, 1, h, kt, 32 * g:32 * g + 32],
                              lambda h: w2[:, 1, h, kt, 0:HD], kt == 0, kt == 1)
            i.then_inc(kv_pe.sem, 1)
            pe.wait_ge(hn_dve.sem, hn_dve.at(3, "newton"))
            headnorm(4, blk, P)
            attention_pe(pe, chunk, free, three)
            pe.wait_ge(lw_dve.sem, lw_dve.at(0))
            with pe.Fori(0, KT) as m:
                c, t = C_LRU + m * 4, T_LRU + m * 4
                for s in range(3):
                    proj(c + s, t + s, s)
                pe.wait_ge(lr_dve.sem, lr_dve.at(m, "w1"))
                for w in range(2):
                    three(psS[:, w, :], lambda h: bd[:, h, w, :], lambda h: xcr[:, h, :], True, True).then_inc(lr_pe.sem, 1)
                proj(c + 3, t + 3, 3, lambda h, kt: attnT[:, h, kt, :])
            with pe.Fori(0, KT // 2) as i:
                for s in range(4):
                    src = lruT if s % 2 else xg
                    if s == 1:
                        pe.wait_ge(lr_dve.sem, lr_dve.at(7))
                    proj(C_MIX + i * 4 + s, T_MIX + i * 4 + s, s, lambda h, kt: src[:, h, kt, :])
            pe.wait_ge(mx_dve.sem, mx_dve.at(7))
            tail_pe(pe, chunk, free, proj, norm, C_WO, T_WO, attnT, 1, 8, 0)

            with pe.Fori(0, LAYERS) as l:
                c0, t0 = l * C_LAYER + C_B2, l * T_LAYER + T_B2
                pe.wait_ge(ly_dve.sem, ly_dve.at(l, "products"))
                mm(psO[:, 0:2], ones, small[:, 32:34], start=True, stop=True).then_inc(ly_pe.sem, 1)
                pe.wait_ge(ly_dve.sem, ly_dve.at(l))
                settled(pe)
                n0 = l * HEADS2
                for x in range(6):
                    proj(c0 + x, t0 + x, x)
                    if 1 <= x <= 4:
                        headnorm2(n0, x - 1)
                values2(n0, 0)
                values2(n0, 1)
                with pe.Fori(0, HEADS2 - 1) as h:
                    n = l * HEADS2 + h
                    c, t = c0 + h * 6 + 6, t0 + h * 6 + 6
                    scores2(n)
                    proj(c, t, 0)
                    proj(c + 1, t + 1, 1)
                    headnorm2(n + 1, 0)
                    transposes2(n)
                    proj(c + 2, t + 2, 2)
                    headnorm2(n + 1, 1)
                    products2(n)
                    proj(c + 3, t + 3, 3)
                    headnorm2(n + 1, 2)
                    pe.wait_ge(h2_dve.sem, h2_dve.at(n * 4 + 6, "newton"))
                    sums2(n)
                    proj(c + 4, t + 4, 4)
                    pe.wait_ge(a2_dve.sem, a2_dve.at(n, "newton"))
                    headnorm2(n + 1, 3, False)
                    proj(c + 5, t + 5, 5)
                    values2(n + 1, 0)
                    values2(n + 1, 1)
                n, c, t = n0 + (HEADS2 - 1), c0 + L_U, t0 + U_U
                scores2(n)
                proj(c, t, 0)
                proj(c + 1, t + 1, 1)
                transposes2(n)
                proj(c + 2, t + 2, 2)
                products2(n)
                proj(c + 3, t + 3, 3)
                sums2(n)
                for m in range(4, KT):
                    proj(c + m, t + m, m)
                pe.wait_ge(up_dve.sem, up_dve.at(l))
                for g in range(4):
                    c, t = c0 + (L_PW + g), t0 + (U_PW + 2 * g)
                    pe.wait_ge(wsplit.sem, wsplit.at(c))
                    for m in range(2):
                        free(t + m)
                        for k in range(2):
                            i = three(psA[:, m, :], lambda x: wsp[:, g % SPLIT, x, 2 * k + m, :],
                                      lambda x: mix2[:, x, 2 * g + k, :], k == 0, k == 1)
                    i.then_inc(used.sem, 1)
                with pe.Fori(0, KT) as m:
                    for s in range(2):
                        proj(c0 + L_GAB + m * 2 + s, t0 + U_GAB + m * 2 + s, s)
                pe.wait_ge(m2_dve.sem, m2_dve.at(l * KT + 7))
                settled(pe)
                tail_pe(pe, chunk, free, proj, norm, c0 + L_WO, t0 + U_WO, mix2, l * 2 + 3, l * 16 + 24, l * FT + FT)
            for t in range(TT):
                if t:
                    pe.wait_ge(ou_act.sem, ou_act.at(t - 1))
                for f in range(KT):
                    i = nc.tensor.transpose(psT[:, f // 4, f % 4 * P:(f % 4 + 1) * P], xT[:, f, t * P:(t + 1) * P], ident)
                i.then_inc(ou_pe.sem, 1)

        @block.vector
        def _(dve):
            v = nc.vector
            count = [0]

            def link(i):
                i.then_inc(su_dve.sem, 1)
                count[0] += 1
                dve.wait_ge(su_dve.sem, count[0])

            def drain(c, t, s, dst):
                dve.wait_ge(used.sem, used.at(c))
                v.scalar_tensor_tensor(dst, psA[:, s % 2, :], -0.5, c_rs[:, :], ALU.mult, ALU.mult).then_inc(drained.sem, 1)

            def flat(b):
                return b[:, :, :, :].rearrange("p h k t -> p h (k t)")

            def residual(n, m, s, gain, add, c=None):
                x = xT[:, :, :].rearrange("p k t -> p (k t)")[:, bass.ds(m * T, T)]
                g2 = flat(xg)
                if add:
                    dve.wait_ge(used.sem, used.at(c))
                    v.tensor_tensor(x, x, psA[:, s, :], ALU.add).then_inc(drained.sem, 1)
                else:
                    dve.wait_ge(su_pe.sem, 3 + n)
                    v.tensor_copy(x, psA[:, s, :]).then_inc(drained.sem, 1)
                dve.wait_ge(res_act.sem, res_act.at(n, "hi"))
                v.scalar_tensor_tensor(g2[:, 1, bass.ds(m * T, T)], x, gain, hi_f(g2[:, 0, bass.ds(m * T, T)]),
                                       ALU.mult, ALU.subtract).then_inc(res_dve.sem, 1)
                dve.wait_ge(res_act.sem, res_act.at(n, "square"))
                v.tensor_tensor(acc[:, :], acc[:, :], sq[:, s, :], ALU.add).then_inc(res_dve.sem, 1)

            def norm(k):
                dve.wait_ge(nm_act.sem, nm_act.at(k))
                v.scalar_tensor_tensor(n_b[:, :], psO[:, :], D * EPS, n_r2[:, :], ALU.add, ALU.mult).then_inc(nm_dve.sem, 1)
                dve.wait_ge(nm_dve.sem, nm_dve.at(k, "newton"))
                v.scalar_tensor_tensor(c_rs[:, :], n_b[:, :], 3.0, n_r0[:, :], ALU.subtract, ALU.mult).then_inc(nm_dve.sem, 1)
                v.memset(acc[:, :], 0.0).then_inc(nm_dve.sem, 1)
                dve.wait_ge(nm_dve.sem, nm_dve.at(k))
                settled(dve)

            def headnorm(n, src, gain, dst_lo, dst_hi, dim, w=T):
                dve.wait_ge(hn_act.sem, hn_act.at(n, "root2"))
                v.scalar_tensor_tensor(n_b[:, 0:w], psO[:, 0:w], dim * EPS, n_r2[:, 0:w], ALU.add, ALU.mult).then_inc(hn_dve.sem, 1)
                dve.wait_ge(hn_dve.sem, hn_dve.at(n, "newton"))
                v.scalar_tensor_tensor(n_b[:, 0:w], n_b[:, 0:w], 3.0, n_r0[:, 0:w], ALU.subtract, ALU.mult).then_inc(hn_dve.sem, 1)
                dve.wait_ge(hn_dve.sem, hn_dve.at(n, "scale"))
                v.scalar_tensor_tensor(h_t[:, 0:w], src, gain, n_b[:, 0:w], ALU.mult, ALU.mult).then_inc(hn_dve.sem, 1)
                dve.wait_ge(hn_act.sem, hn_act.at(n, "hi"))
                v.tensor_tensor(dst_lo, h_t[:, 0:w], hi_f(dst_hi), ALU.subtract).then_inc(hn_dve.sem, 1)

            def pcol(name, i=0):
                return par[:, PAR[name].start + i:PAR[name].start + i + 1]

            v.memset(small[:, 60:61], EPS).then_inc(eps_in.sem, 1)
            link(v.memset(acc[:, :], 0.0))
            link(v.memset(par2[:, :], 0.0))
            link(v.memset(E[:, :, :, :, :].bitcast(F32), 0.0))
            v.memset(vc[:, :, :, :].bitcast(F32), 0.0).then_inc(pad_dve.sem, 1)
            dve.wait_ge(su_pe.sem, 2)
            link(v.tensor_copy(par[:, :], psT[:, 0, 0:PAR_N]))
            link(v.tensor_copy(par2[:, 0:2 * PAR2_N], psT[:, 1, 0:2 * PAR2_N]))
            for f in range(KT):
                residual(f, f, f % 2, pcol("n1", f), False)
            for name in ("qg", "kg"):
                link(v.tensor_scalar(par[:, PAR[name]], par[:, PAR[name]], -0.5, None, ALU.mult))
            dve.wait_ge(g_in, G_DMAS * 16)
            v.tensor_copy(gw[:, 0], gwraw[:, :, :]).then_inc(cg_dve.sem, 1)
            v.tensor_copy(w2[:, :, 0], w2raw[:, :, :, :]).then_inc(su_dve.sem, 1)
            count[0] += 1
            dve.wait_ge(cg_dve.sem, cg_dve.at(0, "gw_hi"))
            v.tensor_tensor(gw[:, 1], gwraw[:, :, :], hi_f(gw[:, 0]), ALU.subtract).then_inc(cg_dve.sem, 1)
            for kv in range(2):
                dve.wait_ge(su_dve.sem, count[0])
                v.tensor_tensor(w2[:, kv, 1], w2raw[:, kv], hi_f(w2[:, kv, 0]), ALU.subtract).then_inc(cg_dve.sem, 1)
            norm(0)
            for kv, name in enumerate(("posk", "posv")):
                link(v.tensor_copy(E[:, kv, 0, 4, 0:16], par[:, PAR[name]]))
                link(v.tensor_tensor(E[:, kv, 1, 4, 0:16], par[:, PAR[name]], hi_f(E[:, kv, 0, 4, 0:16]), ALU.subtract))
            kvf = kvraw[:, :, :].rearrange("p k t -> p (k t)")
            with dve.Fori(0, 3) as i:
                for s in range(4):
                    drain(C_KV + i * 4 + s, T_KV + i * 4 + s, s, kvf[:, bass.ds(i * 4 * T + s * T, T)])
            dve.wait_ge(cg_pe.sem, cg_pe.at(0, "gates"))
            v.scalar_tensor_tensor(gsc[0:48, :], psS[0:48, 0, :], -0.5, c_rs[0:48, :], ALU.mult, ALU.mult).then_inc(cg_dve.sem, 1)
            for n in range(4):
                kv, x = n // 2, n % 2
                dve.wait_ge(e_act.sem, e_act.at(n, "hi"))
                v.tensor_tensor(Et[:, 1], kvraw[:, n, :], hi_f(Et[:, 0]), ALU.subtract).then_inc(e_dve.sem, 1)
                dve.wait_ge(e_dve.sem, e_dve.at(n, "lo"))
                for odd in range(2):
                    v.tensor_copy(E[odd * HD:(odd + 1) * HD, kv, :, 2 * x + 1, 0:T // 2],
                                  Et[HD:P, :, odd::2]).then_inc(e_dve.sem, 1)
            for n in range(4):
                kv, m = n // 2, n % 2
                dve.wait_ge(used.sem, used.at(C_CMP + 2 * n + 1))
                v.tensor_tensor(bcol[:, n:n + 1], psA[:, m, P:P + 1], pcol("b1v" if kv else "b1k", m), ALU.add).then_inc(ch_dve.sem, 1)
                dve.wait_ge(ch_act.sem, ch_act.at(n))
                v.tensor_tensor(hidr[:, kv, 1, m], hidc[:, m, :], hi_f(hidr[:, kv, 0, m]), ALU.subtract).then_inc(drained.sem, 1)
            for n in range(4):
                br, x = n // 2, n % 2
                headnorm(n, kvraw[:, 4 + 4 * br + x, :], pcol("kg", 1 + br), kn[:, br, x, 1], kn[:, br, x, 0], HD)
            for n in range(4):
                br, x = n // 2, n % 2
                dve.wait_ge(vt_act.sem, vt_act.at(n))
                v.tensor_tensor(vtok[:, br, 1, :, x * P:(x + 1) * P], psT[:, n % 3, :].rearrange("p (k d) -> p k d", d=P),
                                hi_f(vtok[:, br, 0, :, x * P:(x + 1) * P]), ALU.subtract).then_inc(vt_dve.sem, 1)
            dve.wait_ge(kv_pe.sem, 1)
            v.tensor_scalar(kcraw[:, :], psS[:, 0, 0:P], pcol("b2k"), None, ALU.add).then_inc(kv_dve.sem, 1)
            v.tensor_tensor(vcraw[0:32], psS[0:32, 1, 256:512].rearrange("p (g d) -> p g d", d=HD),
                            b2v[0:32, :].unsqueeze(1).broadcast_to([32, GROUPS, HD]), ALU.add).then_inc(kv_dve.sem, 1)
            dve.wait_ge(kv_dve.sem, kv_dve.at(0, "v"))
            dve.wait_ge(pad_dve.sem, pad_dve.at(0, "vc"))

            def diagonal(h, b):
                return vc[32 * b:32 * b + 32, h, :, b * HD:(b + 1) * HD]

            for b in range(2):
                v.tensor_copy(diagonal(0, b), vcraw[0:32, b::2, :]).then_inc(kv_dve.sem, 1)
            for b in range(2):
                dve.wait_ge(kv_dve.sem, kv_dve.at(0, f"v_hi{b}"))
                if b:
                    v.tensor_copy(vcraw2[32:64], vcraw[0:32]).then_inc(kv_dve.sem, 1)
                    dve.wait_ge(kv_dve.sem, kv_dve.at(0, "v_moved"))
                src = (vcraw, vcraw2)[b][32 * b:32 * b + 32, b::2, :]
                v.tensor_tensor(diagonal(1, b), src, hi_f(diagonal(0, b)), ALU.subtract).then_inc(kv_dve.sem, 1)
            headnorm(4, kcraw[:, :], pcol("kg", 0), kc[:, 1], kc[:, 0], HD, P)

            def query(n):
                drain(C_Q + n, T_Q + n, n, qraw[:, :])

            def query_norm(n):
                dve.wait_ge(qr_act.sem, qr_act.at(n))
                v.scalar_tensor_tensor(n_b[:, :], psA[:, (n + 1) % 2, :], HD * EPS, n_r2[:, :], ALU.add, ALU.mult).then_inc(q_dve.sem, 1)
                dve.wait_ge(q_dve.sem, q_dve.at(n, "newton"))
                v.scalar_tensor_tensor(n_b[:, :], n_b[:, :], 3.0, n_r0[:, :], ALU.subtract, ALU.mult).then_inc(q_dve.sem, 1)
                dve.wait_ge(q_dve.sem, q_dve.at(n, "scale"))
                v.scalar_tensor_tensor(h_t[:, :], qraw[:, :], pcol("qg"), n_b[:, :], ALU.mult, ALU.mult).then_inc(q_dve.sem, 1)

            def query_lo(n):
                for hd in range(2):
                    rows = slice(hd * HD, (hd + 1) * HD)
                    dve.wait_ge(qi_act.sem, qi_act.at(n, f"head{hd}"))
                    v.tensor_tensor(qz[rows, hd, 1, :], h_t[rows, :], hi_f(qz[rows, hd, 0, :]), ALU.subtract).then_inc(q_dve.sem, 1)

            def biases(n, hds, c=False):
                for hd in hds:
                    h = CONST["slope"].start + n + 8 * hd
                    dst, name = (cbias, "cdist") if c else (bias, "dist")
                    v.tensor_scalar(dst[:, hd, :], con[:, CONST[name]], con[:, h:h + 1], None, ALU.mult).then_inc(b_dve.sem, 1)

            def maxima(U, xs):
                n, hd, o = U // 4, U % 4 // 2, 32 * (U % 2)
                dve.wait_ge(b_dve.sem, b_dve.at(n, f"head{hd}"))
                for x in xs:
                    qt = TT - 1 - x
                    w = P * (qt + 1)
                    dve.wait_ge(us_pe.sem, us_pe.at(U, f"s{x}"))
                    v.tensor_tensor_reduce(out=Pm[:, U % 2, P_AT[qt]:P_AT[qt] + w], in0=bias[:, hd, T - w:T],
                                           in1=psS[:, x % 2, 0:w], scale=1.0, scalar=-3e38, op0=ALU.add,
                                           op1=ALU.max, accum_out=st[:, o + qt:o + qt + 1]).then_inc(um_dve.sem, 1)
                if 3 in xs:
                    dve.wait_ge(um_dve.sem, um_dve.at(U, "max3"))
                    v.tensor_scalar(st[:, o + 4:o + 8], st[:, o:o + 4], -HD ** -0.5, None, ALU.mult).then_inc(um_dve.sem, 1)

            def probabilities(U):
                n, hd, br, o = U // 4, U % 4 // 2, U % 2, 32 * (U % 2)
                dve.wait_ge(ue_act.sem, ue_act.at(U))
                v.reciprocal(st[:, o + 12:o + 16], st[:, o + 8:o + 12]).then_inc(ug_dve.sem, 1)
                dve.wait_ge(ug_dve.sem, ug_dve.at(U, "rec"))
                g = 3 * (n + 8 * hd) + 1 + br
                v.tensor_tensor(st[:, o + 16:o + 20].unsqueeze(2), st[:, o + 12:o + 16].unsqueeze(2), gates[:, :, g:g + 1],
                                ALU.mult).then_inc(ug_dve.sem, 1)
                dve.wait_ge(ug_dve.sem, ug_dve.at(U))
                for qt in range(TT):
                    pq = Pm[:, U % 2, P_AT[qt]:P_AT[qt] + P * (qt + 1)]
                    v.tensor_scalar(pq, pq, st[:, o + 16 + qt:o + 17 + qt], None, ALU.mult).then_inc(up_dve1.sem, 1)

            def lo(U):
                dve.wait_ge(uh_act.sem, uh_act.at(U))
                v.tensor_tensor(PT[:, 1, :], psT[:, :, :].rearrange("p b t -> p (b t)")[:, 0:1280], hi_f(PT[:, 0, :]),
                                ALU.subtract).then_inc(ul_dve.sem, 1)

            pcq = Pc[:, :, :, :].rearrange("p q h n -> p h q n")

            def per_row(o):
                return cst[:, o:o + 8].rearrange("p (h q o) -> p h q o", h=2, o=1).broadcast_to([P, 2, TT, 32])

            def c_maxima(n):
                dve.wait_ge(b_dve.sem, b_dve.at(n))
                dve.wait_ge(cs_pe.sem, cs_pe.at(n))
                v.tensor_tensor(pcq, psS[:, :, 0:P].rearrange("p h (q n) -> p h q n", n=32),
                                cbias[:, :, :].rearrange("p h (q n) -> p h q n", n=32), ALU.add).then_inc(cm_dve.sem, 1)
                dve.wait_ge(cm_dve.sem, cm_dve.at(n, "add"))
                v.tensor_reduce(cst[:, 0:8].rearrange("p (h q) -> p h q", h=2), pcq, AX.X, ALU.max).then_inc(cm_dve.sem, 1)
                dve.wait_ge(cm_dve.sem, cm_dve.at(n, "max"))
                v.tensor_tensor(pcq, pcq, per_row(0), ALU.subtract).then_inc(cm_dve.sem, 1)

            def c_probabilities(n):
                def step(i, name):
                    i.then_inc(cp_dve.sem, 1)
                    dve.wait_ge(cp_dve.sem, cp_dve.at(n, name))

                dve.wait_ge(ce_act.sem, ce_act.at(n))
                mask = con[:, CONST["cmask"]].rearrange("p (q n) -> p q n", n=32).unsqueeze(1).broadcast_to([P, 2, TT, 32])
                step(v.tensor_tensor(pcq, pcq, mask, ALU.mult), "mask")
                step(v.tensor_reduce(cst[:, 8:16].rearrange("p (h q) -> p h q", h=2), pcq, AX.X, ALU.add), "sum")
                step(v.tensor_scalar(cst[:, 16:24], cst[:, 8:16], 1e-30, None, ALU.max), "guard")
                step(v.reciprocal(cst[:, 24:32], cst[:, 16:24]), "rec")
                gt = gates[:, :, :].rearrange("p q (h m r) -> p h q m r", h=2, r=3)[:, :, :, n, 0:1]
                step(v.tensor_tensor(cst[:, 32:40].rearrange("p (h q o) -> p h q o", h=2, o=1),
                                     cst[:, 24:32].rearrange("p (h q o) -> p h q o", h=2, o=1), gt, ALU.mult), "gate")
                v.tensor_tensor(pcq, pcq, per_row(32), ALU.mult).then_inc(cp_dve.sem, 1)

            def c_lo(n):
                dve.wait_ge(ch_act2.sem, ch_act2.at(n))
                v.tensor_tensor(PTc[1][0:HD, :], psA[0:HD, n % 2, :], hi_f(PTc[0][0:HD, :]), ALU.subtract).then_inc(cl_dve.sem, 1)

            def out_lo(n, hd):
                rows = slice(hd * HD, (hd + 1) * HD)
                dve.wait_ge(oh_act.sem, oh_act.at(2 * n + hd))
                v.tensor_tensor(attnT[rows, 1, n, :], psO[rows, :], hi_f(attnT[rows, 0, n, :]), ALU.subtract).then_inc(ol_dve.sem, 1)

            def unit(U, extra=None):
                if U + 2 < 32:
                    maxima(U + 2, (0, 1))
                lo(U)
                if extra is not None:
                    c_lo(extra)
                if U + 2 < 32:
                    maxima(U + 2, (2, 3))
                if U + 1 < 32:
                    probabilities(U + 1)

            for hd in range(2):
                v.memset(qz[HD - hd * HD:P - hd * HD, hd, :, :].bitcast(F32), 0.0).then_inc(pad_dve.sem, 1)
                v.memset(PTc[hd][HD:P, :].bitcast(F32), 0.0).then_inc(pad_dve.sem, 1)
            query(0)
            query_norm(0)
            query_lo(0)
            biases(0, (0, 1))
            biases(0, (0, 1), True)
            query(1)
            maxima(0, range(4))
            maxima(1, range(4))
            probabilities(0)
            for n in range(8):
                U, last = 4 * n, n == 7
                if n:
                    out_lo(n - 1, 1)
                c_maxima(n)
                unit(U)
                if not last:
                    query_norm(n + 1)
                c_probabilities(n)
                if not last:
                    biases(n + 1, (0,))
                unit(U + 1, n)
                if not last:
                    query_lo(n + 1)
                out_lo(n, 0)
                unit(U + 2)
                if not last:
                    biases(n + 1, (1,))
                    biases(n + 1, (0, 1), True)
                unit(U + 3)
                if n < 6:
                    query(n + 2)
            out_lo(7, 1)

            dve.wait_ge(cv_pe.sem, cv_pe.at(15))
            link(v.memset(acc[:, :], 0.0))
            lam = par[:, PAR["lam"]]
            z, f1, f2, f3 = (small[:, 16 + 8 * j:24 + 8 * j] for j in range(4))
            v.scalar_tensor_tensor(z, lam, -1.0, lam, ALU.mult, ALU.max).then_inc(sp_dve.sem, 1)
            dve.wait_ge(sp_act.sem, 1)
            link(v.tensor_scalar(f1, z, 2.0, None, ALU.add))
            link(v.reciprocal(f2, f1))
            link(v.tensor_tensor(f1, z, f2, ALU.mult))
            link(v.tensor_tensor(f2, f1, f1, ALU.mult))
            link(v.tensor_scalar(f3, f2, 1.0 / 19, None, ALU.mult))
            for odd in (17, 15, 13, 11, 9, 7, 5, 3):
                link(v.scalar_tensor_tensor(f3, f3, 1.0 / odd, f2, ALU.add, ALU.mult))
            link(v.scalar_tensor_tensor(f3, f3, 1.0, f1, ALU.add, ALU.mult))
            link(v.tensor_scalar(f1, lam, -8.0, 0.0, ALU.mult, ALU.max))
            link(v.scalar_tensor_tensor(small[:, 0:8], f3, 16.0, f1, ALU.mult, ALU.add))
            link(v.tensor_scalar(small[:, 8:16], small[:, 0:8], -1.0, None, ALU.mult))
            v.memset(bd[:, :, :, :].bitcast(F32), 0.0).then_inc(lw_dve.sem, 1)
            v.memset(lx[:, 0:3], 0.0).then_inc(lw_dve.sem, 1)
            dve.wait_ge(lw_dve.sem, lw_dve.at(0))
            dve.wait_ge(lw_in, 32)

            def col(name, i):
                return par[:, bass.ds(i + PAR[name].start, 1)]

            r_, i_, t_, a_, u_ = lt
            s_, o_ = t_, i_
            with dve.Fori(0, KT) as m:
                def step(i):
                    i.then_inc(lr_dve.sem, 1)

                def own(name):
                    dve.wait_ge(lr_dve.sem, lr_dve.at(m, name))

                def act(name):
                    dve.wait_ge(lr_act.sem, lr_act.at(m, name))

                c, t = C_LRU + m * 4, T_LRU + m * 4
                drain(c, t, 0, lx[:, 3:T + 3])
                dve.wait_ge(drained.sem, drained.at(t))
                step(v.tensor_scalar(xc[:, :], lx[:, 3:T + 3], col("cw", m + 3 * KT), col("cb", m), ALU.mult, ALU.add))
                for k in range(3):
                    own(f"tap{k}")
                    step(v.scalar_tensor_tensor(xc[:, :], lx[:, 2 - k:T + 2 - k], col("cw", m + (2 - k) * KT), xc[:, :],
                                                ALU.mult, ALU.add))
                drain(c + 1, t + 1, 1, gl[:, :])
                act("hi")
                step(v.tensor_tensor(xcr[:, 1], xc[:, :], hi_f(xcr[:, 0]), ALU.subtract))
                for b in range(2):
                    rows = slice(b * HD, (b + 1) * HD)
                    act(f"w{b}")
                    raw = lruw[:, :, :, :].rearrange("p w m j -> p w (m j)")[rows, :, bass.ds(m * HD, HD)]
                    step(v.tensor_tensor(bd[rows, 1, :, rows], raw, hi_f(bd[rows, 0, :, rows]), ALU.subtract))
                drain(c + 2, t + 2, 2, mg[:, :])
                act("tanh")
                step(v.tensor_scalar(u_[:, :], t_[:, :], 1.0, None, ALU.add))
                own("one")
                step(v.reciprocal(u_[:, :], u_[:, :]))
                own("rec")
                step(v.tensor_tensor(u_[:, :], u_[:, :], t_[:, :], ALU.mult))
                step(v.tensor_tensor(o_[:, :], i_[:, :], xc[:, :], ALU.mult))
                dve.wait_ge(used.sem, used.at(c + 3))
                v.tensor_tensor(mixT[:, :, :].rearrange("p k t -> p (k t)")[:, bass.ds(m * T, T)], mg[:, :], psA[:, 1, :],
                                ALU.mult).then_inc(drained.sem, 1)
                act("root")
                own("ix")
                step(v.tensor_tensor(u_[:, :], s_[:, :], o_[:, :], ALU.mult))
                own("b")
                step(v.tensor_tensor_scan(o_[:, :], a_[:, :], u_[:, :], 0.0, ALU.mult, ALU.add))
                own("scan")
                step(v.tensor_tensor(u_[:, :], o_[:, :], gl[:, :], ALU.mult))
                act("out_hi")
                at = bass.ds(m * T, T)
                step(v.tensor_tensor(flat(lruT)[:, 1, at], u_[:, :], hi_f(flat(lruT)[:, 0, at]), ALU.subtract))
                own("out_lo")

            mrgf, mixf = flat(attnT), mixT[:, :, :].rearrange("p k t -> p (k t)")
            with dve.Fori(0, KT) as m:
                c, t = C_MIX + m * 2, T_MIX + m * 2
                at = bass.ds(m * T, T)
                drain(c, t, 0, mg[:, :])
                dve.wait_ge(used.sem, used.at(c + 1))
                dve.wait_ge(mx_act.sem, mx_act.at(m, "gate"))
                v.tensor_tensor(gl[:, :], mg[:, :], psA[:, 1, :], ALU.mult).then_inc(drained.sem, 1)
                dve.wait_ge(drained.sem, drained.at(t + 1))
                v.tensor_tensor(xc[:, :], gl[:, :], mixf[:, at], ALU.add).then_inc(mx_dve.sem, 1)
                dve.wait_ge(mx_act.sem, mx_act.at(m, "hi"))
                v.tensor_tensor(mrgf[:, 1, at], xc[:, :], hi_f(mrgf[:, 0, at]), ALU.subtract).then_inc(mx_dve.sem, 1)

            def tail_dve(c0, t0, k, n, ff, gain2, gain1):
                with dve.Fori(0, 4) as i:
                    for s in range(2):
                        residual(i * 2 + (n + s), i * 2 + s, s, gain2(i * 2 + s), True, c0 + i * 2 + s)
                norm(k)
                hf = flat(hid)
                with dve.Fori(0, FT) as f:
                    c, t = c0 + 8 + f * 2, t0 + 8 + f * 2
                    drain(c, t, 0, fg[:, 0, :])
                    drain(c + 1, t + 1, 1, fu[:, :])
                    dve.wait_ge(drained.sem, drained.at(t + 1))
                    dve.wait_ge(ff_act.sem, ff_act.at(f + ff, "silu"))
                    v.tensor_tensor(ft[:, :], fg[:, 1, :], fu[:, :], ALU.mult).then_inc(ff_dve.sem, 1)
                    dve.wait_ge(ff_act.sem, ff_act.at(f + ff, "hi"))
                    at = bass.ds(f * T, T)
                    v.tensor_tensor(hf[:, 1, at], ft[:, :], hi_f(hf[:, 0, at]), ALU.subtract).then_inc(ff_dve.sem, 1)
                c1, t1 = c0 + 8 + 2 * FT, t0 + 8 + 2 * FT
                with dve.Fori(0, 4) as i:
                    for s in range(2):
                        residual(i * 2 + (n + 8 + s), i * 2 + s, s, gain1(i * 2 + s), True, c1 + i * 6 + (3 * s + 2))
                norm(k + 1)

            def col2(i):
                return par2[:, bass.ds(i, 1)]

            tail_dve(C_WO, T_WO, 1, 8, 0, lambda m: col("n2", m), lambda m: col2(m + PAR2["n1"].start))

            def layer_col(name, m=0):
                return lay[:, PAR2[name].start + m:PAR2[name].start + m + 1]

            def headnorm2(n, x):
                c = n * 4 + x

                def step(i, name):
                    i.then_inc(h2_dve.sem, 1)
                    dve.wait_ge(h2_dve.sem, h2_dve.at(c, name))

                r32 = slice(0, 32)
                dve.wait_ge(h2_root.sem, h2_root.at(c, "root2"))
                step(v.scalar_tensor_tensor(n_b[:, :], psO[:, :], QK2 * EPS, n_r2[:, :], ALU.add, ALU.mult), "newton")
                step(v.scalar_tensor_tensor(n_b[:, :], n_b[:, :], 3.0, n_r0[:, :], ALU.subtract, ALU.mult), "scale")
                step(v.scalar_tensor_tensor(norm2[:, :], raw2[:, x, :], layer_col("kg" if x >= 2 else "qg"), n_b[:, :], ALU.mult, ALU.mult), "apply")
                settled(dve)
                step(v.stream_shuffle(rot[r32, :], norm2[r32, :], [(p + 16) % 32 for p in range(32)]), "swap")
                step(v.tensor_tensor(rot[r32, :], rot[r32, :], con2[r32, CON2["sin"]], ALU.mult), "sin")
                step(v.tensor_tensor(norm2[r32, :], norm2[r32, :], con2[r32, CON2["cos"]], ALU.mult), "cos")
                step(v.tensor_tensor(norm2[r32, :], norm2[r32, :], rot[r32, :], ALU.add), "rot")
                dve.wait_ge(h2_hi.sem, h2_hi.at(c, "hi"))
                v.tensor_tensor(qk2[:, x, 1], norm2[:, :], hi_f(qk2[:, x, 0]), ALU.subtract).then_inc(h2_dve.sem, 1)

            def values2(n, x):
                dve.wait_ge(v2_act.sem, v2_act.at(n * 2 + x))
                at = slice(x * P, (x + 1) * P)
                v.tensor_tensor(vtok2[:, 1, :, at], psT[:, x, :].rearrange("p (k d) -> p k d", d=P), hi_f(vtok2[:, 0, :, at]),
                                ALU.subtract).then_inc(v2_dve.sem, 1)

            def softmax2(n):
                def step(i):
                    i.then_inc(a2_dve.sem, 1)

                def own(name):
                    dve.wait_ge(a2_dve.sem, a2_dve.at(n, name))

                for c in range(2):
                    o = 32 * c
                    for x, qt in enumerate((3, 2, 1, 0)):
                        w = P * (qt + 1)
                        dve.wait_ge(a2_pe.sem, a2_pe.at(n, f"s{c}_{x}"))
                        settled(dve)
                        step(v.tensor_tensor_reduce(out=Pm2[:, c, P_AT[qt]:P_AT[qt] + w], in0=con2[:, CON2["chunk"]][:, T - w:T],
                                                    in1=psS[:, x % 2, 0:w], scale=1.0, scalar=-3.3e38, op0=ALU.add, op1=ALU.max,
                                                    accum_out=st2[:, o + qt:o + qt + 1]))
                    own(f"max{c}_3")
                    step(v.tensor_scalar(st2[:, o + 4:o + 8], st2[:, o:o + 4], -QK2 ** -0.5, None, ALU.mult))
                dve.wait_ge(a2_act.sem, a2_act.at(n, "exp1_3"))
                sums = st2[:, :].rearrange("p (c x) -> p c x", c=2)
                step(v.reciprocal(sums[:, :, 12:16], sums[:, :, 8:12]))
                own("rec")
                step(v.tensor_scalar(st2[:, 48:52], st2[:, 44:48], small[:, 36:37], None, ALU.mult))
                own("neg")
                for qt in range(TT):
                    at = slice(P_AT[qt], P_AT[qt] + P * (qt + 1))
                    step(v.tensor_scalar(Pm2[:, 0, at], Pm2[:, 0, at], st2[:, 12 + qt:13 + qt], None, ALU.mult))
                for qt in range(TT):
                    at = slice(P_AT[qt], P_AT[qt] + P * (qt + 1))
                    own(f"scale{qt}")
                    step(v.scalar_tensor_tensor(Pm2[:, 0, at], Pm2[:, 1, at], st2[:, 48 + qt:49 + qt], Pm2[:, 0, at], ALU.mult, ALU.add))

            def lo2(n):
                dve.wait_ge(a2_act.sem, a2_act.at(n, "hi"))
                v.tensor_tensor(PT2[:, 1, :], psT[:, :, :].rearrange("p b t -> p (b t)")[:, 0:1280], hi_f(PT2[:, 0, :]),
                                ALU.subtract).then_inc(a2_dve.sem, 1)

            def copy2(n):
                dve.wait_ge(a2_pe.sem, a2_pe.at(n, "v"))
                for d in range(2):
                    v.tensor_copy(os2[:, d, :], psS[:, d, :]).then_inc(a2_dve.sem, 1)

            def out2(n, h):
                dve.wait_ge(a2_act.sem, a2_act.at(n, "root2"))
                v.scalar_tensor_tensor(n_b[:, :], psO[:, :], V2 * EPS, n_r2[:, :], ALU.add, ALU.mult).then_inc(a2_dve.sem, 1)
                dve.wait_ge(a2_dve.sem, a2_dve.at(n, "newton"))
                v.scalar_tensor_tensor(n_b[:, :], n_b[:, :], 3.0, n_r0[:, :], ALU.subtract, ALU.mult).then_inc(a2_dve.sem, 1)
                dve.wait_ge(a2_dve.sem, a2_dve.at(n, "scale"))
                af = aT2[:, :, :].rearrange("p k t -> p (k t)")
                for d in range(2):
                    v.scalar_tensor_tensor(af[:, bass.ds(h * 2 * T + d * T, T)] if not isinstance(h, int) else aT2[:, 2 * h + d, :], os2[:, d, :], layer_col("sub", d), n_b[:, :],
                                           ALU.mult, ALU.mult).then_inc(a2_dve.sem, 1)

            dve.wait_ge(c2_in, 16)
            with dve.Fori(0, LAYERS) as l:
                c0, t0 = l * C_LAYER + C_B2, l * T_LAYER + T_B2

                def once(i, name):
                    i.then_inc(ly_dve.sem, 1)
                    dve.wait_ge(ly_dve.sem, ly_dve.at(l, name))

                once(v.tensor_copy(lay[:, :], par2[:, bass.ds(l * PAR2_N, PAR2_N + KT)]), "copy")
                once(v.tensor_scalar(lay[:, PAR2["qg"].start:PAR2["kg"].stop], lay[:, PAR2["qg"].start:PAR2["kg"].stop], -0.5, None, ALU.mult), "gains")
                init = con[:, bass.ds(l * 2 + CONST["lam"].start, 1)]
                once(v.tensor_scalar(lay[:, PAR2["sub"]], lay[:, PAR2["sub"]], con[:, bass.ds(l * 2 + (CONST["lam"].start + 1), 1)], None, ALU.mult), "sub")
                lq = lay[:, PAR2["lam"]].rearrange("p (c x) -> p c x", x=2)
                once(v.tensor_tensor(small[:, 32:34].unsqueeze(2), lq[:, :, 0:1], lq[:, :, 1:2], ALU.mult), "products")
                dve.wait_ge(ly_act.sem, ly_act.at(l))
                once(v.tensor_tensor(small[:, 36:37], small[:, 35:36], small[:, 34:35], ALU.subtract), "diff")
                once(v.tensor_tensor(small[:, 36:37], small[:, 36:37], init, ALU.subtract), "lambda")
                settled(dve)
                def tile2(c, t, x):
                    drain(c + x, t + x, x, raw2[:, x, :])
                    if x >= 4:
                        dve.wait_ge(drained.sem, drained.at(t + x))

                def raw_values(c, t, x):
                    tile2(c, t, 4 + x)
                    v.sem_inc(v2_raw.sem, 1)

                n0 = l * HEADS2
                tile2(c0, t0, 0)
                for x in range(4):
                    if x < 3:
                        tile2(c0, t0, x + 1)
                    else:
                        raw_values(c0, t0, 0)
                    headnorm2(n0, x)
                raw_values(c0, t0, 1)
                values2(n0, 0)
                values2(n0, 1)
                settled(dve)
                with dve.Fori(0, HEADS2 - 1) as h:
                    n = l * HEADS2 + h
                    c, t = c0 + h * 6 + 6, t0 + h * 6 + 6
                    softmax2(n)
                    tile2(c, t, 0)
                    tile2(c, t, 1)
                    lo2(n)
                    headnorm2(n + 1, 0)
                    tile2(c, t, 2)
                    headnorm2(n + 1, 1)
                    copy2(n)
                    tile2(c, t, 3)
                    headnorm2(n + 1, 2)
                    out2(n, h)
                    raw_values(c, t, 0)
                    headnorm2(n + 1, 3)
                    raw_values(c, t, 1)
                    values2(n + 1, 0)
                    values2(n + 1, 1)

                def upool(i):
                    i.then_inc(up_dve.sem, 1)

                def pool2(m):
                    g = m // 2
                    w, e = POOL_W[g], CONST["edge"].start + sum(POOL_W[:g])
                    t, c = t0 + (U_U + m), c0 + (L_U + m)
                    drain(c, t, m, ur[:, m % 2, 16:T + 16])
                    dve.wait_ge(drained.sem, drained.at(t))
                    src = ur[:, m % 2]
                    for k in range(g + 1):
                        dst, b = (ya, yb)[k % 2], 1 << k
                        lo = 2 * b - 1
                        upool(v.tensor_tensor(dst[:, lo:T + 16], src[:, lo:T + 16], src[:, lo - b:T + 16 - b], ALU.add))
                        dve.wait_ge(up_dve.sem, up_dve.at(l, f"y{m}_{k}"))
                        src = dst
                    upool(v.tensor_tensor(src[:, 16:16 + w], src[:, 16:16 + w], con[:, e:e + w], ALU.mult))
                    dve.wait_ge(up_dve.sem, up_dve.at(l, f"edge{m}"))
                    upool(v.scalar_tensor_tensor(pr[:, :], src[:, 16:T + 16], 1.0 / w, ur[:, m % 2, 16:T + 16], ALU.mult, ALU.subtract))
                    dve.wait_ge(up_act.sem, up_act.at(l * KT + m))
                    upool(v.tensor_tensor(mix2[:, 1, m], pr[:, :], hi_f(mix2[:, 0, m]), ALU.subtract))

                n = n0 + (HEADS2 - 1)
                softmax2(n)
                for b in range(2):
                    upool(v.memset(ur[:, b, 0:16], 0.0))
                pool2(0)
                lo2(n)
                pool2(1)
                copy2(n)
                pool2(2)
                pool2(3)
                out2(n, HEADS2 - 1)
                for m in range(4, KT):
                    pool2(m)
                for m in range(KT):
                    dve.wait_ge(used.sem, used.at(c0 + (L_PW + m // 2)))
                    v.tensor_scalar(poolT[:, m, :], psA[:, m % 2, :], layer_col("ps", m), None, ALU.mult).then_inc(drained.sem, 1)
                dve.wait_ge(drained.sem, drained.at(t0 + (U_PW + 7)))
                settled(dve)
                pf, af = (x[:, :, :].rearrange("p k t -> p (k t)") for x in (poolT, aT2))
                with dve.Fori(0, KT) as m:
                    n = l * KT + m
                    at = bass.ds(m * T, T)
                    for s in range(2):
                        drain(c0 + L_GAB + m * 2 + s, t0 + U_GAB + m * 2 + s, s, mg2[:, s, :])
                    for s, (name, src) in enumerate((("ga", pf), ("gb", af))):
                        dve.wait_ge(m2_act.sem, m2_act.at(n, name))
                        v.tensor_tensor(mg2[:, s, :], mg2[:, s, :], src[:, at], ALU.mult).then_inc(m2_dve.sem, 1)
                    dve.wait_ge(m2_dve.sem, m2_dve.at(n, "attn"))
                    v.tensor_tensor(mt2[:, :], mg2[:, 0, :], mg2[:, 1, :], ALU.add).then_inc(m2_dve.sem, 1)
                    dve.wait_ge(m2_act.sem, m2_act.at(n, "hi"))
                    v.tensor_tensor(flat(mix2)[:, 1, at], mt2[:, :], hi_f(flat(mix2)[:, 0, at]), ALU.subtract).then_inc(m2_dve.sem, 1)

                def gain(name):
                    start = PAR2_N if name == "next" else PAR2[name].start
                    return lambda m: lay[:, bass.ds(m + start, 1)]

                tail_dve(c0 + L_WO, t0 + U_WO, l * 2 + 3, l * 16 + 24, l * FT + FT, gain("n2"), gain("next"))

        @block.scalar
        def _(act):
            ac = nc.scalar.activation

            def flat(b):
                return b[:, :, :, :].rearrange("p h k t -> p h (k t)")

            act.dma_start(con[:, :], a["const"][:, 0:CONST_2]).then_inc(c_in, 16)
            done = [0]

            def rows(dst, r0, src, cols=slice(0, P)):
                n = src.shape[0]
                act.dma_start(dst[r0:r0 + n, cols], src).then_inc(p_in, 16)
                done[0] += 1

            def vec(name, l=0):
                return a[name][l].rearrange("(r p) -> r p", p=P)

            for key, name in (("n1", "norm1_g"), ("n2", "norm2_g"), ("cb", "conv_b"), ("ba", "lru_ba"), ("bi", "lru_bi"),
                              ("lam", "lru_lambda"), ("b1k", "cmp_b1_k"), ("b1v", "cmp_b1_v")):
                rows(prow, PAR[key].start, vec(name))
            rows(prow, PAR["cw"].start, a["conv_w"][0].rearrange("k o (m p) -> (k o m) p", p=P))
            for half in range(2):
                cols = slice(half * HD, (half + 1) * HD)
                rows(prow, PAR["qg"].start, a["q_norm_g"], cols)
                rows(prow, PAR["kg"].start, a["k_norm_g"][0], cols)
                rows(prow, PAR["b2k"].start, a["cmp_b2_k"], cols)
            for key, name in (("posk", "cmp_pos_k"), ("posv", "cmp_pos_v")):
                rows(prow, PAR[key].start, a[name][0].rearrange("(j l) d -> j (l d)", l=2))
            for l in range(LAYERS):
                for key, name in (("n1", "norm1_g_2"), ("n2", "norm2_g_2"), ("ps", "pool_scale_2"), ("qg", "q_norm_g_2"),
                                  ("kg", "k_norm_g_2"), ("sub", "subln_g_2")):
                    rows(prow2, l * PAR2_N + PAR2[key].start, vec(name, l))
                for j, name in enumerate(("lam_q1_2", "lam_k1_2", "lam_q2_2", "lam_k2_2")):
                    rows(prow2, l * PAR2_N + PAR2["lam"].start + j, vec(name, l))
            assert done[0] == P_DMAS, done
            gd = 0
            for dst, src in ((gwraw[:, :, :], w_in.rearrange("(k p) n -> p k n", p=P)[:, :, 2560:2608]),
                             (w2raw[:, 0, :, 0:HD], a["cmp_w2_k"][0].rearrange("(k p) d -> p k d", p=P)),
                             (w2raw[:, 0, :, HD:P], a["cmp_w2_k"][0].rearrange("(k p) d -> p k d", p=P)),
                             (w2raw[:, 1, :, 0:HD], a["cmp_w2_v"][0].rearrange("(k p) d -> p k d", p=P)),
                             (w2raw[:, 1, :, HD:P], a["cmp_w2_v"][0].rearrange("(k p) d -> p k d", p=P)),
                             (b2v[0:32, :], a["cmp_b2_v"][0].partition_broadcast(32))):
                act.dma_start(dst, src).then_inc(g_in, 16)
                gd += 1
            assert gd == G_DMAS

            def logexp():
                nc.scalar.preload_act_table_set("natural_log_exp_and_others")

            def roots(sums, dim, of, n, w=T):
                ac(n_r2[:, 0:w], sums, ACT.Ln, bias=small[:, 60:61], scale=1.0 / dim).then_inc(of.sem, 1)
                act.wait_ge(of.sem, of.at(n, "log"))
                ac(n_r0[:, 0:w], n_r2[:, 0:w], ACT.Exp, scale=-0.5).then_inc(of.sem, 1)
                act.wait_ge(of.sem, of.at(n, "root"))
                ac(n_r2[:, 0:w], n_r0[:, 0:w], ACT.Square, scale=dim ** -0.5).then_inc(of.sem, 1)

            def residual(n, t, m, s, gain):
                x = xT[:, :, :].rearrange("p k t -> p (k t)")[:, bass.ds(m * T, T)]
                act.wait_ge(drained.sem, drained.at(t))
                ac(flat(xg)[:, 0, bass.ds(m * T, T)], x, ACT.Copy, scale=gain).then_inc(res_act.sem, 1)
                ac(sq[:, s, :], x, ACT.Square).then_inc(res_act.sem, 1)

            def norm(k):
                logexp()
                act.wait_ge(nm_pe.sem, nm_pe.at(k))
                roots(psO[:, :], D, nm_act, k)

            def headnorm(n, src, dst_hi, dim, w=T):
                ac(h_sq[:, 0:w], src, ACT.Square).then_inc(hn_act.sem, 1)
                act.wait_ge(hn_pe.sem, hn_pe.at(n))
                roots(psO[:, 0:w], dim, hn_act, n, w)
                act.wait_ge(hn_dve.sem, hn_dve.at(n, "apply"))
                ac(dst_hi, h_t[:, 0:w], ACT.Copy).then_inc(hn_act.sem, 1)

            def pcol(name, i=0):
                return par[:, PAR[name].start + i:PAR[name].start + i + 1]

            act.wait_ge(eps_in.sem, 1)
            for f in range(KT):
                residual(f, f, f, f % 2, pcol("n1", f))
            norm(0)
            for n in range(4):
                kv, x = n // 2, n % 2
                if n:
                    act.wait_ge(e_dve.sem, e_dve.at(n - 1))
                    act.wait_ge(e_act.sem, e_act.at(n - 1))
                act.wait_ge(drained.sem, drained.at(T_KV + n))
                ac(Et[:, 0], kvraw[:, n, :], ACT.Copy).then_inc(e_act.sem, 1)
                act.wait_ge(e_dve.sem, e_dve.at(n, "lo"))
                for odd in range(2):
                    ac(E[odd * HD:(odd + 1) * HD, kv, :, 2 * x, 0:T // 2], hi_f(Et[0:HD, :, odd::2]), ACT.Copy).then_inc(e_act.sem, 1)
            act.wait_ge(cg_pe.sem, cg_pe.at(0))
            ac(gates[:, :, :], psS[:, 1, 0:192].rearrange("p (t g) -> p t g", g=48), ACT.Sigmoid).then_inc(cg_act.sem, 1)
            for n in range(4):
                kv, m = n // 2, n % 2
                act.wait_ge(ch_dve.sem, n + 1)
                ac(hidc[:, m, :], psA[:, m, 0:P], ACT.Gelu_apprx_tanh, bias=bcol[:, n:n + 1]).then_inc(ch_act.sem, 1)
                act.wait_ge(ch_act.sem, ch_act.at(n, "gelu"))
                ac(hidr[:, kv, 0, m], hidc[:, m, :], ACT.Copy).then_inc(ch_act.sem, 1)
            logexp()
            for n in range(4):
                br, x = n // 2, n % 2
                headnorm(n, kvraw[:, 4 + 4 * br + x, :], kn[:, br, x, 0], HD)
            for n in range(4):
                br, x = n // 2, n % 2
                act.wait_ge(vt_pe.sem, vt_pe.at(n))
                ac(vtok[:, br, 0, :, x * P:(x + 1) * P], psT[:, n % 3, :].rearrange("p (k d) -> p k d", d=P), ACT.Copy).then_inc(vt_act.sem, 1)
            act.wait_ge(kv_dve.sem, kv_dve.at(0, "k"))
            headnorm(4, kcraw[:, :], kc[:, 0], HD, P)

            def query_square(n):
                act.wait_ge(drained.sem, drained.at(T_Q + n))
                ac(h_sq[:, :], qraw[:, :], ACT.Square).then_inc(qs_act.sem, 1)

            def query_roots(n):
                act.wait_ge(q_pe.sem, q_pe.at(n))
                roots(psA[:, (n + 1) % 2, :], HD, qr_act, n)

            def query_hi(n):
                act.wait_ge(q_dve.sem, q_dve.at(n, "apply"))
                for hd in range(2):
                    rows = slice(hd * HD, (hd + 1) * HD)
                    ac(qz[rows, hd, 0, :], h_t[rows, :], ACT.Copy).then_inc(qi_act.sem, 1)

            def exps(U):
                o = 32 * (U % 2)
                act.wait_ge(um_dve.sem, um_dve.at(U))
                for qt in range(TT):
                    pq = Pm[:, U % 2, P_AT[qt]:P_AT[qt] + P * (qt + 1)]
                    ac(pq, pq, ACT.Exp, bias=st[:, o + 4 + qt:o + 5 + qt], scale=HD ** -0.5,
                       accum_out=st[:, o + 8 + qt:o + 9 + qt]).then_inc(ue_act.sem, 1)

            def hi(U):
                act.wait_ge(ut_pe.sem, ut_pe.at(U))
                if U:
                    act.wait_ge(uv_pe.sem, uv_pe.at(U - 1))
                ac(PT[:, 0, :], psT[:, :, :].rearrange("p b t -> p (b t)")[:, 0:1280], ACT.Copy).then_inc(uh_act.sem, 1)

            def c_exps(n):
                act.wait_ge(cm_dve.sem, cm_dve.at(n))
                pcf = Pc[:, :, :, :].rearrange("p q h n -> p (q h n)")
                ac(pcf, pcf, ACT.Exp, scale=HD ** -0.5).then_inc(ce_act.sem, 1)

            def c_hi(n):
                act.wait_ge(ct_pe.sem, ct_pe.at(n))
                ac(PTc[0][0:HD, :], psA[0:HD, n % 2, :], ACT.Copy).then_inc(ch_act2.sem, 1)

            def out_hi(n, hd):
                rows = slice(hd * HD, (hd + 1) * HD)
                act.wait_ge(cv_pe.sem, cv_pe.at(2 * n + hd))
                ac(attnT[rows, 0, n, :], psO[rows, :], ACT.Copy).then_inc(oh_act.sem, 1)

            query_square(0)
            query_roots(0)
            query_hi(0)
            query_square(1)
            exps(0)
            exps(1)
            for n in range(8):
                U, last = 4 * n, n == 7
                if n:
                    out_hi(n - 1, 1)
                c_exps(n)
                hi(U)
                if not last:
                    query_roots(n + 1)
                exps(U + 2)
                hi(U + 1)
                c_hi(n)
                exps(U + 3)
                if not last:
                    query_hi(n + 1)
                out_hi(n, 0)
                hi(U + 2)
                if not last:
                    exps(U + 4)
                hi(U + 3)
                if not last:
                    exps(U + 5)
                if n < 6:
                    query_square(n + 2)
            out_hi(7, 1)

            act.wait_ge(ol_dve.sem, ol_dve.at(15))
            for w, name in enumerate(("lru_wa", "lru_wi")):
                act.dma_start(lruw[:, w, :, :], a[name][0].rearrange("(m b) k j -> (b k) m j", b=2)).then_inc(lw_in, 16)
            z = small[:, 16:24]
            act.wait_ge(sp_dve.sem, 1)
            ac(z, z, ACT.Exp, scale=-1.0).then_inc(sp_act.sem, 1)
            act.wait_ge(lw_in, 32)
            act.wait_ge(lw_dve.sem, lw_dve.at(0))

            def col(name, i):
                return par[:, bass.ds(i + PAR[name].start, 1)]

            r_, i_, t_, a_, u_ = lt
            s_, o_ = t_, i_
            with act.Fori(0, KT) as m:
                def step(i):
                    i.then_inc(lr_act.sem, 1)

                def own(name):
                    act.wait_ge(lr_act.sem, lr_act.at(m, name))

                def dve(name):
                    act.wait_ge(lr_dve.sem, lr_dve.at(m, name))

                dve("tap3")
                step(ac(xcr[:, 0], xc[:, :], ACT.Copy))
                for b in range(2):
                    rw = slice(b * HD, (b + 1) * HD)
                    raw = lruw[:, :, :, :].rearrange("p w m j -> p w (m j)")[rw, :, bass.ds(m * HD, HD)]
                    step(ac(bd[rw, 0, :, rw], raw, ACT.Copy))
                act.wait_ge(drained.sem, drained.at(T_LRU + m * 4 + 1))
                step(ac(gl[:, :], gl[:, :], ACT.Gelu_apprx_tanh))
                act.wait_ge(drained.sem, drained.at(T_LRU + m * 4 + 2))
                step(ac(mg[:, :], mg[:, :], ACT.Sigmoid))
                act.wait_ge(lr_pe.sem, lr_pe.at(m))
                step(ac(r_[:, :], psS[:, 0, :], ACT.Sigmoid, bias=col("ba", m)))
                step(ac(i_[:, :], psS[:, 1, :], ACT.Sigmoid, bias=col("bi", m)))
                own("r")
                step(ac(t_[:, :], r_[:, :], ACT.Tanh, scale=small[:, bass.ds(m, 1)]))
                step(ac(a_[:, :], r_[:, :], ACT.Exp, scale=small[:, bass.ds(m + 8, 1)]))
                dve("ratio")
                step(ac(s_[:, :], u_[:, :], ACT.Sqrt, scale=2.0))
                dve("out")
                step(ac(flat(lruT)[:, 0, bass.ds(m * T, T)], u_[:, :], ACT.Copy))

            with act.Fori(0, KT) as m:
                act.wait_ge(drained.sem, drained.at(T_MIX + m * 2))
                ac(mg[:, :], mg[:, :], ACT.Sigmoid).then_inc(mx_act.sem, 1)
                act.wait_ge(mx_dve.sem, mx_dve.at(m, "sum"))
                ac(flat(attnT)[:, 0, bass.ds(m * T, T)], xc[:, :], ACT.Copy).then_inc(mx_act.sem, 1)

            act.dma_start(con2[:, :], a["const"][:, CONST_2:CONST_N]).then_inc(c2_in, 16)

            def tail_act(t0, k, n, ff, gain2, gain1):
                with act.Fori(0, 4) as i:
                    for s in range(2):
                        residual(i * 2 + (n + s), t0 + i * 2 + s, i * 2 + s, s, gain2(i * 2 + s))
                norm(k)
                nc.scalar.preload_act_table_set("silu_and_others")
                with act.Fori(0, FT) as f:
                    act.wait_ge(drained.sem, drained.at(t0 + 8 + f * 2))
                    ac(fg[:, 1, :], fg[:, 0, :], ACT.Silu).then_inc(ff_act.sem, 1)
                    act.wait_ge(ff_dve.sem, ff_dve.at(f + ff, "product"))
                    ac(flat(hid)[:, 0, bass.ds(f * T, T)], ft[:, :], ACT.Copy).then_inc(ff_act.sem, 1)
                t1 = t0 + 8 + 2 * FT
                with act.Fori(0, 4) as i:
                    for s in range(2):
                        residual(i * 2 + (n + 8 + s), t1 + i * 2 + s, i * 2 + s, s, gain1(i * 2 + s))
                norm(k + 1)

            tail_act(T_WO, 1, 8, 0, lambda m: col("n2", m), lambda m: par2[:, bass.ds(m + PAR2["n1"].start, 1)])
            def square2(t, n, x):
                act.wait_ge(drained.sem, drained.at(t + x))
                if x >= 2:
                    act.wait_ge(h2_pe.sem, h2_pe.at(n * 4 + (x - 2)))
                ac(sq[:, x % 2, :], raw2[:, x, :], ACT.Square).then_inc(h2_act.sem, 1)

            def roots2(n, x):
                c = n * 4 + x
                act.wait_ge(h2_pe.sem, h2_pe.at(c))
                roots(psO[:, :], QK2, h2_root, c)

            def hi2(n, x):
                c = n * 4 + x
                act.wait_ge(h2_dve.sem, h2_dve.at(c, "rot"))
                ac(qk2[:, x, 0], norm2[:, :], ACT.Copy).then_inc(h2_hi.sem, 1)

            def values2(n, x):
                act.wait_ge(v2_pe.sem, v2_pe.at(n * 2 + x))
                ac(vtok2[:, 0, :, x * P:(x + 1) * P], psT[:, x, :].rearrange("p (k d) -> p k d", d=P), ACT.Copy).then_inc(v2_act.sem, 1)

            def exps2(n):
                for c in range(2):
                    o = 32 * c
                    act.wait_ge(a2_dve.sem, a2_dve.at(n, f"max{c}"))
                    for qt in range(TT):
                        pq = Pm2[:, c, P_AT[qt]:P_AT[qt] + P * (qt + 1)]
                        ac(pq, pq, ACT.Exp, bias=st2[:, o + 4 + qt:o + 5 + qt], scale=QK2 ** -0.5,
                           accum_out=st2[:, o + 8 + qt:o + 9 + qt]).then_inc(a2_act.sem, 1)

            def split2(n):
                act.wait_ge(a2_pe.sem, a2_pe.at(n, "t"))
                ac(PT2[:, 0, :], psT[:, :, :].rearrange("p b t -> p (b t)")[:, 0:1280], ACT.Copy).then_inc(a2_act.sem, 1)

            def outsquares2(n):
                for d in range(2):
                    act.wait_ge(a2_dve.sem, a2_dve.at(n, f"copy{d}"))
                    ac(Pm2[:, 1, d * T:(d + 1) * T], os2[:, d, :], ACT.Square).then_inc(a2_act.sem, 1)

            def outroots2(n):
                act.wait_ge(a2_pe.sem, a2_pe.at(n, "sums"))
                roots(psO[:, :], V2, a2_act, n)

            with act.Fori(0, LAYERS) as l:
                t0 = l * T_LAYER + T_B2
                act.wait_ge(ly_pe.sem, ly_pe.at(l))
                ac(small[:, 34:36], psO[:, 0:2], ACT.Exp).then_inc(ly_act.sem, 1)
                n0 = l * HEADS2
                square2(t0, n0, 0)
                for x in range(4):
                    if x < 3:
                        square2(t0, n0, x + 1)
                    roots2(n0, x)
                    hi2(n0, x)
                values2(n0, 0)
                values2(n0, 1)
                with act.Fori(0, HEADS2 - 1) as h:
                    n = l * HEADS2 + h
                    t = t0 + h * 6 + 6
                    exps2(n)
                    square2(t, n + 1, 0)
                    square2(t, n + 1, 1)
                    roots2(n + 1, 0)
                    split2(n)
                    hi2(n + 1, 0)
                    square2(t, n + 1, 2)
                    roots2(n + 1, 1)
                    hi2(n + 1, 1)
                    outsquares2(n)
                    square2(t, n + 1, 3)
                    roots2(n + 1, 2)
                    hi2(n + 1, 2)
                    outroots2(n)
                    act.wait_ge(a2_dve.sem, a2_dve.at(n, "scale"))
                    roots2(n + 1, 3)
                    hi2(n + 1, 3)
                    values2(n + 1, 0)
                    values2(n + 1, 1)

                def pooled2(m):
                    act.wait_ge(up_dve.sem, up_dve.at(l, f"mean{m}"))
                    ac(mix2[:, 0, m], pr[:, :], ACT.Copy).then_inc(up_act.sem, 1)

                n = n0 + (HEADS2 - 1)
                exps2(n)
                pooled2(0)
                split2(n)
                pooled2(1)
                outsquares2(n)
                pooled2(2)
                pooled2(3)
                outroots2(n)
                for m in range(4, KT):
                    pooled2(m)
                with act.Fori(0, KT) as m:
                    n = l * KT + m
                    for s in range(2):
                        act.wait_ge(drained.sem, drained.at(t0 + U_GAB + m * 2 + s))
                        ac(mg2[:, s, :], mg2[:, s, :], ACT.Sigmoid).then_inc(m2_act.sem, 1)
                    act.wait_ge(m2_dve.sem, m2_dve.at(n, "sum"))
                    ac(flat(mix2)[:, 0, bass.ds(m * T, T)], mt2[:, :], ACT.Copy).then_inc(m2_act.sem, 1)
                tail_act(t0 + U_WO, l * 2 + 3, l * 16 + 24, l * FT + FT, lambda m: lay[:, bass.ds(m + PAR2["n2"].start, 1)],
                         lambda m: lay[:, bass.ds(m + PAR2_N, 1)])

            for t in range(TT):
                act.wait_ge(ou_pe.sem, ou_pe.at(t))
                ac(yout[:, t, :], psT[:, 0:2, :].rearrange("p b d -> p (b d)"), ACT.Copy).then_inc(ou_act.sem, 1)
                act.wait_ge(ou_act.sem, ou_act.at(t))
                act.dma_start(out[0, t * P:(t + 1) * P, :], yout[:, t, :]).then_inc(stored, 16)
            act.wait_ge(stored, TT * 16)


def kernel(**inputs):
    import concourse.bacc as bacc
    from concourse.bass_utils import run_bass_kernel_spmd

    nc = bacc.Bacc("TRN2", target_bir_lowering=False, num_devices=1)
    arrays = {name: np.ascontiguousarray(value) for name, value in inputs.items()}
    arrays["const"] = constants()
    args = {name: nc.dram_tensor(f"in_{name}", x.shape, F32, kind="ExternalInput").ap() for name, x in arrays.items()}
    out = nc.dram_tensor("result", (1, T, D), F32, kind="ExternalOutput").ap()
    build(nc, args, out)
    ran = run_bass_kernel_spmd(nc, [{f"in_{name}": x for name, x in arrays.items()}], core_ids=[0])
    return ran.results[0]["result"]
```

```python
from contextlib import ExitStack

import numpy as np

import concourse.bass as bass
from concourse import mybir

F32 = mybir.dt.float32
F32R = mybir.dt.float32r
ALU = mybir.AluOpType
ACT = mybir.ActivationFunctionType
AX = mybir.AxisListType

P = 128
T = 512
TT = T // P
D = 1024
KT = D // P
EPS = 1e-6
HEADS, HD, GROUPS = 16, 64, 4
NBLK, STRIDE, BLOCK = 31, 16, 32
HID = 256
DFF = 2816
FT = DFF // P
HEADS2, QK2, V2 = 4, 128, 256
LAYERS = 2
POOL_W = (2, 4, 8, 16)
NEG = -1e32

RAW, SPLIT = 4, 2

C_KV, C_CMP, C_Q, C_LRU, C_MIX, C_WO, C_GU, C_DN, C_B2 = np.cumsum(
    [0, 12, 8, 8, 32, 16, 8, 44, 24]).tolist()
L_QKV, L_U, L_GAB0, L_PW, L_GAB1, L_WO, L_GU, L_DN, C_LAYER = np.cumsum(
    [0, 24, 8, 2, 4, 14, 8, 44, 24]).tolist()
L_GAB = L_GAB1 - 2
C_ALL = C_B2 + LAYERS * C_LAYER
T_IN, T_KV, T_CMP, T_Q, T_LRU, T_MIX, T_WO, T_GU, T_DN, T_B2 = np.cumsum(
    [0, 8, 12, 4, 8, 32, 16, 8, 44, 8]).tolist()
U_QKV, U_U, U_GAB, U_WO, U_GU, U_DN, T_LAYER = np.cumsum(
    [0, 24, 8, 16, 8, 44, 8]).tolist()

CONST = {}
_at = 0
for _name, _n in (("ident", P), ("ones", P), ("blk", P), ("dist", T), ("cdist", TT * 32),
                  ("cmask", TT * 32), ("slope", HEADS), ("edge", 32), ("lam", 4),
                  ("cos", T), ("sin", T), ("chunk", T)):
    CONST[_name] = slice(_at, _at + _n)
    _at += _n
CONST_N = _at
CONST_1 = CONST["dist"].start
CONST_2 = CONST["cos"].start
CON2 = {n: slice(x.start - CONST_2, x.stop - CONST_2) for n, x in CONST.items() if x.start >= CONST_2}

PAR = {}
_at = 0
for _name, _n in (("n1", KT), ("n2", KT), ("cw", 4 * KT), ("cb", KT), ("ba", KT), ("bi", KT),
                  ("lam", KT), ("b1k", 2), ("b1v", 2), ("qg", 1), ("kg", 3), ("b2k", 1),
                  ("posk", 16), ("posv", 16)):
    PAR[_name] = slice(_at, _at + _n)
    _at += _n
PAR_N = _at
PAR2 = {}
_at = 0
for _name, _n in (("n1", KT), ("n2", KT), ("ps", KT), ("qg", 1), ("kg", 1), ("lam", 4),
                  ("sub", 2)):
    PAR2[_name] = slice(_at, _at + _n)
    _at += _n
PAR2_N = _at


def constants():
    c = np.zeros((P, CONST_N), np.float32)
    p = np.arange(P)[:, None]
    c[:, CONST["ident"]] = np.eye(P)
    c[:, CONST["ones"]] = 1.0
    c[:, CONST["blk"]] = (p // HD == np.arange(P)[None] // HD)
    rel = np.arange(T)[None] - (T - P) - p
    c[:, CONST["dist"]] = np.where(rel <= 0, rel, NEG)
    t = np.arange(TT)[None, :, None] * P + p[:, :, None]
    n = np.arange(32)[None, None, :]
    d = t - (n * STRIDE + BLOCK - 1)
    ok = (d >= 0) & (n < NBLK)
    c[:, CONST["cdist"]] = np.where(ok, -d, NEG).reshape(P, -1)
    c[:, CONST["cmask"]] = ok.reshape(P, -1)
    slope = np.power(2.0, -8.0 * np.arange(1, HEADS + 1) / HEADS).astype(np.float32)
    c[:, CONST["slope"]] = slope * np.float32(HD ** 0.5)
    rot = 32
    inv = np.float32(500000.0) ** (-np.arange(0, rot, 2, dtype=np.float32) / np.float32(rot))
    ang = np.arange(T, dtype=np.float32)[None] * inv[:, None]
    c[0:rot, CONST["cos"]] = np.concatenate([np.cos(ang)] * 2)
    c[0:rot, CONST["sin"]] = np.concatenate([-np.sin(ang), np.sin(ang)])
    c[:, CONST["chunk"]] = np.where(p // 64 >= (np.arange(T)[None] - (T - P)) // 64, 0.0, -3e38)
    at = CONST["edge"].start
    for w in POOL_W:
        c[:, at:at + w] = np.float32(w) / np.arange(1, w + 1, dtype=np.float32)
        at += w
    for l in range(LAYERS):
        li = 0.8 - 0.6 * np.exp(-0.3 * l)
        c[:, CONST["lam"].start + 2 * l] = li
        c[:, CONST["lam"].start + 2 * l + 1] = -0.5 * (1.0 - li)
    return c


class Steps:

    def __init__(self, sem, names):
        self.sem, self.names = sem, {x: i for i, x in enumerate(names)}

    def at(self, n, name=None):
        return n * len(self.names) + (len(self.names) if name is None else self.names[name] + 1)


P_AT = (0, 128, 384, 768)
PT_AT = (0, 512, 1024, 896)
A2_PE = [f"s{c}_{x}" for c in range(2) for x in range(4)] + ["t", "v", "sums"]
A2_DVE = ([f"max0_{x}" for x in range(4)] + ["max0"] + [f"max1_{x}" for x in range(4)] + ["max1", "rec", "neg"]
          + [f"scale{q}" for q in range(4)] + [f"a{q}" for q in range(4)] + ["lo", "newton", "scale",
                                                                            "out0", "out1"])
A2_ACT = [f"exp{c}_{q}" for c in range(2) for q in range(4)] + ["hi", "copy0", "square0", "copy1", "square1", "log", "root", "root2"]


def pool_steps():
    return [x for m in range(KT) for x in [f"y{m}_{k}" for k in range(m // 2 + 1)]
            + [f"edge{m}", f"mean{m}", f"lo{m}"]]


P_DMAS = 37
G_DMAS = 6


def build(nc, a, out):
    with ExitStack() as ctx:
        top = [-(-nc.sbuf_base // 32) * 32]
        names = [0]

        def place(shape, dt, offset):
            names[0] += 1
            return nc.alloc_sbuf_tensor_at(f"b{names[0]}", [P] + list(shape), dt, offset=offset)

        def keep(*shape, dt=F32):
            t = place(shape, dt, top[0])
            top[0] += -(-int(np.prod(shape)) * 4 // 32) * 32
            return t

        def sem(name):
            return ctx.enter_context(nc.semaphore(name))

        def steps(name, each):
            return Steps(sem(name), each)

        xT = keep(KT, T)
        wraw = keep(RAW, KT * P)
        wsp = keep(SPLIT, 2, KT, P, dt=F32R)
        xg = keep(2, KT, T, dt=F32R)
        con = keep(CONST_2)
        par = keep(PAR_N)
        par2 = keep((LAYERS + 1) * PAR2_N)
        lay = keep(PAR2_N + KT)
        c_rs = keep(T)
        acc_at = top[0]
        acc = keep(T)
        sq = keep(2, T)
        n_r0 = keep(T)
        n_r2 = keep(T)
        n_b = keep(T)
        small = keep(64)

        base = top[0]
        limit = nc.sbuf_usable_end

        class Plan:
            def __init__(self, at=0):
                self.at = at

            def __call__(self, *shape, dt=F32):
                t = place(shape, dt, base + self.at)
                self.at += -(-int(np.prod(shape)) * 4 // 32) * 32
                assert base + self.at <= limit, (base + self.at - limit)
                return t

        pl = Plan()
        attnT = pl(2, KT, T, dt=F32R)
        after_attn = pl.at
        kn = pl(2, 2, 2, T, dt=F32R)
        vtok = pl(2, 2, TT, GROUPS * HD, dt=F32R)
        kc = pl(2, P, dt=F32R)
        vc = pl(2, 2, P, dt=F32R)
        gates = pl(TT, 3 * HEADS)
        before_pair = pl.at
        qraw = pl(T)
        qz = pl(2, 2, T, dt=F32R)
        h_sq, h_t = sq[:, 0, :], sq[:, 1, :]
        bias = pl(2, T)
        cbias = pl(2, TT * 32)
        Pm = pl(2, 1280)
        Pc = pl(TT, 2, 32)
        PT = pl(2, 1280, dt=F32R)
        st = pl(64)
        cst = pl(64)
        PTc = [place([T], F32R, acc_at), pl(T, dt=F32R)]
        pl = Plan()
        kvraw = pl(12, T)
        gwraw = pl(KT, 48)
        gw = pl(2, KT, 48, dt=F32R)
        w2raw = pl(2, 2, P)
        hidc = pl(2, P)
        kcraw = pl(P)
        assert pl.at <= after_attn
        pl = Plan(before_pair)
        E = pl(2, 2, 5, 264, dt=F32R)
        Et = pl(2, T, dt=F32R)
        w2 = pl(2, 2, 2, P, dt=F32R)
        gsc = pl(T)
        hidr = pl(2, 2, 2, P, dt=F32R)
        bcol = pl(8)
        vcraw = pl(GROUPS, HD)
        vcraw2 = pl(GROUPS, HD)
        b2v = pl(HD)
        prow = pl(P)
        prow2 = pl(P)
        pl = Plan()
        xin = pl(TT, D)
        prow0 = pl(P)
        pl = Plan(after_attn)
        lruT = pl(2, KT, T, dt=F32R)
        lruw = pl(2, KT, HD)
        bd = pl(2, 2, P, dt=F32R)
        lx = pl(T + 3)
        xc = pl(T)
        xcr = pl(2, T, dt=F32R)
        gl = pl(T)
        lt = [pl(T) for _ in range(5)]
        mg = sq[:, 0, :]
        mixT = pl(KT, T)
        con2 = place([CONST_N - CONST_2], F32, (limit - (CONST_N - CONST_2) * 4) // 32 * 32)
        pl = Plan()
        aT2 = pl(KT, T)
        after_a2 = pl.at
        Pm2 = pl(2, 1280)
        PT2 = pl(2, 1280, dt=F32R)
        os2 = pl(2, T)
        st2 = pl(64)
        vtok2 = pl(2, TT, V2, dt=F32R)
        before_qk2 = pl.at
        qk2 = pl(4, 2, T, dt=F32R)
        raw2 = pl(6, T)
        rot = pl(T)
        norm2 = pl(T)
        pl = Plan(before_qk2)
        mix2 = pl(2, KT, T, dt=F32R)
        ur = pl(2, T + 16)
        ya, yb = pl(T + 16), pl(T + 16)
        pr = pl(T)
        mg2 = pl(2, T)
        mt2 = pl(T)
        pl = Plan(after_a2)
        poolT = pl(KT, T)
        pl = Plan()
        yout = pl(TT, D)
        pl = Plan()
        hid = pl(2, FT, T, dt=F32R)
        fg = pl(2, T)
        fu = pl(T)
        ft = pl(T)

        def pb(name, *shape):
            return ctx.enter_context(nc.psum_tensor(name, [P] + list(shape), F32))

        psA = pb("psA", 2, T)
        psS = pb("psS", 2, T)
        psT = pb("psT", 3, T)
        psO = pb("psO", T)

        ident, ones, blk = con[:, CONST["ident"]], con[:, CONST["ones"]], con[:, CONST["blk"]]

        wload = [sem(f"weights_loaded{s}") for s in range(RAW)]
        wsplit = steps("weights_split", ["hi", "lo"])
        used = steps("chunk_used", ["all"])
        drained = steps("tile_drained", ["all"])
        x_in = [sem(f"x_loaded{q}") for q in range(4)]
        c_in = sem("constants_loaded")
        c2_in = sem("constants2_loaded")
        p_in = sem("parameters_loaded")
        g1_in = sem("first_gain_loaded")
        g_in = sem("small_weights_loaded")
        lw_in = sem("lru_weights_loaded")
        su_pe = steps("setup_transposed", ["one"])
        su_dve = steps("setup_vector", ["one"])
        res_act = steps("residual_scalar", ["hi", "square"])
        res_dve = steps("residual_vector", ["lo", "sum"])
        nm_pe = steps("norm_sums", ["sum"])
        nm_act = steps("norm_scalar", ["log", "root", "root2"])
        nm_dve = steps("norm_vector", ["newton", "scale", "zero"])
        hn_act = steps("headnorm_scalar", ["square", "log", "root", "root2", "hi"])
        hn_pe = steps("headnorm_sums", ["sum"])
        hn_dve = steps("headnorm_vector", ["newton", "scale", "apply", "lo"])
        cg_dve = steps("small_split_vector", ["gw_hi", "gw_lo", "w2_hi", "w2_lo", "gates"])
        cg_pe = steps("gate_products", ["gates", "transposed"])
        cg_act = steps("gate_sigmoid", ["all"])
        e_act = steps("blocks_scalar", ["hi", "even", "odd"])
        e_dve = steps("blocks_vector", ["lo", "even", "odd"])
        ch_dve = steps("hidden_bias", ["bias"])
        ch_act = steps("hidden_scalar", ["gelu", "hi"])
        vt_pe = steps("values_transposed", ["all"])
        vt_act = steps("values_hi", ["all"])
        vt_dve = steps("values_lo", ["all"])
        kv_pe = steps("compressed_kv", ["all"])
        kv_dve = steps("compressed_vector", ["k", "v", "v_hi0", "v_hi1", "v_lo0", "v_moved", "v_lo1"])
        pad_dve = steps("padding_zeroed", ["vc", "qz0", "ptc0", "qz1", "ptc1"])
        qs_act = steps("query_squares", ["square"])
        qr_act = steps("query_roots", ["log", "root", "root2"])
        qi_act = steps("query_hi", ["head0", "head1"])
        q_pe = steps("query_sums", ["sum"])
        q_dve = steps("query_vector", ["newton", "scale", "apply"])
        ql_pool = steps("query_lo", ["lo0", "lo1"])
        b_pool = steps("biases", ["head0", "compressed0", "compressed1", "head1"])
        us_pe = steps("unit_scores", ["s0", "s1", "s2", "s3"])
        um_dve = steps("unit_maxima", ["max0", "max1", "max2", "max3", "neg"])
        ue_act = steps("unit_exps", ["e0", "e1", "e2", "e3"])
        ug_dve = steps("unit_gates", ["rec", "gate"])
        up_dve1 = steps("unit_probabilities", ["k0", "k1", "k2", "k3"])
        ut_pe = steps("unit_transposed", ["all"])
        uh_act = steps("unit_hi", ["all"])
        ul_dve = steps("unit_lo", ["all"])
        uv_pe = steps("unit_values", ["all"])
        cs_pe = steps("compressed_scores", ["all"])
        cm_dve = steps("compressed_maxima", ["add", "max", "sub"])
        ce_act = steps("compressed_exps", ["exp"])
        cp_dve = steps("compressed_probabilities", ["mask", "sum", "guard", "rec", "gate", "scale"])
        ct_pe = steps("compressed_transposed", ["all"])
        ch_act2 = steps("compressed_hi", ["all"])
        cl_dve = steps("compressed_lo", ["all"])
        cv_pe = steps("head_output", ["all"])
        oh_act = steps("head_output_hi", ["all"])
        ol_dve = steps("head_output_lo", ["all"])
        sp_dve = steps("softplus_vector", ["abs"])
        sp_act = steps("softplus_scalar", ["exp"])
        eps_in = steps("epsilon_set", ["all"])
        lw_dve = steps("lru_zeroed", ["diagonal", "pad"])
        lr_pe = steps("lru_products", ["a", "i"])
        lr_dve = steps("lru_vector", ["tap0", "tap1", "tap2", "tap3", "lo", "w0", "w1", "one", "rec", "ratio",
                                      "ix", "b", "scan", "out", "out_lo"])
        lr_act = steps("lru_scalar", ["hi", "w0", "w1", "gelu", "gate", "r", "i", "tanh", "a", "root", "out_hi"])
        mx_act = steps("mix_scalar", ["gate", "hi"])
        mx_dve = steps("mix_vector", ["sum", "lo"])
        ff_act = steps("ffn_scalar", ["silu", "hi"])
        ff_dve = steps("ffn_vector", ["product", "lo"])
        ly_dve = steps("layer_vector", ["copy", "gains", "sub", "products", "diff", "lambda"])
        ly_pe = steps("layer_sums", ["sum"])
        ly_act = steps("layer_scalar", ["exp"])
        h2_act = steps("headnorm2_squares", ["square", "gain"])
        h2_root = steps("headnorm2_roots", ["log", "root", "root2"])
        h2_hi = steps("headnorm2_hi", ["hi"])
        h2_pe = steps("headnorm2_sums", ["sum"])
        h2_rot = steps("headnorm2_rotated", ["swap", "sin", "cos", "sum"])
        h2_dve = steps("headnorm2_vector", ["newton", "scale", "apply"])
        h2_lo = steps("headnorm2_lo", ["lo"])
        v2_raw = steps("values2_drained", ["all"])
        v2_pe = steps("values2_transposed", ["all"])
        v2_act = steps("values2_hi", ["all"])
        v2_dve = steps("values2_lo", ["all"])
        a2_pe = steps("attention2_products", A2_PE)
        a2_dve = steps("attention2_vector", A2_DVE)
        a2_act = steps("attention2_scalar", A2_ACT)
        up_dve = steps("pool_vector", ["pad0", "pad1"] + pool_steps())
        up_act = steps("pool_hi", ["hi"])
        pw_dve = steps("pools_drained", ["all"])
        m2_act = steps("mix2_scalar", ["ga", "gb", "hi"])
        m2_dve = steps("mix2_vector", ["pool", "attn", "sum", "lo"])
        ou_pe = steps("output_transposed", ["all"])
        ou_act = steps("output_copied", ["all"])
        stored = sem("stored")

        def hi_f(x):
            return x.bitcast(F32)

        settles = sem("waits_settled")

        def settled(engine):
            engine.sem_inc(settles, 1)

        block = ctx.enter_context(nc.Block())

        def col_tile(w, kts, m):
            v = w.rearrange("(k p) n -> p k n", p=P)
            h = kts // 2
            return [(0, h, v[:, 0:h, bass.ds(m, P)]), (h, kts, v[:, h:kts, bass.ds(m, P)])]

        w_in, w_in2 = a["w_in"][0], a["w_in_2"]

        def tail(stage, c0, wo, gate, up, down):
            stage(c0, 8, lambda i, s: wo(i * 4 * P + s * P))
            stage(c0 + 8, 2 * FT, lambda i, s: (up if s % 2 else gate)(i * 2 * P + (s // 2) * P))
            stage(c0 + 8 + 2 * FT, 24, lambda i, s: down(s % 3 * KT, i * 4 * P + (s // 3) * P), per=12)

        @block.sync
        def _(sp):
            def load(c, s, parts, dst=None, settle=False):
                if not isinstance(c, int) or c >= RAW:
                    sp.wait_ge(wsplit.sem, wsplit.at(c - RAW))
                    if settle:
                        settled(sp)
                slot = wraw[:, s, :].rearrange("p (k n) -> p k n", n=P)
                for lo, hi, src in parts:
                    sp.dma_start(slot[:, lo:hi, :] if dst is None else dst(slot, lo), src).then_inc(wload[s], 16)

            def stage(c0, n, parts, per=RAW, dst=None):
                with sp.Fori(0, n // per) as i:
                    for s in range(per):
                        load(c0 + i * per + s, s % RAW, parts(i, s), dst)

            for q in range(4):
                cols = slice(q * D // 4, (q + 1) * D // 4)
                sp.dma_start(xin[:, :, cols], a["x"][0, :, cols].rearrange("(t p) d -> p t d", p=P)).then_inc(x_in[q], 16)
            wc = w_in.rearrange("(k p) n -> p k n", p=P)

            def halves(col, apart):
                return [(b, 0, wc[:, :, bass.ds(col + b * apart, HD)]) for b in range(2)]

            def to_half(slot, b):
                return slot[:, :, b * HD:(b + 1) * HD]

            for s in range(RAW):
                load(s, s, halves(D + s // 2 * GROUPS * HD + s % 2 * HD, 2 * HD), to_half)
            sp.dma_start(con[:, CONST_1:], a["const"][:, CONST_1:CONST_2]).then_inc(p_in, 16)
            done = [0]

            def rows(dst, r0, src, cols=slice(0, P)):
                n = src.shape[0]
                sp.dma_start(dst[r0:r0 + n, cols], src).then_inc(p_in, 16)
                done[0] += 1

            def vec(name, l=0):
                return a[name][l].rearrange("(r p) -> r p", p=P)

            for key, name in (("n1", "norm1_g"), ("n2", "norm2_g"), ("cb", "conv_b"), ("ba", "lru_ba"), ("bi", "lru_bi"),
                              ("lam", "lru_lambda"), ("b1k", "cmp_b1_k"), ("b1v", "cmp_b1_v")):
                rows(prow, PAR[key].start, vec(name))
            rows(prow, PAR["cw"].start, a["conv_w"][0].rearrange("k o (m p) -> (k o m) p", p=P))
            for half in range(2):
                cols = slice(half * HD, (half + 1) * HD)
                rows(prow, PAR["qg"].start, a["q_norm_g"], cols)
                rows(prow, PAR["kg"].start, a["k_norm_g"][0], cols)
                rows(prow, PAR["b2k"].start, a["cmp_b2_k"], cols)
            for key, name in (("posk", "cmp_pos_k"), ("posv", "cmp_pos_v")):
                rows(prow, PAR[key].start, a[name][0].rearrange("(j l) d -> j (l d)", l=2))
            for l in range(LAYERS):
                for key, name in (("n1", "norm1_g_2"), ("n2", "norm2_g_2"), ("ps", "pool_scale_2"), ("qg", "q_norm_g_2"),
                                  ("kg", "k_norm_g_2"), ("sub", "subln_g_2")):
                    rows(prow2, l * PAR2_N + PAR2[key].start, vec(name, l))
                for j, name in enumerate(("lam_q1_2", "lam_k1_2", "lam_q2_2", "lam_k2_2")):
                    rows(prow2, l * PAR2_N + PAR2["lam"].start + j, vec(name, l))
            assert done[0] == P_DMAS, done
            gd = 0
            for dst, src in ((gwraw[:, :, :], w_in.rearrange("(k p) n -> p k n", p=P)[:, :, 2560:2608]),
                             (w2raw[:, 0, :, 0:HD], a["cmp_w2_k"][0].rearrange("(k p) d -> p k d", p=P)),
                             (w2raw[:, 0, :, HD:P], a["cmp_w2_k"][0].rearrange("(k p) d -> p k d", p=P)),
                             (w2raw[:, 1, :, 0:HD], a["cmp_w2_v"][0].rearrange("(k p) d -> p k d", p=P)),
                             (w2raw[:, 1, :, HD:P], a["cmp_w2_v"][0].rearrange("(k p) d -> p k d", p=P)),
                             (b2v[0:32, :], a["cmp_b2_v"][0].partition_broadcast(32))):
                sp.dma_start(dst, src).then_inc(g_in, 16)
                gd += 1
            assert gd == G_DMAS

            stage(C_KV + 4, 8, lambda i, s: halves(i * (2 * GROUPS * HD) + D + (2 + s // 2) * GROUPS * HD + s % 2 * HD, 2 * HD),
                  dst=to_half)
            for kv, name in enumerate(("cmp_w1_k", "cmp_w1_v")):
                w1 = a[name][0].rearrange("l d f -> (l d) f")
                for s in range(4):
                    half = w1[(s % 2) * D:(s % 2 + 1) * D, :]
                    load(C_CMP + 4 * kv + s, s, col_tile(half, KT, (s // 2) * P))
            stage(C_Q, 8, lambda i, s: halves(i * (4 * HD) + s * HD, D // 2), dst=to_half)
            o3 = 2608
            woa = a["w_o_attn"][0].rearrange("(b k d) n -> b d k n", b=2, d=HD)
            o5 = o3 + 2 * D
            with sp.Fori(0, KT) as i:
                for s in range(3):
                    load(C_LRU + i * 4 + s, s, col_tile(w_in, KT, i * P + o3 + s * D))
                load(C_LRU + i * 4 + 3, 3, [(b, 0, woa[b, :, :, bass.ds(i * P, P)]) for b in range(2)],
                     lambda slot, b: slot[b * HD:(b + 1) * HD, :, :], settle=True)
            with sp.Fori(0, KT // 2) as i:
                for s in range(4):
                    m = i * 2 * P + (s // 2) * P
                    load(C_MIX + i * 4 + s, s, col_tile(a["w_o_lru"][0], KT, m) if s % 2 else col_tile(w_in, KT, m + (o5 + D)), settle=s == 1)

            def down(r, m):
                k = min(KT, FT - r)
                return col_tile(a["w_down"][0][r * P:(r + k) * P, :], k, m)

            tail(stage, C_WO, lambda m: col_tile(a["w_out"][0], KT, m), lambda m: col_tile(a["w_gate"][0], KT, m),
                 lambda m: col_tile(a["w_up"][0], KT, m), down)

            def stacked(name):
                return a[name].rearrange("l (k p) n -> p (l k) n", p=P)

            wi2, wo2, wf2, wd2 = (stacked(x) for x in ("w_in_2", "w_out_2", "w_ffn_in_2", "w_ffn_out_2"))
            pw2 = a["pool_w_2"].rearrange("l g (k p) (m n) -> p (l g k) m n", p=P, n=P)
            with sp.Fori(0, LAYERS) as l:
                def col2(w, col, k0=0, kts=KT, each=KT):
                    h = kts // 2
                    return [(b, e, w[:, bass.ds(l * each + (k0 + b), e - b), bass.ds(col, P)]) for b, e in ((0, h), (h, kts))]

                c0 = l * C_LAYER + C_B2
                with sp.Fori(0, 2) as i:
                    for s in range(12):
                        x = s % 6
                        load(c0 + i * 12 + s, s % RAW,
                             col2(wi2, i * (2 * V2) + (D * (1 + x // 2) + s // 6 * V2 + x % 2 * P)))
                stage(c0 + L_U, 8, lambda i, s: col2(wi2, i * 4 * P + s * P))
                def gates(m, s):
                    return col2(wi2, m * P + (D * (4 + s % 2) + s // 2 * P))

                for s in range(2):
                    load(c0 + (L_GAB0 + s), s, gates(0, s), settle=s == 0)
                for g in range(4):
                    load(c0 + (L_PW + g), (L_PW + g) % RAW, [(2 * k, 2 * k + 2, pw2[:, bass.ds(l * 8 + (g * 2 + k), 1), :, :].squeeze(1)) for k in range(2)], settle=True)
                for s in range(2):
                    load(c0 + (L_GAB1 + s), (L_GAB1 + s) % RAW, gates(1, s), settle=s == 0)
                stage(c0 + (L_GAB + 4), 12, lambda i, s: gates(i * 2 + 2, s))
                tail(stage, c0 + L_WO, lambda m: col2(wo2, m), lambda m: col2(wf2, m), lambda m: col2(wf2, m + DFF),
                     lambda r, m: col2(wd2, m, r, min(KT, FT - r), FT))

        @block.gpsimd
        def _(pool):
            def split(c, rnd, s):
                pool.wait_ge(wload[s], rnd * 32 + 32)
                if not isinstance(c, int) or c >= SPLIT:
                    pool.wait_ge(used.sem, used.at(c - SPLIT))
                if not isinstance(c, int):
                    settled(pool)
                w = wsp[:, s % SPLIT].rearrange("p h k n -> p h (k n)")
                nc.gpsimd.tensor_tensor(w[:, 0], wraw[:, s], ones[:, 0:1].broadcast_to([P, KT * P]), ALU.mult).then_inc(wsplit.sem, 1)
                pool.wait_ge(wsplit.sem, wsplit.at(c, "hi"))
                nc.gpsimd.tensor_tensor(w[:, 1], wraw[:, s], hi_f(w[:, 0]), ALU.subtract).then_inc(wsplit.sem, 1)

            pool.wait_ge(c_in, 16)
            for s in range(RAW):
                split(s, 0, s)
            with pool.Fori(1, C_Q // RAW) as i:
                for s in range(RAW):
                    split(i * RAW + s, i, s)

            def bias_of(n, hd, c=False):
                h = CONST["slope"].start + n + 8 * hd
                dst, name = (cbias, "cdist") if c else (bias, "dist")
                dist = con[:, CONST[name]]
                nc.gpsimd.tensor_tensor(dst[:, hd, :], dist, con[:, h:h + 1].broadcast_to(list(dist.shape)), ALU.mult).then_inc(b_pool.sem, 1)

            def query_lo(n):
                pool.wait_ge(b_pool.sem, b_pool.at(n, "head1" if n == 0 else "compressed1"))
                for hd in range(2):
                    rows = slice(hd * HD, (hd + 1) * HD)
                    pool.wait_ge(qi_act.sem, qi_act.at(n, f"head{hd}"))
                    nc.gpsimd.tensor_tensor(qz[rows, hd, 1, :], h_t[rows, :], hi_f(qz[rows, hd, 0, :]), ALU.subtract).then_inc(ql_pool.sem, 1)
                    pool.wait_ge(ql_pool.sem, ql_pool.at(n, f"lo{hd}"))

            def split_query(n):
                split(C_Q + n, (C_Q + n) // RAW, n % RAW)

            split_query(0)
            split_query(1)
            pool.wait_ge(pad_dve.sem, pad_dve.at(0, "vc"))
            bias_of(0, 0)
            bias_of(0, 0, True)
            bias_of(0, 1, True)
            bias_of(0, 1)
            query_lo(0)
            split_query(2)
            for n in range(8):
                if n < 7:
                    pool.wait_ge(um_dve.sem, um_dve.at(4 * n + 1, "max3"))
                    bias_of(n + 1, 0)
                    pool.wait_ge(cm_dve.sem, cm_dve.at(n, "add"))
                    bias_of(n + 1, 0, True)
                    bias_of(n + 1, 1, True)
                    query_lo(n + 1)
                    pool.wait_ge(um_dve.sem, um_dve.at(4 * n + 3, "max3"))
                    bias_of(n + 1, 1)
                if n < 5:
                    split_query(n + 3)
            with pool.Fori(C_LRU // RAW, C_ALL // RAW) as i:
                for s in range(RAW):
                    split(i * RAW + s, i, s)

        def tail_pe(pe, chunk, free, proj, norm, split_by, c0, t0, src, ready, k, n, ff):
            with pe.Fori(0, 4) as i:
                for s in range(2):
                    proj(c0 + i * 2 + s, t0 + i * 2 + s, s, lambda h, kt: src[:, h, kt, :], None if s else ready)
            proj(c0 + 8, t0 + 8, 0, ready=split_by(res_dve, n))
            norm(k, n + 7)
            proj(c0 + 9, t0 + 9, 1)
            with pe.Fori(1, FT) as i:
                for s in range(2):
                    proj(c0 + 8 + i * 2 + s, t0 + 8 + i * 2 + s, s)
            c1, t1 = c0 + 8 + 2 * FT, t0 + 8 + 2 * FT
            with pe.Fori(0, 4) as i:
                for m in range(2):
                    free(t1 + i * 2 + m)
                    for q in range(3):
                        s = 3 * m + q
                        rows = min(KT, FT - q * KT)
                        pe.wait_ge(ff_dve.sem, ff_dve.at(ff + q * KT + rows - 1))
                        chunk(c1 + i * 6 + s, s, psA[:, m, :], lambda h, kt: hid[:, h, q * KT + kt, :], rows, q == 0, q == 2)

        def attention_pe(pe, free, three, compressed, compressed_norm):
            mm = nc.tensor.matmul

            def query(n, kts):
                if kts[0] == 0:
                    if n < 2:
                        pe.wait_ge(drained.sem, drained.at(T_CMP + n))
                    else:
                        pe.wait_ge(cm_dve.sem, cm_dve.at(n - 2, "add"))
                    pe.wait_ge(wsplit.sem, wsplit.at(C_Q + n))
                for kt in kts:
                    i = three(psA[:, n % 2, :], lambda h: wsp[:, n % 2, h, kt, :], lambda h: xg[:, h, kt, :], kt == 0, kt == KT - 1, True)
                if kts[-1] == KT - 1:
                    i.then_inc(used.sem, 1)

            def query_sums(n):
                pe.wait_ge(qs_act.sem, qs_act.at(n))
                mm(psA[:, n % 2, :], blk, h_sq[:, :], start=True, stop=True).then_inc(q_pe.sem, 1)

            def scores(U, xs):
                n, hd, br = U // 4, U % 4 // 2, U % 2
                if U % 4 == 0 and 0 in xs:
                    pe.wait_ge(ql_pool.sem, ql_pool.at(n))
                for x in xs:
                    qt = TT - 1 - x
                    if x >= 2:
                        pe.wait_ge(um_dve.sem, um_dve.at(U, f"max{x - 2}"))
                    elif U:
                        pe.wait_ge(um_dve.sem, um_dve.at(U - 1, f"max{x + 2}"))
                    w = P * (qt + 1)
                    three(psS[:, x % 2, 0:w], lambda h: qz[:, hd, h, qt * P:(qt + 1) * P],
                          lambda h: kn[:, br, n // 4, h, 0:w], True, True).then_inc(us_pe.sem, 1)

            def transposes(U):
                if U:
                    pe.wait_ge(ul_dve.sem, ul_dve.at(U - 1))
                for qt in range(TT):
                    pe.wait_ge(up_dve1.sem, up_dve1.at(U, f"k{qt}"))
                    for kt in range(qt + 1):
                        to = PT_AT[kt] + (qt - kt) * P
                        i = nc.tensor.transpose(psT[:, to // T, to % T:to % T + P],
                                                Pm[:, U % 2, P_AT[qt] + kt * P:P_AT[qt] + (kt + 1) * P], ident)
                i.then_inc(ut_pe.sem, 1)

            def values(U):
                n, hd, br = U // 4, U % 4 // 2, U % 2
                if br == 0 and U:
                    pe.wait_ge(ol_dve.sem, ol_dve.at(U // 2 - 1))
                pe.wait_ge(ul_dve.sem, ul_dve.at(U))
                for kt in range(TT):
                    w = T - kt * P
                    i = three(psO[:, kt * P:T], lambda h: vtok[:, br, h, kt, n // 4 * P:(n // 4 + 1) * P],
                              lambda h: PT[:, h, PT_AT[kt]:PT_AT[kt] + w], br == 0 and kt == 0, False, True)
                i.then_inc(uv_pe.sem, 1)

            def c_scores(n):
                for hd in range(2):
                    for qt in range(TT):
                        at = hd * P + qt * 32
                        i = three(psA[:, n % 2, at:at + 32], lambda h: qz[:, hd, h, qt * P:(qt + 1) * P],
                                  lambda h: kc[:, h, 32 * (2 * (n // 4) + hd):32 * (2 * (n // 4) + hd) + 32], True, True)
                i.then_inc(cs_pe.sem, 1)

            def c_transposes(n):
                pe.wait_ge(cp_dve.sem, cp_dve.at(n))
                if n < 7:
                    pe.wait_ge(q_dve.sem, q_dve.at(n + 1, "newton"))
                for qt in range(TT):
                    i = nc.tensor.transpose(psA[0:HD, (n + 1) % 2, qt * P:(qt + 1) * P],
                                            Pc[:, qt, :, :].rearrange("p h n -> p (h n)"), ident)
                i.then_inc(ct_pe.sem, 1)

            def c_values(n, hd):
                pe.wait_ge(cl_dve.sem, cl_dve.at(n))
                three(psO[:, :], lambda h: vc[:, h, n // 4, :], lambda h: PTc[h][:, :], False, True, True).then_inc(cv_pe.sem, 1)

            x4 = range(4)
            query(0, range(KT))
            query_sums(0)
            compressed()
            query(1, range(KT))
            pe.wait_ge(kv_dve.sem, kv_dve.at(0, "v"))
            scores(0, (0, 1))
            compressed_norm()
            scores(0, (2, 3))
            scores(1, x4)
            query_sums(1)
            pe.wait_ge(hn_dve.sem, hn_dve.at(4))
            c_scores(0)

            def unit(U, *beside):
                if U + 2 < 32:
                    scores(U + 2, (0, 1))
                transposes(U)
                for f, *args in beside[:1]:
                    f(*args)
                if U + 2 < 32:
                    scores(U + 2, (2, 3))
                for f, *args in beside[1:]:
                    f(*args)
                values(U)

            for n in range(8):
                U, last, ahead = 4 * n, n == 7, n < 6
                unit(U, *[(query, n + 2, range(4))] * ahead)
                unit(U + 1, (c_transposes, n), *[(query, n + 2, range(4, 8))] * ahead)
                c_values(n, 0)
                unit(U + 2, *[(c_scores, n + 1)] * (not last))
                unit(U + 3, *[(query_sums, n + 2)] * ahead)
                c_values(n, 1)

        @block.tensor
        def _(pe):
            mm = nc.tensor.matmul

            def chunk(c, s, dst, rhs, kts=KT, first=True, last=True, ready=None):
                pe.wait_ge(wsplit.sem, wsplit.at(c))
                w = wsp[:, s % SPLIT]
                for kt in range(kts):
                    if ready is not None:
                        ready(kt)
                    for n, (wh, xh) in enumerate(((0, 0), (0, 1), (1, 0))):
                        i = mm(dst, w[:, wh, kt, :], rhs(xh, kt), start=first and kt == 0 and n == 0,
                               stop=last and kt == kts - 1 and n == 2)
                i.then_inc(used.sem, 1)

            def free(t):
                pe.wait_ge(drained.sem, drained.at(t - 2))

            def rhs_x(h, kt):
                return xg[:, h, kt, :]

            def proj(c, t, s, rhs=rhs_x, ready=None):
                free(t)
                chunk(c, s, psA[:, s % 2, :], rhs, ready=ready)

            def split_by(of, n):
                def ready(kt):
                    if kt in (0, KT - 1):
                        pe.wait_ge(of.sem, of.at(n + max(kt, KT - 2)))
                return ready

            def three(dst, lh, rh, start=False, stop=False, skip=False):
                for n, (x, y) in enumerate(((0, 0), (0, 1), (1, 0))):
                    i = mm(dst, lh(x), rh(y), start=start and n == 0, stop=stop and n == 2, skip_group_check=skip)
                return i

            def norm(k, n):
                pe.wait_ge(res_dve.sem, res_dve.at(n))
                mm(psO[:, :], ones, acc[:, :], start=True, stop=True).then_inc(nm_pe.sem, 1)

            def headnorm(n, sums, w=T):
                pe.wait_ge(hn_act.sem, hn_act.at(n, "square"))
                mm(psO[:, 0:w], sums, h_sq[:, 0:w], start=True, stop=True).then_inc(hn_pe.sem, 1)

            def headnorm2(n, x):
                if x:
                    pe.wait_ge(h2_dve.sem, h2_dve.at(n * 4 + (x - 1), "newton"))
                pe.wait_ge(h2_act.sem, h2_act.at(n * 4 + x, "square"))
                mm(psO[:, :], ones, sq[:, x % 2, :], start=True, stop=True).then_inc(h2_pe.sem, 1)

            def values2(n, x):
                pe.wait_ge(v2_raw.sem, v2_raw.at(n * 2 + x))
                for t in range(TT):
                    i = nc.tensor.transpose(psT[:, x, t * P:(t + 1) * P], raw2[:, 4 + x, t * P:(t + 1) * P], ident)
                i.then_inc(v2_pe.sem, 1)

            def scores2(n):
                pe.wait_ge(h2_lo.sem, h2_lo.at(n * 4 + 3))
                for c in range(2):
                    for x, qt in enumerate((3, 2, 1, 0)):
                        if c or x >= 2:
                            pe.wait_ge(a2_dve.sem, a2_dve.at(n, f"max{c}_{x - 2}" if x >= 2 else f"max0_{x + 2}"))
                        three(psS[:, x % 2, 0:P * (qt + 1)], lambda h: qk2[:, c, h, qt * P:(qt + 1) * P],
                              lambda h: qk2[:, 2 + c, h, 0:P * (qt + 1)], True, True).then_inc(a2_pe.sem, 1)

            def transposes2(n):
                pe.wait_ge(v2_dve.sem, v2_dve.at(n * 2 + 1))
                for qt in range(TT):
                    pe.wait_ge(a2_dve.sem, a2_dve.at(n, f"a{qt}"))
                    for kt in range(qt + 1):
                        to = PT_AT[kt] + (qt - kt) * P
                        i = nc.tensor.transpose(psT[:, to // T, to % T:to % T + P],
                                                Pm2[:, 0, P_AT[qt] + kt * P:P_AT[qt] + (kt + 1) * P], ident)
                i.then_inc(a2_pe.sem, 1)

            def products2(n):
                pe.wait_ge(a2_dve.sem, a2_dve.at(n, "lo"))
                for d in range(2):
                    for kt in range(TT):
                        w = T - kt * P
                        i = three(psS[:, d, kt * P:T], lambda h: vtok2[:, h, kt, d * P:(d + 1) * P],
                                  lambda h: PT2[:, h, PT_AT[kt]:PT_AT[kt] + w], kt == 0, kt == TT - 1, True)
                i.then_inc(a2_pe.sem, 1)

            def sums2(n):
                pe.wait_ge(a2_act.sem, a2_act.at(n, "square1"))
                mm(psT[:, 2, :], ones, Pm2[:, 1, 0:T], start=True, stop=False)
                mm(psT[:, 2, :], ones, Pm2[:, 1, T:2 * T], start=False, stop=True).then_inc(a2_pe.sem, 1)

            pe.wait_ge(c_in, 16)
            pe.wait_ge(g1_in, 16)
            nc.tensor.transpose(psT[:, 0, 0:KT], prow0[0:KT, :], con[0:KT, 0:KT]).then_inc(su_pe.sem, 1)
            for f in range(KT):
                if f % 2 == 0:
                    pe.wait_ge(x_in[f // 2], 16)
                if f >= 2:
                    free(f)
                for t in range(TT):
                    i = nc.tensor.transpose(psA[:, f % 2, t * P:(t + 1) * P], xin[:, t, f * P:(f + 1) * P], ident)
                i.then_inc(su_pe.sem, 1)
            for s in range(4):
                proj(C_KV + s, T_KV + s, s, ready=None if s else lambda kt: pe.wait_ge(res_dve.sem, res_dve.at(kt)))
                if s == 0:
                    norm(0, 7)
            with pe.Fori(1, 3) as i:
                for s in range(4):
                    proj(C_KV + i * 4 + s, T_KV + i * 4 + s, s)
            pe.wait_ge(p_in, P_DMAS * 16 + 16)
            nc.tensor.transpose(psS[:, 1, 0:PAR_N], prow[0:PAR_N, :], con[0:PAR_N, 0:PAR_N]).then_inc(su_pe.sem, 1)
            nc.tensor.transpose(psS[:, 1, 256:256 + 2 * PAR2_N], prow2[0:2 * PAR2_N, :],
                                con[0:2 * PAR2_N, 0:2 * PAR2_N]).then_inc(su_pe.sem, 1)
            pe.wait_ge(cg_dve.sem, cg_dve.at(0, "gw_lo"))
            for kt in range(KT):
                i = three(psS[0:48, 0, :], lambda h: gw[:, h, kt, :], lambda h: xg[:, h, kt, :], kt == 0, kt == KT - 1)
            i.then_inc(cg_pe.sem, 1)

            def v_transposes(n):
                src = kvraw[:, (6, 7, 10, 11)[n], :]
                for t in range(TT):
                    i = nc.tensor.transpose(psT[:, n % 3, t * P:(t + 1) * P], src[:, t * P:(t + 1) * P], ident)
                i.then_inc(vt_pe.sem, 1)

            pe.wait_ge(drained.sem, drained.at(T_KV + 11))
            for n in range(3):
                v_transposes(n)

            def gate_transposes():
                for t in range(TT):
                    i = nc.tensor.transpose(psT[:, 1, 48 * t:48 * t + 48], gsc[0:48, t * P:(t + 1) * P], con[0:48, 0:48])
                i.then_inc(cg_pe.sem, 1)

            pe.wait_ge(nm_dve.sem, nm_dve.at(0, "newton"))
            headnorm(0, blk)
            pe.wait_ge(e_act.sem, e_act.at(3))
            pe.wait_ge(e_dve.sem, e_dve.at(3))
            pe.wait_ge(cg_dve.sem, cg_dve.at(0, "gates"))
            for kv, bank in enumerate((psA, psS)):
                for s in range(4):
                    m, half = s // 2, s % 2
                    if half == 0 and kv == 0:
                        free(T_CMP + m)
                    chunk(C_CMP + 4 * kv + s, s, bank[:, m, 0:160].rearrange("p (g n) -> p g n", n=32),
                          lambda h, kt: E[:, kv, h, :, half * KT + kt:half * KT + kt + 249:8],
                          first=half == 0, last=half == 1)
                    n = 2 * kv + (s + 1) // 2
                    if half == 1 and n < 4:
                        pe.wait_ge(hn_dve.sem, hn_dve.at(n - 1, "newton"))
                        headnorm(n, blk)
                    if half == 1 and n == 1:
                        pe.wait_ge(vt_dve.sem, vt_dve.at(1))
                        v_transposes(3)
                        gate_transposes()

            def compressed():
                pe.wait_ge(drained.sem, drained.at(T_CMP + 3))
                for kt in range(2):
                    i = three(psS[:, 0, 0:P], lambda h: w2[:, 0, h, kt, :], lambda h: hidr[:, 0, h, kt, :], kt == 0, kt == 1)
                for g in range(GROUPS):
                    for kt in range(2):
                        i = three(psS[0:32, 1, 256 + g * HD:256 + (g + 1) * HD],
                                  lambda h: hidr[:, 1, h, kt, 32 * g:32 * g + 32],
                                  lambda h: w2[:, 1, h, kt, 0:HD], kt == 0, kt == 1)
                i.then_inc(kv_pe.sem, 1)

            def compressed_norm():
                pe.wait_ge(hn_dve.sem, hn_dve.at(3, "newton"))
                headnorm(4, blk, P)

            attention_pe(pe, free, three, compressed, compressed_norm)
            with pe.Fori(0, KT) as m:
                c, t = C_LRU + m * 4, T_LRU + m * 4
                for s in range(3):
                    proj(c + s, t + s, s)
                pe.wait_ge(lr_dve.sem, lr_dve.at(m, "w1"))
                for w in range(2):
                    three(psS[:, w, :], lambda h: bd[:, h, w, :], lambda h: xcr[:, h, :], True, True).then_inc(lr_pe.sem, 1)
                proj(c + 3, t + 3, 3, lambda h, kt: attnT[:, h, kt, :])
            with pe.Fori(0, KT // 2) as i:
                for s in range(4):
                    src = lruT if s % 2 else xg
                    if s == 1:
                        pe.wait_ge(lr_dve.sem, lr_dve.at(7))
                    proj(C_MIX + i * 4 + s, T_MIX + i * 4 + s, s, lambda h, kt: src[:, h, kt, :])
            tail_pe(pe, chunk, free, proj, norm, split_by, C_WO, T_WO, attnT, split_by(mx_dve, 0), 1, 8, 0)

            with pe.Fori(0, LAYERS) as l:
                c0, t0 = l * C_LAYER + C_B2, l * T_LAYER + T_B2
                n0 = l * HEADS2
                for x in range(6):
                    proj(c0 + x, t0 + x, x, ready=None if x else split_by(res_dve, l * 16 + 16))
                    if x == 0:
                        norm(l * 2 + 2, l * 16 + 23)
                        pe.wait_ge(ly_dve.sem, ly_dve.at(l, "products"))
                        mm(psT[:, 2, 0:2], ones, small[:, 32:34], start=True, stop=True).then_inc(ly_pe.sem, 1)
                    if 1 <= x <= 4:
                        headnorm2(n0, x - 1)
                values2(n0, 0)
                values2(n0, 1)
                with pe.Fori(0, HEADS2 - 1) as h:
                    n = l * HEADS2 + h
                    c, t = c0 + h * 6 + 6, t0 + h * 6 + 6
                    proj(c, t, 0)
                    scores2(n)
                    proj(c + 1, t + 1, 1)
                    headnorm2(n + 1, 0)
                    proj(c + 2, t + 2, 2)
                    transposes2(n)
                    headnorm2(n + 1, 1)
                    proj(c + 3, t + 3, 3)
                    products2(n)
                    headnorm2(n + 1, 2)
                    proj(c + 4, t + 4, 4)
                    sums2(n)
                    headnorm2(n + 1, 3)
                    proj(c + 5, t + 5, 5)
                    values2(n + 1, 0)
                    values2(n + 1, 1)
                n, c, t = n0 + (HEADS2 - 1), c0 + L_U, t0 + U_U
                proj(c, t, 0)
                scores2(n)
                proj(c + 1, t + 1, 1)
                proj(c + 2, t + 2, 2)
                transposes2(n)
                proj(c + 3, t + 3, 3)
                products2(n)
                proj(c + 4, t + 4, 4)
                sums2(n)
                for m in range(5, KT):
                    proj(c + m, t + m, m)
                for s in range(2):
                    proj(c0 + (L_GAB0 + s), t0 + (U_GAB + s), s)
                pe.wait_ge(up_dve.sem, up_dve.at(l))
                for g in range(4):
                    c = c0 + (L_PW + g)
                    pe.wait_ge(wsplit.sem, wsplit.at(c))
                    if g >= 2:
                        pe.wait_ge(pw_dve.sem, pw_dve.at(l * KT + (2 * g - 3)))
                    for m in range(2):
                        for k in range(2):
                            i = three((psS, psT)[g % 2][:, m, :], lambda x: wsp[:, g % SPLIT, x, 2 * k + m, :],
                                      lambda x: mix2[:, x, 2 * g + k, :], k == 0, k == 1)
                    i.then_inc(used.sem, 1)
                with pe.Fori(1, KT) as m:
                    for s in range(2):
                        proj(c0 + L_GAB + m * 2 + s, t0 + U_GAB + m * 2 + s, s)
                tail_pe(pe, chunk, free, proj, norm, split_by, c0 + L_WO, t0 + U_WO, mix2, split_by(m2_dve, l * KT), l * 2 + 3, l * 16 + 24, l * FT + FT)
            pe.wait_ge(drained.sem, drained.at(T_B2 + LAYERS * T_LAYER - 1))
            for t in range(TT):
                if t >= 2:
                    pe.wait_ge(ou_act.sem, ou_act.at(t - 2))
                for f in range(KT):
                    i = nc.tensor.transpose((psT, psS)[t % 2][:, f // 4, f % 4 * P:(f % 4 + 1) * P], xT[:, f, t * P:(t + 1) * P], ident)
                i.then_inc(ou_pe.sem, 1)

        @block.vector
        def _(dve):
            v = nc.vector
            count = [0]

            def link(i):
                i.then_inc(su_dve.sem, 1)
                count[0] += 1
                dve.wait_ge(su_dve.sem, count[0])

            def drain(c, t, s, dst):
                dve.wait_ge(used.sem, used.at(c))
                v.scalar_tensor_tensor(dst, psA[:, s % 2, :], -0.5, c_rs[:, :], ALU.mult, ALU.mult).then_inc(drained.sem, 1)

            def flat(b):
                return b[:, :, :, :].rearrange("p h k t -> p h (k t)")

            def residual(n, m, s, gain, add, c=None):
                x = xT[:, :, :].rearrange("p k t -> p (k t)")[:, bass.ds(m * T, T)]
                g2 = flat(xg)
                if add:
                    dve.wait_ge(used.sem, used.at(c))
                    v.tensor_tensor(x, x, psA[:, s, :], ALU.add).then_inc(drained.sem, 1)
                dve.wait_ge(res_act.sem, res_act.at(n, "hi"))
                v.scalar_tensor_tensor(g2[:, 1, bass.ds(m * T, T)], x, gain, hi_f(g2[:, 0, bass.ds(m * T, T)]),
                                       ALU.mult, ALU.subtract).then_inc(res_dve.sem, 1)
                if not add and n:
                    dve.wait_ge(res_dve.sem, res_dve.at(n - 1))
                dve.wait_ge(res_act.sem, res_act.at(n, "square"))
                v.tensor_tensor(acc[:, :], acc[:, :], sq[:, s, :], ALU.add).then_inc(res_dve.sem, 1)

            def norm(k):
                dve.wait_ge(nm_act.sem, nm_act.at(k))
                v.scalar_tensor_tensor(n_b[:, :], psO[:, :], D * EPS, n_r2[:, :], ALU.add, ALU.mult).then_inc(nm_dve.sem, 1)
                dve.wait_ge(nm_dve.sem, nm_dve.at(k, "newton"))
                v.scalar_tensor_tensor(c_rs[:, :], n_b[:, :], 3.0, n_r0[:, :], ALU.subtract, ALU.mult).then_inc(nm_dve.sem, 1)
                v.memset(acc[:, :], 0.0).then_inc(nm_dve.sem, 1)
                dve.wait_ge(nm_dve.sem, nm_dve.at(k))
                settled(dve)

            def headnorm(n, src, gain, dst_lo, dst_hi, dim, w=T):
                dve.wait_ge(hn_act.sem, hn_act.at(n, "root2"))
                v.scalar_tensor_tensor(n_b[:, 0:w], psO[:, 0:w], dim * EPS, n_r2[:, 0:w], ALU.add, ALU.mult).then_inc(hn_dve.sem, 1)
                dve.wait_ge(hn_dve.sem, hn_dve.at(n, "newton"))
                v.scalar_tensor_tensor(n_b[:, 0:w], n_b[:, 0:w], 3.0, n_r0[:, 0:w], ALU.subtract, ALU.mult).then_inc(hn_dve.sem, 1)
                dve.wait_ge(hn_dve.sem, hn_dve.at(n, "scale"))
                v.scalar_tensor_tensor(h_t[:, 0:w], src, gain, n_b[:, 0:w], ALU.mult, ALU.mult).then_inc(hn_dve.sem, 1)
                dve.wait_ge(hn_act.sem, hn_act.at(n, "hi"))
                v.tensor_tensor(dst_lo, h_t[:, 0:w], hi_f(dst_hi), ALU.subtract).then_inc(hn_dve.sem, 1)

            def pcol(name, i=0):
                return par[:, PAR[name].start + i:PAR[name].start + i + 1]

            def setup_copy(f):
                dve.wait_ge(su_pe.sem, 2 + f)
                v.tensor_copy(xT[:, f, :], psA[:, f % 2, :]).then_inc(drained.sem, 1)

            v.memset(small[:, 60:61], EPS).then_inc(eps_in.sem, 1)
            link(v.memset(acc[:, :], 0.0))
            link(v.memset(par2[:, :], 0.0))
            link(v.memset(E[:, :, :, 0:GROUPS, T // 2:].bitcast(F32), 0.0))
            link(v.memset(E[:, :, :, GROUPS, :].bitcast(F32), 0.0))
            v.memset(vc[:, :, :, :].bitcast(F32), 0.0).then_inc(pad_dve.sem, 1)
            dve.wait_ge(su_pe.sem, 1)
            link(v.tensor_copy(par[:, PAR["n1"]], psT[:, 0, 0:KT]))
            setup_copy(0)
            for f in range(KT):
                if f + 1 < KT:
                    setup_copy(f + 1)
                residual(f, f, f % 2, pcol("n1", f), False)
            norm(0)
            dve.wait_ge(g_in, G_DMAS * 16)
            v.tensor_copy(gw[:, 0], gwraw[:, :, :]).then_inc(cg_dve.sem, 1)
            v.tensor_copy(w2[:, :, 0], w2raw[:, :, :, :]).then_inc(su_dve.sem, 1)
            count[0] += 1
            dve.wait_ge(cg_dve.sem, cg_dve.at(0, "gw_hi"))
            v.tensor_tensor(gw[:, 1], gwraw[:, :, :], hi_f(gw[:, 0]), ALU.subtract).then_inc(cg_dve.sem, 1)
            for kv in range(2):
                dve.wait_ge(su_dve.sem, count[0])
                v.tensor_tensor(w2[:, kv, 1], w2raw[:, kv], hi_f(w2[:, kv, 0]), ALU.subtract).then_inc(cg_dve.sem, 1)

            def blocks(n):
                kv, x = n // 2, n % 2
                dve.wait_ge(e_act.sem, e_act.at(n, "hi"))
                v.tensor_tensor(Et[:, 1], kvraw[:, n, :], hi_f(Et[:, 0]), ALU.subtract).then_inc(e_dve.sem, 1)
                dve.wait_ge(e_dve.sem, e_dve.at(n, "lo"))
                for odd in range(2):
                    v.tensor_copy(E[odd * HD:(odd + 1) * HD, kv, :, 2 * x + 1, 0:T // 2],
                                  Et[HD:P, :, odd::2]).then_inc(e_dve.sem, 1)

            for n in range(12):
                drain(C_KV + n, T_KV + n, n, kvraw[:, n, :])
                if 4 <= n < 8:
                    blocks(n - 4)
            dve.wait_ge(su_pe.sem, KT + 3)
            link(v.tensor_copy(par[:, KT:], psS[:, 1, KT:PAR_N]))
            link(v.tensor_copy(par2[:, 0:2 * PAR2_N], psS[:, 1, 256:256 + 2 * PAR2_N]))
            for name in ("qg", "kg"):
                link(v.tensor_scalar(par[:, PAR[name]], par[:, PAR[name]], -0.5, None, ALU.mult))
            lam = par[:, PAR["lam"]]
            z, f1, f2, f3 = (small[:, 16 + 8 * j:24 + 8 * j] for j in range(4))
            v.scalar_tensor_tensor(z, lam, -1.0, lam, ALU.mult, ALU.max).then_inc(sp_dve.sem, 1)
            for kv, name in enumerate(("posk", "posv")):
                link(v.tensor_copy(E[:, kv, 0, GROUPS, 0:16], par[:, PAR[name]]))
                link(v.tensor_tensor(E[:, kv, 1, GROUPS, 0:16], par[:, PAR[name]], hi_f(E[:, kv, 0, GROUPS, 0:16]), ALU.subtract))
            dve.wait_ge(cg_pe.sem, cg_pe.at(0, "gates"))
            v.scalar_tensor_tensor(gsc[0:48, :], psS[0:48, 0, :], -0.5, c_rs[0:48, :], ALU.mult, ALU.mult).then_inc(cg_dve.sem, 1)

            def key_norm(n):
                br, x = n // 2, n % 2
                headnorm(n, kvraw[:, 4 + 4 * br + x, :], pcol("kg", 1 + br), kn[:, br, x, 1], kn[:, br, x, 0], HD)

            def value_lo(n):
                br, x = n // 2, n % 2
                dve.wait_ge(vt_act.sem, vt_act.at(n))
                v.tensor_tensor(vtok[:, br, 1, :, x * P:(x + 1) * P], psT[:, n % 3, :].rearrange("p (k d) -> p k d", d=P),
                                hi_f(vtok[:, br, 0, :, x * P:(x + 1) * P]), ALU.subtract).then_inc(vt_dve.sem, 1)


            def softplus():
                dve.wait_ge(sp_act.sem, 1)
                link(v.tensor_scalar(f1, z, 2.0, None, ALU.add))
                link(v.reciprocal(f2, f1))
                link(v.tensor_tensor(f1, z, f2, ALU.mult))
                link(v.tensor_tensor(f2, f1, f1, ALU.mult))
                link(v.tensor_scalar(f3, f2, 1.0 / 19, None, ALU.mult))
                for odd in (17, 15, 13, 11, 9, 7, 5, 3):
                    link(v.scalar_tensor_tensor(f3, f3, 1.0 / odd, f2, ALU.add, ALU.mult))
                link(v.scalar_tensor_tensor(f3, f3, 1.0, f1, ALU.add, ALU.mult))
                link(v.tensor_scalar(f1, lam, -8.0, 0.0, ALU.mult, ALU.max))
                link(v.scalar_tensor_tensor(small[:, 0:8], f3, 16.0, f1, ALU.mult, ALU.add))
                link(v.tensor_scalar(small[:, 8:16], small[:, 0:8], -1.0, None, ALU.mult))

            key_norm(0)
            for n in range(3):
                value_lo(n)
            for n in range(1, 4):
                key_norm(n)
                if n == 1:
                    value_lo(3)
                if n == 2:
                    softplus()
            for n in range(4):
                kv, m = n // 2, n % 2
                dve.wait_ge(used.sem, used.at(C_CMP + 2 * n + 1))
                bank = (psA, psS)[kv]
                v.tensor_tensor(bcol[:, n:n + 1], bank[:, m, P:P + 1], pcol("b1v" if kv else "b1k", m), ALU.add).then_inc(ch_dve.sem, 1)
                dve.wait_ge(ch_act.sem, ch_act.at(n))
                v.tensor_tensor(hidr[:, kv, 1, m], hidc[:, m, :], hi_f(hidr[:, kv, 0, m]), ALU.subtract).then_inc(drained.sem, 1)
            def query(n):
                drain(C_Q + n, T_Q + n, n, qraw[:, :])

            def query_norm(n):
                dve.wait_ge(qr_act.sem, qr_act.at(n))
                v.scalar_tensor_tensor(n_b[:, :], psA[:, n % 2, :], HD * EPS, n_r2[:, :], ALU.add, ALU.mult).then_inc(q_dve.sem, 1)
                dve.wait_ge(q_dve.sem, q_dve.at(n, "newton"))
                v.scalar_tensor_tensor(n_b[:, :], n_b[:, :], 3.0, n_r0[:, :], ALU.subtract, ALU.mult).then_inc(q_dve.sem, 1)
                dve.wait_ge(q_dve.sem, q_dve.at(n, "scale"))
                if n:
                    dve.wait_ge(ql_pool.sem, ql_pool.at(n - 1))
                v.scalar_tensor_tensor(h_t[:, :], qraw[:, :], pcol("qg"), n_b[:, :], ALU.mult, ALU.mult).then_inc(q_dve.sem, 1)

            def maxima(U, xs):
                n, hd, o = U // 4, U % 4 // 2, 32 * (U % 2)
                dve.wait_ge(b_pool.sem, b_pool.at(n, f"head{hd}"))
                for x in xs:
                    qt = TT - 1 - x
                    w = P * (qt + 1)
                    dve.wait_ge(us_pe.sem, us_pe.at(U, f"s{x}"))
                    v.tensor_tensor_reduce(out=Pm[:, U % 2, P_AT[qt]:P_AT[qt] + w], in0=bias[:, hd, T - w:T],
                                           in1=psS[:, x % 2, 0:w], scale=1.0, scalar=-3e38, op0=ALU.add,
                                           op1=ALU.max, accum_out=st[:, o + qt:o + qt + 1]).then_inc(um_dve.sem, 1)
                if 3 in xs:
                    dve.wait_ge(um_dve.sem, um_dve.at(U, "max3"))
                    v.tensor_scalar(st[:, o + 4:o + 8], st[:, o:o + 4], -HD ** -0.5, None, ALU.mult).then_inc(um_dve.sem, 1)

            def probabilities(U):
                n, hd, br, o = U // 4, U % 4 // 2, U % 2, 32 * (U % 2)
                dve.wait_ge(ue_act.sem, ue_act.at(U))
                v.reciprocal(st[:, o + 12:o + 16], st[:, o + 8:o + 12]).then_inc(ug_dve.sem, 1)
                dve.wait_ge(ug_dve.sem, ug_dve.at(U, "rec"))
                g = 3 * (n + 8 * hd) + 1 + br
                v.tensor_tensor(st[:, o + 16:o + 20].unsqueeze(2), st[:, o + 12:o + 16].unsqueeze(2), gates[:, :, g:g + 1],
                                ALU.mult).then_inc(ug_dve.sem, 1)
                dve.wait_ge(ug_dve.sem, ug_dve.at(U))
                for qt in range(TT):
                    pq = Pm[:, U % 2, P_AT[qt]:P_AT[qt] + P * (qt + 1)]
                    v.tensor_scalar(pq, pq, st[:, o + 16 + qt:o + 17 + qt], None, ALU.mult).then_inc(up_dve1.sem, 1)

            def lo(U):
                dve.wait_ge(uh_act.sem, uh_act.at(U))
                v.tensor_tensor(PT[:, 1, :], psT[:, :, :].rearrange("p b t -> p (b t)")[:, 0:1280], hi_f(PT[:, 0, :]),
                                ALU.subtract).then_inc(ul_dve.sem, 1)

            pcq = Pc[:, :, :, :].rearrange("p q h n -> p h q n")

            def per_row(o):
                return cst[:, o:o + 8].rearrange("p (h q o) -> p h q o", h=2, o=1).broadcast_to([P, 2, TT, 32])

            def c_maxima(n):
                dve.wait_ge(b_pool.sem, b_pool.at(n, "compressed1"))
                dve.wait_ge(cs_pe.sem, cs_pe.at(n))
                v.tensor_tensor(pcq, psA[:, n % 2, 0:2 * P].rearrange("p (h q n) -> p h q n", h=2, n=32),
                                cbias[:, :, :].rearrange("p h (q n) -> p h q n", n=32), ALU.add).then_inc(cm_dve.sem, 1)
                dve.wait_ge(cm_dve.sem, cm_dve.at(n, "add"))
                v.tensor_reduce(cst[:, 0:8].rearrange("p (h q) -> p h q", h=2), pcq, AX.X, ALU.max).then_inc(cm_dve.sem, 1)
                dve.wait_ge(cm_dve.sem, cm_dve.at(n, "max"))
                v.tensor_tensor(pcq, pcq, per_row(0), ALU.subtract).then_inc(cm_dve.sem, 1)

            def c_probabilities(n):
                def step(i, name):
                    i.then_inc(cp_dve.sem, 1)
                    dve.wait_ge(cp_dve.sem, cp_dve.at(n, name))

                dve.wait_ge(ce_act.sem, ce_act.at(n))
                mask = con[:, CONST["cmask"]].rearrange("p (q n) -> p q n", n=32).unsqueeze(1).broadcast_to([P, 2, TT, 32])
                step(v.tensor_tensor(pcq, pcq, mask, ALU.mult), "mask")
                step(v.tensor_reduce(cst[:, 8:16].rearrange("p (h q) -> p h q", h=2), pcq, AX.X, ALU.add), "sum")
                step(v.tensor_scalar(cst[:, 16:24], cst[:, 8:16], 1e-30, None, ALU.max), "guard")
                step(v.reciprocal(cst[:, 24:32], cst[:, 16:24]), "rec")
                gt = gates[:, :, :].rearrange("p q (h m r) -> p h q m r", h=2, r=3)[:, :, :, n, 0:1]
                step(v.tensor_tensor(cst[:, 32:40].rearrange("p (h q o) -> p h q o", h=2, o=1),
                                     cst[:, 24:32].rearrange("p (h q o) -> p h q o", h=2, o=1), gt, ALU.mult), "gate")
                v.tensor_tensor(pcq, pcq, per_row(32), ALU.mult).then_inc(cp_dve.sem, 1)

            def c_lo(n):
                dve.wait_ge(ch_act2.sem, ch_act2.at(n))
                v.tensor_tensor(PTc[1][0:HD, :], psA[0:HD, (n + 1) % 2, :], hi_f(PTc[0][0:HD, :]), ALU.subtract).then_inc(cl_dve.sem, 1)

            def out_lo(n, hd):
                rows = slice(hd * HD, (hd + 1) * HD)
                dve.wait_ge(oh_act.sem, oh_act.at(2 * n + hd))
                v.tensor_tensor(attnT[rows, 1, n, :], psO[rows, :], hi_f(attnT[rows, 0, n, :]), ALU.subtract).then_inc(ol_dve.sem, 1)

            def unit(U, out=None):
                if U + 1 < 32:
                    probabilities(U + 1)
                if out is not None:
                    out_lo(*out)
                if U + 2 < 32:
                    dve.wait_ge(ut_pe.sem, ut_pe.at(U))
                    maxima(U + 2, (0, 1))
                lo(U)
                if U + 2 < 32:
                    maxima(U + 2, (2, 3))

            query(0)
            for hd in range(2):
                v.memset(qz[HD - hd * HD:P - hd * HD, hd, :, :].bitcast(F32), 0.0).then_inc(pad_dve.sem, 1)
                v.memset(PTc[hd][HD:P, :].bitcast(F32), 0.0).then_inc(pad_dve.sem, 1)
            query_norm(0)
            dve.wait_ge(kv_pe.sem, 1)
            v.tensor_scalar(kcraw[:, :], psS[:, 0, 0:P], pcol("b2k"), None, ALU.add).then_inc(kv_dve.sem, 1)
            v.tensor_tensor(vcraw[0:32], psS[0:32, 1, 256:512].rearrange("p (g d) -> p g d", d=HD),
                            b2v[0:32, :].unsqueeze(1).broadcast_to([32, GROUPS, HD]), ALU.add).then_inc(kv_dve.sem, 1)
            dve.wait_ge(kv_dve.sem, kv_dve.at(0, "v"))
            dve.wait_ge(pad_dve.sem, pad_dve.at(0, "vc"))

            def diagonal(h, b):
                return vc[32 * b:32 * b + 32, h, :, b * HD:(b + 1) * HD]

            for b in range(2):
                v.tensor_copy(diagonal(0, b), vcraw[0:32, b::2, :]).then_inc(kv_dve.sem, 1)
            for b in range(2):
                dve.wait_ge(kv_dve.sem, kv_dve.at(0, f"v_hi{b}"))
                if b:
                    v.tensor_copy(vcraw2[32:64], vcraw[0:32]).then_inc(kv_dve.sem, 1)
                    dve.wait_ge(kv_dve.sem, kv_dve.at(0, "v_moved"))
                src = (vcraw, vcraw2)[b][32 * b:32 * b + 32, b::2, :]
                v.tensor_tensor(diagonal(1, b), src, hi_f(diagonal(0, b)), ALU.subtract).then_inc(kv_dve.sem, 1)
            query(1)
            dve.wait_ge(ql_pool.sem, ql_pool.at(0))
            headnorm(4, kcraw[:, :], pcol("kg", 0), kc[:, 1], kc[:, 0], HD, P)
            maxima(0, range(4))
            maxima(1, range(4))
            c_maxima(0)
            probabilities(0)
            c_probabilities(0)
            for n in range(8):
                U, last = 4 * n, n == 7
                unit(U, (n - 1, 1) if n else None)
                if not last:
                    query_norm(n + 1)
                unit(U + 1)
                c_lo(n)
                unit(U + 2, (n, 0))
                if n < 6:
                    query(n + 2)
                if not last:
                    c_maxima(n + 1)
                unit(U + 3)
                if not last:
                    c_probabilities(n + 1)
            out_lo(7, 1)

            dve.wait_ge(cv_pe.sem, cv_pe.at(15))
            link(v.memset(acc[:, :], 0.0))
            v.memset(bd[:, :, :, :].bitcast(F32), 0.0).then_inc(lw_dve.sem, 1)
            v.memset(lx[:, 0:3], 0.0).then_inc(lw_dve.sem, 1)
            dve.wait_ge(lw_dve.sem, lw_dve.at(0))

            def col(name, i):
                return par[:, bass.ds(i + PAR[name].start, 1)]

            r_, i_, t_, a_, u_ = lt
            s_, o_ = t_, i_
            with dve.Fori(0, KT) as m:
                def step(i):
                    i.then_inc(lr_dve.sem, 1)

                def own(name):
                    dve.wait_ge(lr_dve.sem, lr_dve.at(m, name))

                def act(name):
                    dve.wait_ge(lr_act.sem, lr_act.at(m, name))

                c, t = C_LRU + m * 4, T_LRU + m * 4
                drain(c, t, 0, lx[:, 3:T + 3])
                dve.wait_ge(drained.sem, drained.at(t))
                step(v.tensor_scalar(xc[:, :], lx[:, 3:T + 3], col("cw", m + 3 * KT), col("cb", m), ALU.mult, ALU.add))
                for k in range(3):
                    own(f"tap{k}")
                    step(v.scalar_tensor_tensor(xc[:, :], lx[:, 2 - k:T + 2 - k], col("cw", m + (2 - k) * KT), xc[:, :],
                                                ALU.mult, ALU.add))
                drain(c + 1, t + 1, 1, gl[:, :])
                act("hi")
                step(v.tensor_tensor(xcr[:, 1], xc[:, :], hi_f(xcr[:, 0]), ALU.subtract))
                dve.wait_ge(lw_in, 32)
                for b in range(2):
                    rows = slice(b * HD, (b + 1) * HD)
                    act(f"w{b}")
                    raw = lruw[:, :, :, :].rearrange("p w m j -> p w (m j)")[rows, :, bass.ds(m * HD, HD)]
                    step(v.tensor_tensor(bd[rows, 1, :, rows], raw, hi_f(bd[rows, 0, :, rows]), ALU.subtract))
                drain(c + 2, t + 2, 2, mg[:, :])
                act("tanh")
                step(v.tensor_scalar(u_[:, :], t_[:, :], 1.0, None, ALU.add))
                own("one")
                step(v.reciprocal(u_[:, :], u_[:, :]))
                own("rec")
                step(v.tensor_tensor(u_[:, :], u_[:, :], t_[:, :], ALU.mult))
                step(v.tensor_tensor(o_[:, :], i_[:, :], xc[:, :], ALU.mult))
                dve.wait_ge(used.sem, used.at(c + 3))
                v.tensor_tensor(mixT[:, :, :].rearrange("p k t -> p (k t)")[:, bass.ds(m * T, T)], mg[:, :], psA[:, 1, :],
                                ALU.mult).then_inc(drained.sem, 1)
                act("root")
                own("ix")
                step(v.tensor_tensor(u_[:, :], s_[:, :], o_[:, :], ALU.mult))
                own("b")
                step(v.tensor_tensor_scan(o_[:, :], a_[:, :], u_[:, :], 0.0, ALU.mult, ALU.add))
                own("scan")
                step(v.tensor_tensor(u_[:, :], o_[:, :], gl[:, :], ALU.mult))
                act("out_hi")
                at = bass.ds(m * T, T)
                step(v.tensor_tensor(flat(lruT)[:, 1, at], u_[:, :], hi_f(flat(lruT)[:, 0, at]), ALU.subtract))
                own("out_lo")

            mrgf, mixf = flat(attnT), mixT[:, :, :].rearrange("p k t -> p (k t)")
            with dve.Fori(0, KT) as m:
                c, t = C_MIX + m * 2, T_MIX + m * 2
                at = bass.ds(m * T, T)
                drain(c, t, 0, mg[:, :])
                dve.wait_ge(used.sem, used.at(c + 1))
                dve.wait_ge(mx_act.sem, mx_act.at(m, "gate"))
                v.tensor_tensor(gl[:, :], mg[:, :], psA[:, 1, :], ALU.mult).then_inc(drained.sem, 1)
                dve.wait_ge(drained.sem, drained.at(t + 1))
                v.tensor_tensor(xc[:, :], gl[:, :], mixf[:, at], ALU.add).then_inc(mx_dve.sem, 1)
                dve.wait_ge(mx_act.sem, mx_act.at(m, "hi"))
                v.tensor_tensor(mrgf[:, 1, at], xc[:, :], hi_f(mrgf[:, 0, at]), ALU.subtract).then_inc(mx_dve.sem, 1)

            def tail_dve(c0, t0, k, n, ff, gain2, gain1):
                with dve.Fori(0, 4) as i:
                    for s in range(2):
                        residual(i * 2 + (n + s), i * 2 + s, s, gain2(i * 2 + s), True, c0 + i * 2 + s)
                norm(k)
                hf = flat(hid)
                with dve.Fori(0, FT) as f:
                    c, t = c0 + 8 + f * 2, t0 + 8 + f * 2
                    drain(c, t, 0, fg[:, 0, :])
                    drain(c + 1, t + 1, 1, fu[:, :])
                    dve.wait_ge(drained.sem, drained.at(t + 1))
                    dve.wait_ge(ff_act.sem, ff_act.at(f + ff, "silu"))
                    v.tensor_tensor(ft[:, :], fg[:, 1, :], fu[:, :], ALU.mult).then_inc(ff_dve.sem, 1)
                    dve.wait_ge(ff_act.sem, ff_act.at(f + ff, "hi"))
                    at = bass.ds(f * T, T)
                    v.tensor_tensor(hf[:, 1, at], ft[:, :], hi_f(hf[:, 0, at]), ALU.subtract).then_inc(ff_dve.sem, 1)
                c1, t1 = c0 + 8 + 2 * FT, t0 + 8 + 2 * FT
                with dve.Fori(0, 4) as i:
                    for s in range(2):
                        residual(i * 2 + (n + 8 + s), i * 2 + s, s, gain1(i * 2 + s), True, c1 + i * 6 + (3 * s + 2))

            def col2(i):
                return par2[:, bass.ds(i, 1)]

            tail_dve(C_WO, T_WO, 1, 8, 0, lambda m: col("n2", m), lambda m: col2(m + PAR2["n1"].start))

            def layer_col(name, m=0):
                return lay[:, PAR2[name].start + m:PAR2[name].start + m + 1]

            r32 = slice(0, 32)

            def rotated2(n, x):
                c = n * 4 + x

                def step(i, name):
                    i.then_inc(h2_rot.sem, 1)
                    dve.wait_ge(h2_rot.sem, h2_rot.at(c, name))

                dve.wait_ge(h2_act.sem, h2_act.at(c, "gain"))
                settled(dve)
                step(v.stream_shuffle(rot[r32, :], raw2[r32, x, :], [(p + 16) % 32 for p in range(32)]), "swap")
                step(v.tensor_tensor(rot[r32, :], rot[r32, :], con2[r32, CON2["sin"]], ALU.mult), "sin")
                step(v.tensor_tensor(raw2[r32, x, :], raw2[r32, x, :], con2[r32, CON2["cos"]], ALU.mult), "cos")
                v.tensor_tensor(raw2[r32, x, :], raw2[r32, x, :], rot[r32, :], ALU.add).then_inc(h2_rot.sem, 1)

            def headnorm2(n, x):
                c = n * 4 + x
                dve.wait_ge(h2_root.sem, h2_root.at(c, "root2"))
                v.scalar_tensor_tensor(n_b[:, :], psO[:, :], QK2 * EPS, n_r2[:, :], ALU.add, ALU.mult).then_inc(h2_dve.sem, 1)
                dve.wait_ge(h2_dve.sem, h2_dve.at(c, "newton"))
                v.scalar_tensor_tensor(n_b[:, :], n_b[:, :], 3.0, n_r0[:, :], ALU.subtract, ALU.mult).then_inc(h2_dve.sem, 1)
                dve.wait_ge(h2_dve.sem, h2_dve.at(c, "scale"))
                dve.wait_ge(h2_rot.sem, h2_rot.at(c))
                v.tensor_tensor(norm2[:, :], raw2[:, x, :], n_b[:, :], ALU.mult).then_inc(h2_dve.sem, 1)

            def low2(n, x):
                dve.wait_ge(h2_hi.sem, h2_hi.at(n * 4 + x, "hi"))
                v.tensor_tensor(qk2[:, x, 1], norm2[:, :], hi_f(qk2[:, x, 0]), ALU.subtract).then_inc(h2_lo.sem, 1)

            def values2(n, x):
                dve.wait_ge(v2_act.sem, v2_act.at(n * 2 + x))
                at = slice(x * P, (x + 1) * P)
                v.tensor_tensor(vtok2[:, 1, :, at], psT[:, x, :].rearrange("p (k d) -> p k d", d=P), hi_f(vtok2[:, 0, :, at]),
                                ALU.subtract).then_inc(v2_dve.sem, 1)

            def softmax2(n):
                def step(i):
                    i.then_inc(a2_dve.sem, 1)

                def own(name):
                    dve.wait_ge(a2_dve.sem, a2_dve.at(n, name))

                for c in range(2):
                    o = 32 * c
                    for x, qt in enumerate((3, 2, 1, 0)):
                        w = P * (qt + 1)
                        dve.wait_ge(a2_pe.sem, a2_pe.at(n, f"s{c}_{x}"))
                        settled(dve)
                        step(v.tensor_tensor_reduce(out=Pm2[:, c, P_AT[qt]:P_AT[qt] + w], in0=con2[:, CON2["chunk"]][:, T - w:T],
                                                    in1=psS[:, x % 2, 0:w], scale=1.0, scalar=-3.3e38, op0=ALU.add, op1=ALU.max,
                                                    accum_out=st2[:, o + qt:o + qt + 1]))
                    own(f"max{c}_3")
                    step(v.tensor_scalar(st2[:, o + 4:o + 8], st2[:, o:o + 4], -QK2 ** -0.5, None, ALU.mult))
                dve.wait_ge(a2_act.sem, a2_act.at(n, "exp1_3"))
                sums = st2[:, :].rearrange("p (c x) -> p c x", c=2)
                step(v.reciprocal(sums[:, :, 12:16], sums[:, :, 8:12]))
                own("rec")
                step(v.tensor_scalar(st2[:, 48:52], st2[:, 44:48], small[:, 36:37], None, ALU.mult))
                own("neg")
                for qt in range(TT):
                    at = slice(P_AT[qt], P_AT[qt] + P * (qt + 1))
                    step(v.tensor_scalar(Pm2[:, 0, at], Pm2[:, 0, at], st2[:, 12 + qt:13 + qt], None, ALU.mult))
                for qt in range(TT):
                    at = slice(P_AT[qt], P_AT[qt] + P * (qt + 1))
                    own(f"scale{qt}")
                    step(v.scalar_tensor_tensor(Pm2[:, 0, at], Pm2[:, 1, at], st2[:, 48 + qt:49 + qt], Pm2[:, 0, at], ALU.mult, ALU.add))

            def lo2(n):
                dve.wait_ge(a2_act.sem, a2_act.at(n, "hi"))
                v.tensor_tensor(PT2[:, 1, :], psT[:, :, :].rearrange("p b t -> p (b t)")[:, 0:1280], hi_f(PT2[:, 0, :]),
                                ALU.subtract).then_inc(a2_dve.sem, 1)

            def out2(n, h):
                dve.wait_ge(a2_act.sem, a2_act.at(n, "root2"))
                v.scalar_tensor_tensor(n_b[:, :], psT[:, 2, :], V2 * EPS, n_r2[:, :], ALU.add, ALU.mult).then_inc(a2_dve.sem, 1)
                dve.wait_ge(a2_dve.sem, a2_dve.at(n, "newton"))
                v.scalar_tensor_tensor(n_b[:, :], n_b[:, :], 3.0, n_r0[:, :], ALU.subtract, ALU.mult).then_inc(a2_dve.sem, 1)
                dve.wait_ge(a2_dve.sem, a2_dve.at(n, "scale"))
                af = aT2[:, :, :].rearrange("p k t -> p (k t)")
                for d in range(2):
                    v.scalar_tensor_tensor(af[:, bass.ds(h * 2 * T + d * T, T)] if not isinstance(h, int) else aT2[:, 2 * h + d, :], os2[:, d, :], layer_col("sub", d), n_b[:, :],
                                           ALU.mult, ALU.mult).then_inc(a2_dve.sem, 1)

            dve.wait_ge(c2_in, 16)
            with dve.Fori(0, LAYERS) as l:
                c0, t0 = l * C_LAYER + C_B2, l * T_LAYER + T_B2

                def once(i, name):
                    i.then_inc(ly_dve.sem, 1)
                    dve.wait_ge(ly_dve.sem, ly_dve.at(l, name))

                dve.wait_ge(res_dve.sem, res_dve.at(l * 16 + 23))
                once(v.tensor_copy(lay[:, :], par2[:, bass.ds(l * PAR2_N, PAR2_N + KT)]), "copy")
                once(v.tensor_scalar(lay[:, PAR2["qg"].start:PAR2["kg"].stop], lay[:, PAR2["qg"].start:PAR2["kg"].stop], -0.5, None, ALU.mult), "gains")
                init = con[:, bass.ds(l * 2 + CONST["lam"].start, 1)]
                once(v.tensor_scalar(lay[:, PAR2["sub"]], lay[:, PAR2["sub"]], con[:, bass.ds(l * 2 + (CONST["lam"].start + 1), 1)], None, ALU.mult), "sub")
                lq = lay[:, PAR2["lam"]].rearrange("p (c x) -> p c x", x=2)
                once(v.tensor_tensor(small[:, 32:34].unsqueeze(2), lq[:, :, 0:1], lq[:, :, 1:2], ALU.mult), "products")
                norm(l * 2 + 2)

                def tile2(c, t, x):
                    drain(c + x, t + x, x, raw2[:, x, :])
                    if x >= 4:
                        dve.wait_ge(drained.sem, drained.at(t + x))

                def raw_values(c, t, x):
                    tile2(c, t, 4 + x)
                    v.sem_inc(v2_raw.sem, 1)

                n0 = l * HEADS2
                tile2(c0, t0, 0)
                rotated2(n0, 0)
                tile2(c0, t0, 1)
                rotated2(n0, 1)
                for x in range(4):
                    headnorm2(n0, x)
                    if x < 2:
                        tile2(c0, t0, x + 2)
                    else:
                        raw_values(c0, t0, x - 2)
                    low2(n0, x)
                    if x < 2:
                        rotated2(n0, x + 2)
                dve.wait_ge(ly_act.sem, ly_act.at(l))
                once(v.tensor_tensor(small[:, 36:37], small[:, 35:36], small[:, 34:35], ALU.subtract), "diff")
                once(v.tensor_tensor(small[:, 36:37], small[:, 36:37], init, ALU.subtract), "lambda")
                values2(n0, 0)
                values2(n0, 1)
                settled(dve)
                with dve.Fori(0, HEADS2 - 1) as h:
                    n = l * HEADS2 + h
                    c, t = c0 + h * 6 + 6, t0 + h * 6 + 6
                    tile2(c, t, 0)
                    softmax2(n)
                    tile2(c, t, 1)
                    rotated2(n + 1, 0)
                    headnorm2(n + 1, 0)
                    lo2(n)
                    low2(n + 1, 0)
                    tile2(c, t, 2)
                    rotated2(n + 1, 1)
                    headnorm2(n + 1, 1)
                    low2(n + 1, 1)
                    tile2(c, t, 3)
                    rotated2(n + 1, 2)
                    headnorm2(n + 1, 2)
                    raw_values(c, t, 0)
                    low2(n + 1, 2)
                    rotated2(n + 1, 3)
                    headnorm2(n + 1, 3)
                    low2(n + 1, 3)
                    raw_values(c, t, 1)
                    out2(n, h)
                    values2(n + 1, 0)
                    values2(n + 1, 1)

                def upool(i):
                    i.then_inc(up_dve.sem, 1)

                def pool_drain(m):
                    drain(c0 + (L_U + m), t0 + (U_U + m), m, ur[:, m % 2, 16:T + 16])

                def pool2(m):
                    g = m // 2
                    w, e = POOL_W[g], CONST["edge"].start + sum(POOL_W[:g])
                    dve.wait_ge(drained.sem, drained.at(t0 + (U_U + m)))
                    src = ur[:, m % 2]
                    for k in range(g + 1):
                        dst, b = (ya, yb)[k % 2], 1 << k
                        lo = 2 * b - 1
                        upool(v.tensor_tensor(dst[:, lo:T + 16], src[:, lo:T + 16], src[:, lo - b:T + 16 - b], ALU.add))
                        dve.wait_ge(up_dve.sem, up_dve.at(l, f"y{m}_{k}"))
                        src = dst
                    upool(v.tensor_tensor(src[:, 16:16 + w], src[:, 16:16 + w], con[:, e:e + w], ALU.mult))
                    dve.wait_ge(up_dve.sem, up_dve.at(l, f"edge{m}"))
                    upool(v.scalar_tensor_tensor(pr[:, :], src[:, 16:T + 16], 1.0 / w, ur[:, m % 2, 16:T + 16], ALU.mult, ALU.subtract))
                    dve.wait_ge(up_act.sem, up_act.at(l * KT + m))
                    upool(v.tensor_tensor(mix2[:, 1, m], pr[:, :], hi_f(mix2[:, 0, m]), ALU.subtract))

                n = n0 + (HEADS2 - 1)
                for b in range(2):
                    upool(v.memset(ur[:, b, 0:16], 0.0))
                pool_drain(0)
                softmax2(n)
                pool_drain(1)
                pool2(0)
                lo2(n)
                pool2(1)
                for m in range(2, KT):
                    pool_drain(m)
                    pool2(m)
                    if m == 3:
                        out2(n, HEADS2 - 1)
                def merge_drain(c, m):
                    for s in range(2):
                        drain(c + s, t0 + U_GAB + m * 2 + s, s, mg2[:, s, :])

                pf, af = (x[:, :, :].rearrange("p k t -> p (k t)") for x in (poolT, aT2))

                def merge(m):
                    n = l * KT + m
                    at = bass.ds(m * T, T)
                    for s, (name, src) in enumerate((("ga", pf), ("gb", af))):
                        dve.wait_ge(m2_act.sem, m2_act.at(n, name))
                        v.tensor_tensor(mg2[:, s, :], mg2[:, s, :], src[:, at], ALU.mult).then_inc(m2_dve.sem, 1)
                    dve.wait_ge(m2_dve.sem, m2_dve.at(n, "attn"))
                    v.tensor_tensor(mt2[:, :], mg2[:, 0, :], mg2[:, 1, :], ALU.add).then_inc(m2_dve.sem, 1)
                    dve.wait_ge(m2_act.sem, m2_act.at(n, "hi"))
                    v.tensor_tensor(flat(mix2)[:, 1, at], mt2[:, :], hi_f(flat(mix2)[:, 0, at]), ALU.subtract).then_inc(m2_dve.sem, 1)

                merge_drain(c0 + L_GAB0, 0)
                for m in range(KT):
                    dve.wait_ge(used.sem, used.at(c0 + (L_PW + m // 2)))
                    v.tensor_scalar(poolT[:, m, :], (psS, psT)[m // 2 % 2][:, m % 2, :], layer_col("ps", m), None, ALU.mult).then_inc(pw_dve.sem, 1)
                dve.wait_ge(pw_dve.sem, pw_dve.at(l * KT + 7))
                merge(0)
                settled(dve)
                with dve.Fori(1, KT) as m:
                    merge_drain(c0 + L_GAB + m * 2, m)
                    merge(m)

                def gain(name):
                    start = PAR2_N if name == "next" else PAR2[name].start
                    return lambda m: lay[:, bass.ds(m + start, 1)]

                tail_dve(c0 + L_WO, t0 + U_WO, l * 2 + 3, l * 16 + 24, l * FT + FT, gain("n2"), gain("next"))

        @block.scalar
        def _(act):
            ac = nc.scalar.activation

            def flat(b):
                return b[:, :, :, :].rearrange("p h k t -> p h (k t)")

            act.dma_start(con[:, 0:CONST_1], a["const"][:, 0:CONST_1]).then_inc(c_in, 16)
            act.dma_start(prow0[0:KT, :], a["norm1_g"][0].rearrange("(r p) -> r p", p=P)).then_inc(g1_in, 16)

            def logexp():
                nc.scalar.preload_act_table_set("natural_log_exp_and_others")

            def roots(sums, dim, of, n, w=T):
                ac(n_r2[:, 0:w], sums, ACT.Ln, bias=small[:, 60:61], scale=1.0 / dim).then_inc(of.sem, 1)
                act.wait_ge(of.sem, of.at(n, "log"))
                ac(n_r0[:, 0:w], n_r2[:, 0:w], ACT.Exp, scale=-0.5).then_inc(of.sem, 1)
                act.wait_ge(of.sem, of.at(n, "root"))
                ac(n_r2[:, 0:w], n_r0[:, 0:w], ACT.Square, scale=dim ** -0.5).then_inc(of.sem, 1)

            def residual(n, t, m, s, gain):
                x = xT[:, :, :].rearrange("p k t -> p (k t)")[:, bass.ds(m * T, T)]
                act.wait_ge(drained.sem, drained.at(t))
                ac(flat(xg)[:, 0, bass.ds(m * T, T)], x, ACT.Copy, scale=gain).then_inc(res_act.sem, 1)
                ac(sq[:, s, :], x, ACT.Square).then_inc(res_act.sem, 1)

            def norm(k):
                logexp()
                act.wait_ge(nm_pe.sem, nm_pe.at(k))
                roots(psO[:, :], D, nm_act, k)

            def headnorm(n, src, dst_hi, dim, w=T):
                ac(h_sq[:, 0:w], src, ACT.Square).then_inc(hn_act.sem, 1)
                act.wait_ge(hn_pe.sem, hn_pe.at(n))
                roots(psO[:, 0:w], dim, hn_act, n, w)
                act.wait_ge(hn_dve.sem, hn_dve.at(n, "apply"))
                ac(dst_hi, h_t[:, 0:w], ACT.Copy).then_inc(hn_act.sem, 1)

            def pcol(name, i=0):
                return par[:, PAR[name].start + i:PAR[name].start + i + 1]

            act.wait_ge(eps_in.sem, 1)
            for f in range(KT):
                residual(f, f, f, f % 2, pcol("n1", f))
            norm(0)
            for n in range(4):
                kv, x = n // 2, n % 2
                if n:
                    act.wait_ge(e_dve.sem, e_dve.at(n - 1))
                    act.wait_ge(e_act.sem, e_act.at(n - 1))
                act.wait_ge(drained.sem, drained.at(T_KV + n))
                ac(Et[:, 0], kvraw[:, n, :], ACT.Copy).then_inc(e_act.sem, 1)
                act.wait_ge(e_dve.sem, e_dve.at(n, "lo"))
                for odd in range(2):
                    ac(E[odd * HD:(odd + 1) * HD, kv, :, 2 * x, 0:T // 2], hi_f(Et[0:HD, :, odd::2]), ACT.Copy).then_inc(e_act.sem, 1)
            logexp()
            z = small[:, 16:24]
            act.wait_ge(sp_dve.sem, 1)
            ac(z, z, ACT.Exp, scale=-1.0).then_inc(sp_act.sem, 1)

            def key_norm(n):
                br, x = n // 2, n % 2
                headnorm(n, kvraw[:, 4 + 4 * br + x, :], kn[:, br, x, 0], HD)

            def value_hi(n):
                br, x = n // 2, n % 2
                act.wait_ge(vt_pe.sem, vt_pe.at(n))
                ac(vtok[:, br, 0, :, x * P:(x + 1) * P], psT[:, n % 3, :].rearrange("p (k d) -> p k d", d=P), ACT.Copy).then_inc(vt_act.sem, 1)

            act.wait_ge(drained.sem, drained.at(T_KV + 9))
            key_norm(0)
            for n in range(3):
                value_hi(n)
            for n in range(1, 4):
                key_norm(n)
                if n == 1:
                    value_hi(3)
            act.wait_ge(cg_pe.sem, cg_pe.at(0))
            ac(gates[:, :, :], psT[:, 1, 0:192].rearrange("p (t g) -> p t g", g=48), ACT.Sigmoid).then_inc(cg_act.sem, 1)
            for n in range(4):
                kv, m = n // 2, n % 2
                act.wait_ge(ch_dve.sem, n + 1)
                bank = (psA, psS)[kv]
                ac(hidc[:, m, :], bank[:, m, 0:P], ACT.Gelu_apprx_tanh, bias=bcol[:, n:n + 1]).then_inc(ch_act.sem, 1)
                act.wait_ge(ch_act.sem, ch_act.at(n, "gelu"))
                ac(hidr[:, kv, 0, m], hidc[:, m, :], ACT.Copy).then_inc(ch_act.sem, 1)
            logexp()

            def query_square(n):
                act.wait_ge(drained.sem, drained.at(T_Q + n))
                ac(h_sq[:, :], qraw[:, :], ACT.Square).then_inc(qs_act.sem, 1)

            def query_roots(n):
                act.wait_ge(q_pe.sem, q_pe.at(n))
                roots(psA[:, n % 2, :], HD, qr_act, n)

            def query_hi(n):
                act.wait_ge(q_dve.sem, q_dve.at(n, "apply"))
                for hd in range(2):
                    rows = slice(hd * HD, (hd + 1) * HD)
                    ac(qz[rows, hd, 0, :], h_t[rows, :], ACT.Copy).then_inc(qi_act.sem, 1)

            def exps(U):
                o = 32 * (U % 2)
                act.wait_ge(um_dve.sem, um_dve.at(U))
                for qt in range(TT):
                    pq = Pm[:, U % 2, P_AT[qt]:P_AT[qt] + P * (qt + 1)]
                    ac(pq, pq, ACT.Exp, bias=st[:, o + 4 + qt:o + 5 + qt], scale=HD ** -0.5,
                       accum_out=st[:, o + 8 + qt:o + 9 + qt]).then_inc(ue_act.sem, 1)

            def hi(U):
                act.wait_ge(ut_pe.sem, ut_pe.at(U))
                if U:
                    act.wait_ge(uv_pe.sem, uv_pe.at(U - 1))
                ac(PT[:, 0, :], psT[:, :, :].rearrange("p b t -> p (b t)")[:, 0:1280], ACT.Copy).then_inc(uh_act.sem, 1)

            def c_exps(n):
                act.wait_ge(cm_dve.sem, cm_dve.at(n))
                pcf = Pc[:, :, :, :].rearrange("p q h n -> p (q h n)")
                ac(pcf, pcf, ACT.Exp, scale=HD ** -0.5).then_inc(ce_act.sem, 1)

            def c_hi(n):
                act.wait_ge(ct_pe.sem, ct_pe.at(n))
                ac(PTc[0][0:HD, :], psA[0:HD, (n + 1) % 2, :], ACT.Copy).then_inc(ch_act2.sem, 1)

            def out_hi(n, hd):
                rows = slice(hd * HD, (hd + 1) * HD)
                act.wait_ge(cv_pe.sem, cv_pe.at(2 * n + hd))
                ac(attnT[rows, 0, n, :], psO[rows, :], ACT.Copy).then_inc(oh_act.sem, 1)

            query_square(0)
            query_roots(0)
            query_hi(0)
            act.wait_ge(kv_dve.sem, kv_dve.at(0, "k"))
            headnorm(4, kcraw[:, :], kc[:, 0], HD, P)
            query_square(1)
            exps(0)
            exps(1)
            query_roots(1)
            c_exps(0)
            for n in range(8):
                U, last = 4 * n, n == 7
                if n:
                    out_hi(n - 1, 1)
                hi(U)
                exps(U + 2)
                hi(U + 1)
                c_hi(n)
                if not last:
                    act.wait_ge(us_pe.sem, us_pe.at(U + 3))
                    query_hi(n + 1)
                exps(U + 3)
                out_hi(n, 0)
                hi(U + 2)
                if n < 6:
                    query_square(n + 2)
                if not last:
                    exps(U + 4)
                    c_exps(n + 1)
                hi(U + 3)
                if not last:
                    exps(U + 5)
                if n < 6:
                    query_roots(n + 2)
            out_hi(7, 1)

            act.wait_ge(ol_dve.sem, ol_dve.at(15))
            for w, name in enumerate(("lru_wa", "lru_wi")):
                act.dma_start(lruw[:, w, :, :], a[name][0].rearrange("(m b) k j -> (b k) m j", b=2)).then_inc(lw_in, 16)
            act.wait_ge(lw_dve.sem, lw_dve.at(0))

            def col(name, i):
                return par[:, bass.ds(i + PAR[name].start, 1)]

            r_, i_, t_, a_, u_ = lt
            s_, o_ = t_, i_
            with act.Fori(0, KT) as m:
                def step(i):
                    i.then_inc(lr_act.sem, 1)

                def own(name):
                    act.wait_ge(lr_act.sem, lr_act.at(m, name))

                def dve(name):
                    act.wait_ge(lr_dve.sem, lr_dve.at(m, name))

                dve("tap3")
                step(ac(xcr[:, 0], xc[:, :], ACT.Copy))
                act.wait_ge(lw_in, 32)
                for b in range(2):
                    rw = slice(b * HD, (b + 1) * HD)
                    raw = lruw[:, :, :, :].rearrange("p w m j -> p w (m j)")[rw, :, bass.ds(m * HD, HD)]
                    step(ac(bd[rw, 0, :, rw], raw, ACT.Copy))
                act.wait_ge(drained.sem, drained.at(T_LRU + m * 4 + 1))
                step(ac(gl[:, :], gl[:, :], ACT.Gelu_apprx_tanh))
                act.wait_ge(drained.sem, drained.at(T_LRU + m * 4 + 2))
                step(ac(mg[:, :], mg[:, :], ACT.Sigmoid))
                act.wait_ge(lr_pe.sem, lr_pe.at(m))
                step(ac(r_[:, :], psS[:, 0, :], ACT.Sigmoid, bias=col("ba", m)))
                step(ac(i_[:, :], psS[:, 1, :], ACT.Sigmoid, bias=col("bi", m)))
                own("r")
                step(ac(t_[:, :], r_[:, :], ACT.Tanh, scale=small[:, bass.ds(m, 1)]))
                step(ac(a_[:, :], r_[:, :], ACT.Exp, scale=small[:, bass.ds(m + 8, 1)]))
                dve("ratio")
                step(ac(s_[:, :], u_[:, :], ACT.Sqrt, scale=2.0))
                dve("out")
                step(ac(flat(lruT)[:, 0, bass.ds(m * T, T)], u_[:, :], ACT.Copy))

            with act.Fori(0, KT) as m:
                act.wait_ge(drained.sem, drained.at(T_MIX + m * 2))
                ac(mg[:, :], mg[:, :], ACT.Sigmoid).then_inc(mx_act.sem, 1)
                act.wait_ge(mx_dve.sem, mx_dve.at(m, "sum"))
                ac(flat(attnT)[:, 0, bass.ds(m * T, T)], xc[:, :], ACT.Copy).then_inc(mx_act.sem, 1)

            act.dma_start(con2[:, :], a["const"][:, CONST_2:CONST_N]).then_inc(c2_in, 16)

            def tail_act(t0, k, n, ff, gain2, gain1):
                with act.Fori(0, 4) as i:
                    for s in range(2):
                        residual(i * 2 + (n + s), t0 + i * 2 + s, i * 2 + s, s, gain2(i * 2 + s))
                norm(k)
                nc.scalar.preload_act_table_set("silu_and_others")
                with act.Fori(0, FT) as f:
                    act.wait_ge(drained.sem, drained.at(t0 + 8 + f * 2))
                    ac(fg[:, 1, :], fg[:, 0, :], ACT.Silu).then_inc(ff_act.sem, 1)
                    act.wait_ge(ff_dve.sem, ff_dve.at(f + ff, "product"))
                    ac(flat(hid)[:, 0, bass.ds(f * T, T)], ft[:, :], ACT.Copy).then_inc(ff_act.sem, 1)
                t1 = t0 + 8 + 2 * FT
                with act.Fori(0, 4) as i:
                    for s in range(2):
                        residual(i * 2 + (n + 8 + s), t1 + i * 2 + s, i * 2 + s, s, gain1(i * 2 + s))

            tail_act(T_WO, 1, 8, 0, lambda m: col("n2", m), lambda m: par2[:, bass.ds(m + PAR2["n1"].start, 1)])
            def square2(t, n, x):
                act.wait_ge(drained.sem, drained.at(t + x))
                if x >= 2:
                    act.wait_ge(h2_pe.sem, h2_pe.at(n * 4 + (x - 2)))
                ac(sq[:, x % 2, :], raw2[:, x, :], ACT.Square).then_inc(h2_act.sem, 1)
                act.wait_ge(h2_act.sem, h2_act.at(n * 4 + x, "square"))
                gain = PAR2["kg" if x >= 2 else "qg"]
                ac(raw2[:, x, :], raw2[:, x, :], ACT.Copy, scale=lay[:, gain]).then_inc(h2_act.sem, 1)

            def roots2(n, x):
                c = n * 4 + x
                act.wait_ge(h2_pe.sem, h2_pe.at(c))
                roots(psO[:, :], QK2, h2_root, c)

            def hi2(n, x):
                c = n * 4 + x
                act.wait_ge(h2_dve.sem, h2_dve.at(c, "apply"))
                ac(qk2[:, x, 0], norm2[:, :], ACT.Copy).then_inc(h2_hi.sem, 1)

            def values2(n, x):
                act.wait_ge(v2_pe.sem, v2_pe.at(n * 2 + x))
                ac(vtok2[:, 0, :, x * P:(x + 1) * P], psT[:, x, :].rearrange("p (k d) -> p k d", d=P), ACT.Copy).then_inc(v2_act.sem, 1)

            def exps2(n):
                for c in range(2):
                    o = 32 * c
                    act.wait_ge(a2_dve.sem, a2_dve.at(n, f"max{c}"))
                    for qt in range(TT):
                        pq = Pm2[:, c, P_AT[qt]:P_AT[qt] + P * (qt + 1)]
                        ac(pq, pq, ACT.Exp, bias=st2[:, o + 4 + qt:o + 5 + qt], scale=QK2 ** -0.5,
                           accum_out=st2[:, o + 8 + qt:o + 9 + qt]).then_inc(a2_act.sem, 1)

            def split2(n):
                act.wait_ge(a2_pe.sem, a2_pe.at(n, "t"))
                ac(PT2[:, 0, :], psT[:, :, :].rearrange("p b t -> p (b t)")[:, 0:1280], ACT.Copy).then_inc(a2_act.sem, 1)

            def outsquares2(n):
                act.wait_ge(a2_pe.sem, a2_pe.at(n, "v"))
                for d in range(2):
                    ac(os2[:, d, :], psS[:, d, :], ACT.Copy).then_inc(a2_act.sem, 1)
                    ac(Pm2[:, 1, d * T:(d + 1) * T], psS[:, d, :], ACT.Square).then_inc(a2_act.sem, 1)

            def outroots2(n):
                act.wait_ge(a2_pe.sem, a2_pe.at(n, "sums"))
                roots(psT[:, 2, :], V2, a2_act, n)

            with act.Fori(0, LAYERS) as l:
                t0 = l * T_LAYER + T_B2
                n0 = l * HEADS2
                norm(l * 2 + 2)
                square2(t0, n0, 0)
                act.wait_ge(ly_pe.sem, ly_pe.at(l))
                ac(small[:, 34:36], psT[:, 2, 0:2], ACT.Exp).then_inc(ly_act.sem, 1)
                for x in range(4):
                    if x < 3:
                        square2(t0, n0, x + 1)
                    roots2(n0, x)
                    hi2(n0, x)
                values2(n0, 0)
                values2(n0, 1)
                with act.Fori(0, HEADS2 - 1) as h:
                    n = l * HEADS2 + h
                    t = t0 + h * 6 + 6
                    square2(t, n + 1, 0)
                    exps2(n)
                    roots2(n + 1, 0)
                    square2(t, n + 1, 1)
                    hi2(n + 1, 0)
                    split2(n)
                    roots2(n + 1, 1)
                    square2(t, n + 1, 2)
                    hi2(n + 1, 1)
                    outsquares2(n)
                    roots2(n + 1, 2)
                    square2(t, n + 1, 3)
                    hi2(n + 1, 2)
                    roots2(n + 1, 3)
                    hi2(n + 1, 3)
                    outroots2(n)
                    values2(n + 1, 0)
                    values2(n + 1, 1)

                def pooled2(m):
                    act.wait_ge(up_dve.sem, up_dve.at(l, f"mean{m}"))
                    ac(mix2[:, 0, m], pr[:, :], ACT.Copy).then_inc(up_act.sem, 1)

                n = n0 + (HEADS2 - 1)
                exps2(n)
                pooled2(0)
                split2(n)
                pooled2(1)
                outsquares2(n)
                pooled2(2)
                pooled2(3)
                outroots2(n)
                for m in range(4, KT):
                    pooled2(m)

                def merge(m):
                    n = l * KT + m
                    for s in range(2):
                        act.wait_ge(drained.sem, drained.at(t0 + U_GAB + m * 2 + s))
                        ac(mg2[:, s, :], mg2[:, s, :], ACT.Sigmoid).then_inc(m2_act.sem, 1)
                    act.wait_ge(m2_dve.sem, m2_dve.at(n, "sum"))
                    ac(flat(mix2)[:, 0, bass.ds(m * T, T)], mt2[:, :], ACT.Copy).then_inc(m2_act.sem, 1)

                merge(0)
                with act.Fori(1, KT) as m:
                    merge(m)
                tail_act(t0 + U_WO, l * 2 + 3, l * 16 + 24, l * FT + FT, lambda m: lay[:, bass.ds(m + PAR2["n2"].start, 1)],
                         lambda m: lay[:, bass.ds(m + PAR2_N, 1)])

            for t in range(TT):
                act.wait_ge(ou_pe.sem, ou_pe.at(t))
                ac(yout[:, t, :], (psT, psS)[t % 2][:, 0:2, :].rearrange("p b d -> p (b d)"), ACT.Copy).then_inc(ou_act.sem, 1)
                act.wait_ge(ou_act.sem, ou_act.at(t))
                act.dma_start(out[0, t * P:(t + 1) * P, :], yout[:, t, :]).then_inc(stored, 16)
            act.wait_ge(stored, TT * 16)


def kernel(**inputs):
    import concourse.bacc as bacc
    from concourse.bass_utils import run_bass_kernel_spmd

    nc = bacc.Bacc("TRN2", target_bir_lowering=False, num_devices=1)
    arrays = {name: np.ascontiguousarray(value) for name, value in inputs.items()}
    arrays["const"] = constants()
    args = {name: nc.dram_tensor(f"in_{name}", x.shape, F32, kind="ExternalInput").ap() for name, x in arrays.items()}
    out = nc.dram_tensor("result", (1, T, D), F32, kind="ExternalOutput").ap()
    build(nc, args, out)
    ran = run_bass_kernel_spmd(nc, [{f"in_{name}": x for name, x in arrays.items()}], core_ids=[0])
    return ran.results[0]["result"]
```
